# Optimizing a Trainium2 kernel written in Bass

```python
import jax, jax.numpy as jnp
from jax import lax
import numpy as np

D_MODEL = 1024
BATCH = 1
SEQ = 128
DEPTH = 1
DEC_BATCH = 1
DEC_SEQ = 512
PAST_LEN = 256

GRID_W = 64
D_ATTN = D_MODEL // 2
HEAD_DIM = 64
N_HEADS_A = D_ATTN // HEAD_DIM
WIN_ROWS = 8
WIN_COLS = 16
D_POOL = D_MODEL // 4
POOL_WINDOWS = (2, 4, 8, 16)
POOL_GROUP_DIM = D_POOL // len(POOL_WINDOWS)
D_CONV = D_MODEL // 4
CONV_WIDTH = 31
D_MIX = D_ATTN + D_POOL + D_CONV
D_IN = 3 * D_ATTN + D_POOL + 2 * D_CONV
N_EXPERTS = 16
N_GROUPS = 4
EXPERTS_PER_GROUP = N_EXPERTS // N_GROUPS
TOP_K = 2
D_FF = 512
EPS = 1e-6

kernel_name = "hybrid_natten_pool_conformer_moe_diffusion_step"

def rms_norm(x, g):
    xf = x.astype(jnp.float32)
    y = xf * lax.rsqrt(jnp.mean(xf * xf, axis=-1, keepdims=True) + EPS)
    return (y * g.astype(jnp.float32)).astype(x.dtype)

def ada_modulation(cond, w, b):
    m = jax.nn.silu(cond) @ w + b
    return jnp.split(m, 6, axis=-1)

def input_projection(h, w):
    B, L, _ = h.shape
    z = h @ w
    q = z[..., 0:D_ATTN].reshape(B, L, N_HEADS_A, HEAD_DIM)
    k = z[..., D_ATTN:2 * D_ATTN].reshape(B, L, N_HEADS_A, HEAD_DIM)
    v = z[..., 2 * D_ATTN:3 * D_ATTN].reshape(B, L, N_HEADS_A, HEAD_DIM)
    u_pool = z[..., 3 * D_ATTN:3 * D_ATTN + D_POOL]
    u_conv = z[..., 3 * D_ATTN + D_POOL:]
    return q, k, v, u_pool, u_conv

def context_attention(q, k, v):
    B, L = q.shape[:2]
    s = jnp.einsum('blhd,bmhd->bhlm', q, k).astype(jnp.float32) * (HEAD_DIM ** -0.5)
    p = jax.nn.softmax(s, axis=-1).astype(v.dtype)
    return jnp.einsum('bhlm,bmhd->blhd', p, v).reshape(B, L, D_ATTN)

def neighbourhood_attention(q, k, v, k_ctx, v_ctx, rpb):
    B, N, H, Dh = q.shape
    rows = N // GRID_W
    kr = min(WIN_ROWS, rows)
    r = np.arange(rows)
    rs = np.clip(r - kr // 2, 0, rows - kr)
    row_idx = rs[:, None] + np.arange(kr)[None, :]
    col = np.arange(GRID_W)
    cs = np.clip(col - WIN_COLS // 2, 0, GRID_W - WIN_COLS)
    col_mask = (col[None, :] >= cs[:, None]) & (col[None, :] < cs[:, None] + WIN_COLS)
    dr = row_idx - r[:, None] + (WIN_ROWS - 1)
    dc = np.clip(col[None, :] - col[:, None], -(WIN_COLS - 1), WIN_COLS - 1) + (WIN_COLS - 1)
    bias = rpb[:, dr[:, None, :, None], dc[None, :, None, :]]

    qg = q.reshape(B, rows, GRID_W, H, Dh)
    kg = k.reshape(B, rows, GRID_W, H, Dh)[:, row_idx]
    vg = v.reshape(B, rows, GRID_W, H, Dh)[:, row_idx]
    scale = HEAD_DIM ** -0.5
    s_loc = jnp.einsum('brchd,brjkhd->bhrcjk', qg, kg).astype(jnp.float32) * scale + bias.astype(jnp.float32)
    s_loc = jnp.where(col_mask[:, None, :], s_loc, -jnp.inf)
    s_ctx = jnp.einsum('brchd,bmhd->bhrcm', qg, k_ctx).astype(jnp.float32) * scale
    n_loc = kr * GRID_W
    s = jnp.concatenate([s_loc.reshape(B, H, rows, GRID_W, n_loc), s_ctx], axis=-1)
    p = jax.nn.softmax(s, axis=-1).astype(v.dtype)
    p_loc = p[..., :n_loc].reshape(B, H, rows, GRID_W, kr, GRID_W)
    p_ctx = p[..., n_loc:]
    out = (jnp.einsum('bhrcjk,brjkhd->brchd', p_loc, vg)
           + jnp.einsum('bhrcm,bmhd->brchd', p_ctx, v_ctx))
    return out.reshape(B, N, H * Dh)

def multiscale_pool(u, pool_w, pool_scale):
    B, L, C = u.shape
    uf = u.astype(jnp.float32)
    csum = jnp.concatenate([jnp.zeros((B, 1, C), jnp.float32), jnp.cumsum(uf, axis=1)], axis=1)
    t = np.arange(L)
    outs = []
    for g, w in enumerate(POOL_WINDOWS):
        lo = np.clip(t - w // 2, 0, L - 1)
        hi = np.clip(t + w - w // 2 - 1, 0, L - 1)
        cnt = (hi - lo + 1).astype(np.float32)
        sl = slice(g * POOL_GROUP_DIM, (g + 1) * POOL_GROUP_DIM)
        cg = csum[:, :, sl]
        mean = (cg[:, hi + 1] - cg[:, lo]) / jnp.asarray(cnt)[None, :, None]
        diff = (mean - uf[:, :, sl]).astype(u.dtype)
        outs.append(diff @ pool_w[g])
    return jnp.concatenate(outs, axis=-1) * pool_scale

def conformer_conv(u, conv_w, conv_b, ln_g, ln_b, pw_w, pw_b):
    a, g = jnp.split(u, 2, axis=-1)
    y = a * jax.nn.sigmoid(g)
    y = lax.conv_general_dilated(
        y, conv_w[:, None, :].astype(y.dtype), window_strides=(1,),
        padding=[(CONV_WIDTH // 2, CONV_WIDTH // 2)],
        dimension_numbers=('NWC', 'WIO', 'NWC'), feature_group_count=D_CONV) + conv_b
    yf = y.astype(jnp.float32)
    mu = jnp.mean(yf, axis=-1, keepdims=True)
    var = jnp.mean((yf - mu) ** 2, axis=-1, keepdims=True)
    yn = (yf - mu) * lax.rsqrt(var + EPS) * ln_g.astype(jnp.float32) + ln_b.astype(jnp.float32)
    yn = jax.nn.silu(yn).astype(u.dtype)
    return yn @ pw_w + pw_b

def mix_and_project(a, u_pool, u_conv, pool_w, pool_scale, conv_w, conv_b, ln_g, ln_b, pw_w, pw_b, w_out):
    m = jnp.concatenate([
        a,
        multiscale_pool(u_pool, pool_w, pool_scale),
        conformer_conv(u_conv, conv_w, conv_b, ln_g, ln_b, pw_w, pw_b)], axis=-1)
    return m @ w_out

def grouped_moe(h, w_router, b_router, w_gate, w_up, w_down):
    B, L, D = h.shape
    t = h.reshape(B * L, D)
    aff = jax.nn.sigmoid((t @ w_router).astype(jnp.float32))
    sel = aff + b_router.astype(jnp.float32)
    gscore = lax.top_k(sel.reshape(-1, N_GROUPS, EXPERTS_PER_GROUP), 2)[0].sum(-1)
    gbest = jnp.argmax(gscore, axis=-1)
    in_group = (jnp.arange(N_EXPERTS) // EXPERTS_PER_GROUP)[None, :] == gbest[:, None]
    _, idx = lax.top_k(jnp.where(in_group, sel, -jnp.inf), TOP_K)
    wsel = jnp.take_along_axis(aff, idx, axis=-1)
    wsel = wsel / jnp.sum(wsel, axis=-1, keepdims=True)
    gate = jnp.sum(jax.nn.one_hot(idx, N_EXPERTS, dtype=jnp.float32) * wsel[..., None], axis=1)
    hid = jax.nn.silu(jnp.einsum('td,edf->tef', t, w_gate)) * jnp.einsum('td,edf->tef', t, w_up)
    y = jnp.einsum('tef,efd->td', hid * gate[:, :, None].astype(hid.dtype), w_down)
    return y.reshape(B, L, D)

def setup_inputs(seed: int = 0) -> dict:
    key = jax.random.key(seed)
    ks = jax.random.split(key, 32)

    def nrm(k, shape, s):
        return jax.random.normal(k, shape, jnp.float32) * s

    return {
        "x_prompt": nrm(ks[0], (BATCH, SEQ, D_MODEL), 1.0),
        "x_sample": nrm(ks[1], (DEC_BATCH, DEC_SEQ, D_MODEL), 1.0),
        "cache_k": nrm(ks[2], (DEC_BATCH, DEPTH, PAST_LEN, N_HEADS_A, HEAD_DIM), 1.0),
        "cache_v": nrm(ks[3], (DEC_BATCH, DEPTH, PAST_LEN, N_HEADS_A, HEAD_DIM), 1.0),
        "c": nrm(ks[4], (DEC_BATCH, D_MODEL), 1.0),
        "c_ctx": nrm(ks[5], (D_MODEL,), 1.0),
        "w_ada": nrm(ks[6], (DEPTH, D_MODEL, 6 * D_MODEL), 0.5 * D_MODEL ** -0.5),
        "b_ada": nrm(ks[7], (DEPTH, 6 * D_MODEL), 0.02),
        "norm1_g": 1.0 + nrm(ks[8], (DEPTH, D_MODEL), 0.1),
        "norm2_g": 1.0 + nrm(ks[9], (DEPTH, D_MODEL), 0.1),
        "w_in": nrm(ks[10], (DEPTH, D_MODEL, D_IN), D_MODEL ** -0.5),
        "w_out": nrm(ks[11], (DEPTH, D_MIX, D_MODEL), D_MIX ** -0.5),
        "rpb": nrm(ks[12], (DEPTH, N_HEADS_A, 2 * WIN_ROWS - 1, 2 * WIN_COLS - 1), 0.1),
        "pool_w": nrm(ks[13], (DEPTH, len(POOL_WINDOWS), POOL_GROUP_DIM, POOL_GROUP_DIM), POOL_GROUP_DIM ** -0.5),
        "pool_scale": 1.0 + nrm(ks[14], (DEPTH, D_POOL), 0.1),
        "conv_w": nrm(ks[15], (DEPTH, CONV_WIDTH, D_CONV), CONV_WIDTH ** -0.5),
        "conv_b": nrm(ks[16], (DEPTH, D_CONV), 0.02),
        "conv_ln_g": 1.0 + nrm(ks[17], (DEPTH, D_CONV), 0.1),
        "conv_ln_b": nrm(ks[18], (DEPTH, D_CONV), 0.02),
        "conv_pw_w": nrm(ks[19], (DEPTH, D_CONV, D_CONV), D_CONV ** -0.5),
        "conv_pw_b": nrm(ks[20], (DEPTH, D_CONV), 0.02),
        "w_router": nrm(ks[21], (D_MODEL, N_EXPERTS), D_MODEL ** -0.5),
        "b_router": nrm(ks[22], (N_EXPERTS,), 0.01),
        "moe_w_gate": nrm(ks[23], (DEPTH, N_EXPERTS, D_MODEL, D_FF), D_MODEL ** -0.5),
        "moe_w_up": nrm(ks[24], (DEPTH, N_EXPERTS, D_MODEL, D_FF), D_MODEL ** -0.5),
        "moe_w_down": nrm(ks[25], (DEPTH, N_EXPERTS, D_FF, D_MODEL), D_FF ** -0.5),
        "final_g": 1.0 + nrm(ks[26], (D_MODEL,), 0.1),
    }

def reference(x_prompt, x_sample, cache_k, cache_v, c, c_ctx, w_ada, b_ada, norm1_g, norm2_g,
              w_in, w_out, rpb, pool_w, pool_scale, conv_w, conv_b, conv_ln_g, conv_ln_b,
              conv_pw_w, conv_pw_b, w_router, b_router, moe_w_gate, moe_w_up, moe_w_down, final_g):
    xp = x_prompt
    xs = x_sample
    new_k, new_v = [], []
    for l in range(DEPTH):
        sh1, sc1, g1, sh2, sc2, g2 = ada_modulation(c_ctx, w_ada[l], b_ada[l])
        h = rms_norm(xp, norm1_g[l]) * (1.0 + sc1) + sh1
        q, k, v, u_pool, u_conv = input_projection(h, w_in[l])
        a = context_attention(q, k, v)
        xp = xp + g1 * mix_and_project(a, u_pool, u_conv, pool_w[l], pool_scale[l], conv_w[l], conv_b[l],
                                       conv_ln_g[l], conv_ln_b[l], conv_pw_w[l], conv_pw_b[l], w_out[l])
        h2 = rms_norm(xp, norm2_g[l]) * (1.0 + sc2) + sh2
        xp = xp + g2 * grouped_moe(h2, w_router, b_router, moe_w_gate[l], moe_w_up[l], moe_w_down[l])
        new_k.append(k)
        new_v.append(v)

        sh1, sc1, g1, sh2, sc2, g2 = [m[:, None, :] for m in ada_modulation(c, w_ada[l], b_ada[l])]
        h = rms_norm(xs, norm1_g[l]) * (1.0 + sc1) + sh1
        q, k, v, u_pool, u_conv = input_projection(h, w_in[l])
        a = neighbourhood_attention(q, k, v, cache_k[:, l], cache_v[:, l], rpb[l])
        xs = xs + g1 * mix_and_project(a, u_pool, u_conv, pool_w[l], pool_scale[l], conv_w[l], conv_b[l],
                                       conv_ln_g[l], conv_ln_b[l], conv_pw_w[l], conv_pw_b[l], w_out[l])
        h2 = rms_norm(xs, norm2_g[l]) * (1.0 + sc2) + sh2
        xs = xs + g2 * grouped_moe(h2, w_router, b_router, moe_w_gate[l], moe_w_up[l], moe_w_down[l])

    y_prompt = rms_norm(xp, final_g)
    y_sample = rms_norm(xs, final_g)
    new_cache_k = jnp.stack(new_k, axis=1)
    new_cache_v = jnp.stack(new_v, axis=1)
    return (y_prompt, y_sample, new_cache_k, new_cache_v)


_drawn_inputs = setup_inputs


def setup_inputs(seed=0):
    import zlib

    import numpy as np

    out = dict(_drawn_inputs(seed))
    spreads = {}
    factors = {'cache_k': 3.01,
     'rpb': 8.0,
     'pool_scale': 2.688,
     'conv_b': 6.061,
     'conv_ln_g': 2.879,
     'conv_ln_b': 6.258,
     'conv_pw_b': 8.0}
    for name, (base, spread) in spreads.items():
        noise = np.random.default_rng([zlib.crc32(name.encode()), seed]).standard_normal(out[name].shape)
        drawn = base * np.exp(spread * noise) if base else spread * noise
        out[name] = __import__('jax').numpy.asarray(drawn.astype(out[name].dtype))
    for name, factor in factors.items():
        out[name] = (out[name] * factor).astype(out[name].dtype)
    return out
```

```python
from contextlib import ExitStack

import numpy as np

import concourse.bass as bass
from concourse import mybir
from concourse.alu_op_type import AluOpType as ALU

ACT = mybir.ActivationFunctionType
F32 = mybir.dt.float32
U32 = mybir.dt.uint32
I32 = mybir.dt.int32
AX = mybir.AxisListType

P = 128
D = 1024
KD = D // P
NCTX = 128
NLAT = 512
NTOK = NLAT + NCTX
TT = NTOK // P
ROWS, COLS = 8, 64
G, GC = 8, 8
H, DH = 8, 64
DA = H * DH
PAST = 256
WR, WC = 8, 16
NE, NG, EPG = 16, 4, 4
DFF = 512
FC = DFF // P
TAPS = 31
HALO = TAPS // 2
EPS = 1e-6
NEG = -1e30
PADP = 8
LP = NLAT + 2 * PADP + NCTX + 2 * PADP
LC = NLAT + 2 * HALO + NCTX + 2 * HALO
CTXP = NLAT + 2 * PADP
CTXC = NLAT + 2 * HALO
NACC = LC - 2 * HALO
MAXOV = (2 * NTOK - (P + 1)) // P + 1
MAXOV += MAXOV % 2
NT = NE + MAXOV + 2
BIG = NE + MAXOV
RING = 6

CW = [("ident", P), ("tri", P), ("ones", P), ("iota", P), ("iotat", NT), ("tok", TT), ("tie", 16),
      ("edge", 32), ("invw", 2), ("cols2", 2), ("mask", 3 * 256)]
CO, _o = {}, 0
for _n, _w in CW:
    CO[_n] = (_o, _o + _w)
    _o += _w
CWID = _o

VR = [("b_ada", 48), ("norm1_g", 8), ("norm2_g", 8), ("c_ctx", 8), ("c", 8), ("pool_scale", 2), ("conv_b", 2),
      ("conv_ln_g", 2), ("conv_ln_b", 2), ("conv_pw_b", 2)]
VO, _o = {}, 0
for _n, _w in VR:
    VO[_n] = (_o, _w)
    _o += _w
NVEC = _o


def shape_constants():
    c = np.zeros((P, CWID), np.float32)

    def put(name, v):
        c[:, CO[name][0]:CO[name][1]] = v

    p = np.arange(P)
    put("ident", np.eye(P))
    put("tri", p[:, None] < p[None, :])
    put("ones", 1.0)
    put("iota", p[None, :])
    put("iotat", np.arange(NT)[None, :])
    put("tok", p[:, None] + P * np.arange(TT)[None, :])
    put("tie", (np.arange(4)[None, :] < np.arange(4)[:, None]).reshape(1, 16))
    e = np.ones((P, 2, 2, 8))
    w_of = np.array([[2, 4], [8, 16]])
    for ch in range(2):
        for half in range(2):
            w = w_of[ch, half]
            for i in range(8):
                e[64 * half:64 * half + 64, ch, 0, i] = w / min(w, i + w // 2)
                e[64 * half:64 * half + 64, ch, 1, i] = w / min(w, 8 - i + w // 2)
    put("edge", e.reshape(P, 32))
    put("invw", 1.0 / w_of.T[p // 64])
    put("cols2", 0.0)
    gq, qc = p // 64, p % 8
    k = np.arange(256)
    gk, kc = k // 64, k % 8
    m = np.zeros((P, 3, 256))
    for v, t in enumerate((0, 1, 3)):
        qcol = (2 * t + gq) * 8 + qc
        kcol = (2 * t - 1 + gk) * 8 + kc
        cs = np.clip(qcol - WC // 2, 0, COLS - WC)
        ok = (kcol[None] >= cs[:, None]) & (kcol[None] < cs[:, None] + WC) & (kcol[None] >= 0) & (kcol[None] < COLS)
        m[:, v] = np.where(ok, 0.0, NEG)
    put("mask", m.reshape(P, 768))
    return c


def fill_plan():
    plan = [(("vec",), "D"), (("cw",), "D")]
    plan += [(("xT", i, h), "AD"[h]) for i in range(TT) for h in range(2)]
    for j in range(4):
        plan += [(("ada", j), "A"), (("adT", j), "A")]
    plan += [(("pa", m), "A") for m in range(4)] + [(("pac",), "A")]
    plan += [(("g", m), "A") for m in range(2)] + [(("gc",), "A")]
    plan += [(("ada", j), "A") for j in (4, 5)]
    plan += [(("q", m), "A") for m in range(4)] + [(("qc",), "A")]
    plan += [(("adT", j), "A") for j in (4, 5)]
    plan += [(("ada", j), "A") for j in (6, 7)] + [(("ck", i), "A") for i in range(2)]
    plan += [(("k", m), "A") for m in range(4)] + [(("kc",), "A")]
    plan += [(("adT", j), "A") for j in (6, 7)]
    plan += [(("ada", j), "A") for j in (8, 9)]
    plan += [(("mu",), "D"), (("muc",), "D")]
    plan += [(("v", m), "A") for m in range(2)] + [(("var",), "D"), (("varc",), "D")]
    plan += [(("v", m), "A") for m in range(2, 4)] + [(("vc",), "A")]
    plan += [(("adT", j), "A") for j in (8, 9)]
    plan += [(("ada", j), "A") for j in (10, 11)]
    plan += [(("ko",), "A"), (("pl", 0), "A"), (("pl", 1), "A"), (("plc",), "A")]
    plan += [(("adT", j), "A") for j in (10, 11)]
    plan += [(("pw", 0), "A"), (("pw", 1), "A"), (("pwc",), "A")]
    for i in range(PAIRS + 4):
        if i < PAIRS:
            plan.append((("S", i), "A"))
        if 2 <= i < PAIRS + 2:
            plan.append((("PT", i - 2), "A"))
        if i == 4:
            plan.append((("modT",), "A"))
        if i >= 4 and (i - 4) % 8 == 7:
            plan.append((("aT", (i - 4) // 8), "A"))
    plan += [(("Sc", 0), "D"), (("Sc", 1), "D"), (("PTc", 0), "A"), (("PTc", 1), "A"), (("aT", 4), "A")]
    for i in range(TT + LAG):
        if i < TT:
            plan += [(("wo", i, 0), "D"), (("wo", i, 1), "D")]
        if i >= LAG:
            plan += [(("hT", i - LAG, 0), "A"), (("hT", i - LAG, 1), "A"), (("lg", i - LAG), "A")]
    plan += [(("rank",), "D"), (("table",), "D")]
    return plan


LAG = 2
PAIRS = 4 * H
PLAN = fill_plan()
NTH = {key: n for n, (key, _) in enumerate(PLAN)}
WHO = {key: who for key, who in PLAN}
TURN = {key: sum(1 for k, w in PLAN[:n + 1] if w == who) for n, (key, who) in enumerate(PLAN)}

LOADS = [(("ada", j), ("ada", j)) for j in range(4)]
LOADS += [(("in", 3), ("pac",)), (("in", 4), ("gc",)), (("ada", 4), ("ada", 4)), (("ada", 5), ("ada", 5)),
          (("in", 0), ("qc",)), (("ada", 6), ("ada", 6)), (("ada", 7), ("ada", 7)), (("in", 1), ("kc",)),
          (("ada", 8), ("ada", 8)), (("ada", 9), ("ada", 9)), (("in", 2), ("vc",)),
          (("ada", 10), ("ada", 10)), (("ada", 11), ("ada", 11)),
          (("out", 0), ("wo", TT - 1, 1)), (("out", 1), ("wo", TT - 1, 1))]
LOADNO = {key: n for n, (key, _) in enumerate(LOADS)}
NLOAD = len(LOADS)
EVEN = [(NLOAD + q) % 3 for q in range(3)]
EVEN_BASE = [len([n for n in range(NLOAD) if n % 3 == s]) for s in EVEN]


def build(nc, t):
    ctx = ExitStack()

    def sb(name, shape, dt=F32):
        return ctx.enter_context(nc.sbuf_tensor(name, shape, dt))

    def sem(name):
        return ctx.enter_context(nc.semaphore(name))

    bank = [ctx.enter_context(nc.psum_tensor(f"bank{i}", [P, 512], F32)) for i in range(8)]

    slots = sb("slots", [P, 3, 4096])
    x = sb("x", [P, TT, D])
    ra = sb("ra", [P, KD * NTOK])
    rb = sb("rb", [P, 16984])
    rc = sb("rc", [P, KD * NTOK])
    re = sb("re", [P, 5440])
    cst = sb("cst", [P, CWID])
    vecT = sb("vecT", [P, NVEC])
    cwT = sb("cwT", [P, 2 * TAPS])
    cond = sb("cond", [P, KD, 32])
    mod = sb("mod", [P, 6, 2, KD])
    poolw = sb("poolw", [P, 2, P])
    pww = sb("pww", [P, 2, 256])
    wr = sb("wr", [P, KD, NE])
    br = sb("br", [P, NE])
    st = sb("st", [P, 3, 32])
    ss = sb("ss", [P, 3, TT])
    ridx = sb("ridx", [P, NT], U32)
    gi = sb("gi", [P, 2], U32)
    slot_u = sb("slot_u", [P, 2, TT], U32)
    wts = sb("wts", [P, 2, TT])
    oi = sb("oi", [P, 16], I32)

    def K(name):
        return cst[:, CO[name][0]:CO[name][1]]

    def V(name):
        return vecT[:, VO[name][0]:VO[name][0] + VO[name][1]]

    ident = K("ident")
    hT = ra[:, :].rearrange("p (k n) -> p k n", k=KD)
    bc = ra[:, 0:4096].rearrange("p (b n) -> p b n", b=4)
    cuts, o = [], 0
    for n in (4 * NTOK, 4 * 640, 4 * PAST, 4 * NCTX, 4 * 520, 520, 2 * 520, 512, H * 256, 1024, 2048, 1024):
        cuts.append(rb[:, o:o + n])
        o += n
    assert o <= 16984
    qT, kT, kcT, kpT = (v.rearrange("p (m n) -> p m n", m=4) for v in cuts[0:4])
    vl = cuts[4].rearrange("p (j h e) -> p j h e", j=4, h=H)
    vp = cuts[5].rearrange("p (h e) -> p h e", h=H)
    vc = cuts[6].rearrange("p (j h e) -> p j h e", j=2, h=H)
    at = cuts[7]
    raw = cuts[8].rearrange("p (h r w) -> p h r w", h=H, r=8)
    bm = cuts[9].rearrange("p (b n) -> p b n", b=4)
    pr = cuts[10].rearrange("p (b n) -> p b n", b=4)
    pts = cuts[11].rearrange("p (b n) -> p b n", b=2)
    hT0 = cuts[9].rearrange("p (k n) -> p k n", k=KD)
    ckr = cuts[10][:, 0:1024].rearrange("p (j n) -> p j n", j=2)
    odd = rb[:, 0:12288].rearrange("p (q n) -> p q n", q=3)
    bc2 = rb[:, 12288:14336].rearrange("p (b n) -> p b n", b=2)
    h2 = rb[:, 14336:16384].rearrange("p (b n) -> p b n", b=2)
    rtmp = rb[:, 16384:16896]
    rowhot = rb[:, 12288:12288 + 10 * P].rearrange("p (b n) -> p b n", b=10)
    tilehot = rb[:, 13568:13568 + 10 * NT].rearrange("p (b n) -> p b n", b=10)
    up, s1, s2 = (rc[:, i * 2 * LP:(i + 1) * 2 * LP].rearrange("p (m n) -> p m n", m=2) for i in range(3))
    adr = rc[:, 6 * LP + 64:6 * LP + 64 + 2 * P].rearrange("p (b n) -> p b n", b=2)
    mT = rc[:, :].rearrange("p (k n) -> p k n", k=KD)
    xn = re[:, 0:2048].rearrange("p (b n) -> p b n", b=2)
    junk = re[:, 2048:3072]
    junk2 = ra[:, 4096:5120]
    e0, e1, e2, e3 = 2 * LC, 2 * LC + 2 * NTOK, 2 * LC + 2 * NTOK + 2 * NACC, 2 * LC + 4 * NTOK + 2 * NACC
    yc = re[:, 0:e0].rearrange("p (m n) -> p m n", m=2)
    sg = re[:, e0:e1].rearrange("p (m n) -> p m n", m=2)
    acc = re[:, e1:e2].rearrange("p (m n) -> p m n", m=2)
    df = re[:, e2:e3].rearrange("p (m n) -> p m n", m=2)
    rs = re[:, 0:NTOK]
    mrow = re[0:64, 5312:5440]
    vrow, cwrow, rprow = re[:, 5000:5128], re[:, 5128:5256], re[:, 5256:5304]
    h2T = re[:, 0:5120].rearrange("p (k n) -> p k n", k=KD)
    xg = rc[:, 0:2048].rearrange("p (b n) -> p b n", b=2)
    xt = rc[:, 2048:4096].rearrange("p (b k n) -> p b k n", b=2, k=KD)
    hid = rc[:, 4096:5120].rearrange("p (b f n) -> p b f n", b=2, f=FC)
    yo = re[:, 0:2048].rearrange("p (b n) -> p b n", b=2)
    gs = re[:, 2048:2560].rearrange("p (b n) -> p b n", b=2)
    wset = [[slots[:, s, :] for s in EVEN], [odd[:, q, :] for q in range(3)]]
    fy = slots[:, :, :].rearrange("p a b -> p (a b)")[:, 0:2 * TT * D].rearrange("p (c k n) -> p c k n", c=TT, k=2)
    pa_, pb_ = ra[:, 4096:4416], ra[:, 4416:4736]
    rw = re[:, 5120:5440]

    S = {n: sem(n) for n in """cst_in vec_in small_in poolw_in cachek_in cachev_in rpb_in rpad_out rwin_out raw_in bc_in bc2_in
        psum_full evac_a evac_d cond_zero cond_ready ssq_ready ms_ready sqrt_ready xn_ready mod_ready h_ready h0_ready
        pads_ready rpad_ready ones_ready tap_done df_ready sq_ready sd_ready yn_ready
        act_ready bm_ready smax_done pv_done o_free expc_done mrow_out kcache_out vcache_out
        x1_ready ssq2_ready ms2_ready sqrt2_ready hn_ready h2_ready route_ready hot_ready ridx_ready oi_ready
        xt_full xt_evac_a xt_evac_d gu_full silu_done hid_done y_full y_evac_a y_evac_d bcend_in
        fsum_ready fmul_ready x2_ready ssq3_ready ms3_ready sqrt3_ready out_ready out_done
        zeros_ready zeros_out moe_stored over_stored gi_seen xg_seen gi_ready dve_chain pool_chain act_chain""".split()}
    w_slot = [sem(f"w_slot{i}") for i in range(3)]
    w_odd = [sem(f"w_odd{i}") for i in range(3)]
    x_in = [sem(f"x_in{i}") for i in range(TT)]
    h2_out = [sem(f"h2_out{i}") for i in range(2)]
    xg_in = [sem(f"xg_in{i}") for i in range(2)]
    y_out = [sem(f"y_out{i}") for i in range(2)]
    fy_in = [sem(f"fy_in{i}") for i in range(TT)]

    def chained(eng, name):
        n = [0]

        def link(ins):
            n[0] += 1
            ins.then_inc(S[name], 1)
            eng.wait_ge(S[name], n[0])
        return link

    def filled(eng, *key):
        eng.wait_ge(S["psum_full"], NTH[key] + 1)
        return bank[NTH[key] % RING]

    def emptied(eng, *key):
        eng.wait_ge(S["evac_a" if WHO[key] == "A" else "evac_d"], TURN[key])

    def group(ap):
        return ap.rearrange("p (r g c) -> p g r c", r=ROWS, g=G)

    def ungroup(ap):
        return ap.rearrange("p (g r c) -> p g r c", r=ROWS, g=G)

    def ge(eng, s, n):
        if not (isinstance(n, int) and n <= 0):
            eng.wait_ge(S[s] if isinstance(s, str) else s, n)

    def over_tiles(eng, body, over_body=None):
        for b in range(2):
            body(0, b)
        with eng.Fori(1, NE // 2) as i:
            for b in range(2):
                body(i, b)
        eng.wait_ge(S["oi_ready"], 1)
        more = eng.value_load(oi[0:1, 0:1], min_val=0, max_val=MAXOV)
        with eng.Fori(NE // 2, NE // 2 + MAXOV // 2) as i:
            for b in range(2):
                with eng.If(more > i * 2 + (b - NE)):
                    (over_body or body)(i, b)
            eng.nop()

    block = ctx.enter_context(nc.Block())

    @block.sync
    def _(sp):
        for n, (key, _) in enumerate(LOADS):
            if n >= 3:
                sp.wait_ge(S["psum_full"], NTH[LOADS[n - 3][1]] + 1)
            kind, j = key
            if kind == "ada":
                src = t["w_ada"][0].rearrange("(k p) n -> p k n", p=P)[:, :, 512 * j:512 * j + 512]
            elif kind == "in":
                src = t["w_in"][0].rearrange("(k p) n -> p k n", p=P)[:, :, 512 * j:min(512 * j + 512, 2304)]
            else:
                src = t["w_out"][0].rearrange("(k p) n -> p k n", p=P)[:, 4 * j:4 * j + 4, :]
            if n == 9:
                sp.wait_ge(S["zeros_ready"], 1)
                for q in range(NE, BIG):
                    sp.dma_start(t["yd"][q * P:(q + 1) * P, :], cuts[11]).then_inc(S["zeros_out"], 16)
            k, w = src.shape[1], src.shape[2]
            sp.dma_start(slots[:, n % 3, 0:k * w].rearrange("p (k n) -> p k n", k=k), src).then_inc(w_slot[n % 3], 16)

        def expert(q, e):
            if q < 2:
                return t["moe_w_gate" if q == 0 else "moe_w_up"][0, e].rearrange("(p k) n -> p (k n)", k=KD)
            return t["moe_w_down"][0, e].rearrange("(p k) n -> p (k n)", k=FC)

        def load(b, q, e):
            s = w_odd[q] if b else w_slot[EVEN[q]]
            sp.dma_start(wset[b][q], expert(q, e)).then_inc(s, 16)

        for q in range(3):
            sp.wait_ge(S["psum_full"], NTH[LOADS[NLOAD - 3 + q][1]] + 1)
            load(0, q, 0)
            if q == 0:
                emptied(sp, "aT", 4)
                for r in range(3):
                    load(1, r, 1)

        def store(b, tile):
            sp.wait_ge(S["y_evac_a"], tile + 1)
            sp.wait_ge(S["y_evac_d"], tile + 1)
            sp.dma_start(t["yd"][bass.ds(tile * P, P), :], yo[:, b, :]).then_inc(y_out[b], 16)

        with sp.Fori(0, NE // 2 - 1) as i:
            for b in range(2):
                tile = i * 2 + b
                sp.wait_ge(S["gu_full"], tile * 2 + 2)
                load(b, 0, tile + 2)
                load(b, 1, tile + 2)
                sp.wait_ge(S["y_full"], tile * 2 + 2)
                load(b, 2, tile + 2)
                store(b, tile)
        sp.wait_ge(S["oi_ready"], 1)
        more = sp.value_load(oi[0:1, 0:1], min_val=0, max_val=MAXOV)

        def load_more(b, tile, n):
            at_n = slice(n + 1, n + 2) if isinstance(n, int) else bass.ds(n + 1, 1)
            e = sp.value_load(oi[0:1, at_n], min_val=0, max_val=NE - 1)
            sp.wait_ge(S["gu_full"], tile * 2 + 2)
            load(b, 0, e)
            load(b, 1, e)
            sp.wait_ge(S["y_full"], tile * 2 + 2)
            load(b, 2, e)

        for b in range(2):
            with sp.If(more > b):
                load_more(b, NE - 2 + b, b)
            store(b, NE - 2 + b)
        with sp.Fori(0, MAXOV // 2) as i:
            for b in range(2):
                with sp.If(more > i * 2 + (2 + b)):
                    load_more(b, i * 2 + (NE + b), i * 2 + (2 + b))
                with sp.If(more > i * 2 + b):
                    store(b, i * 2 + (NE + b))
                    sp.wait_ge(y_out[b], i * 16 + 16 * (NE // 2 + 1))
                    sp.sem_inc(S["over_stored"], 1)
            sp.nop()
        for b in range(2):
            sp.wait_ge(y_out[b], 16 * (NE // 2))
        sp.sem_inc(S["moe_stored"], 1)

        for c in range(TT):
            sp.wait_ge(S["out_ready"], c + 1)
            if c < 4:
                for g in range(2):
                    sp.dma_start(t["y_sample"][0].rearrange("(r g c) d -> g r c d", r=ROWS, g=G)[2 * c + g],
                                 fy[64 * g:64 * g + 64, c, 1, :]).then_inc(S["out_done"], 16)
            else:
                sp.dma_start(t["y_prompt"][0], fy[:, c, 1, :]).then_inc(S["out_done"], 16)
        sp.wait_ge(S["out_done"], 16 * 9)

    @block.scalar
    def _(act):
        link = chained(act, "act_chain")
        sc = nc.scalar

        def evac(out, in_, func=ACT.Copy, last=True, **kw):
            ins = sc.activation(out, in_, func, **kw)
            if last:
                ins.then_inc(S["evac_a"], 1)

        o = 0
        for name, rows in VR:
            src = t[name]
            if len(src.shape) == 2:
                src = src[0]
            act.dma_start(vrow[o:o + rows, :], src.rearrange("(a p) -> a p", p=P)).then_inc(S["vec_in"], 16)
            o += rows
        act.dma_start(cwrow[0:2 * TAPS, :], t["conv_w"][0].rearrange("k (m p) -> (k m) p", p=P)).then_inc(S["vec_in"], 16)
        act.dma_start(cst[:, :], t["consts"]).then_inc(S["cst_in"], 16)
        for i in range(4):
            for g in range(2):
                act.dma_start(x[64 * g:64 * g + 64, i, :],
                              t["x_sample"][0].rearrange("(r g c) d -> g r c d", r=ROWS, g=G)[2 * i + g]).then_inc(x_in[i], 16)
        act.dma_start(x[:, 4, :], t["x_prompt"][0]).then_inc(x_in[4], 16)
        act.dma_start(pww[:, :, :], t["conv_pw_w"][0].rearrange("(k p) n -> p k n", p=P)).then_inc(S["small_in"], 16)
        act.dma_start(wr[:, :, :], t["w_router"].rearrange("(k p) n -> p k n", p=P)).then_inc(S["small_in"], 16)
        act.dma_start(br[:, :], t["b_router"].rearrange("(a n) -> a n", a=1).to_broadcast([P, NE])).then_inc(S["small_in"], 16)
        act.dma_start(ckr[:, :, :], t["cache_k"][0, 0].rearrange("(j p) h e -> p j (h e)", p=P)).then_inc(S["cachek_in"], 16)
        for j in range(2):
            act.dma_start(vc[:, j, :, 0:DH], t["cache_v"][0, 0, j * P:(j + 1) * P]).then_inc(S["cachev_in"], 16)

        emptied(act, "cw")
        act.wait_ge(S["cond_zero"], 1)
        sc.activation(cond[:, :, 0], V("c_ctx"), ACT.Silu)
        sc.activation(cond[:, :, 1], V("c"), ACT.Silu).then_inc(S["cond_ready"], 1)
        for i in range(TT):
            act.wait_ge(x_in[i], 32 if i < 4 else 16)
            ins = sc.activation(junk, x[:, i, :], ACT.Square, accum_out=ss[:, 0, i:i + 1])
            if i < TT - 1:
                link(ins)
        ins.then_inc(S["ssq_ready"], 1)
        act.wait_ge(S["ms_ready"], 1)
        sc.activation(ss[:, 1, :], ss[:, 0, :], ACT.Sqrt).then_inc(S["sqrt_ready"], 1)
        for i in range(TT):
            b = filled(act, "xT", i, 0)
            evac(hT[:, 0:4, i * P:(i + 1) * P], b[:, :].rearrange("p (k n) -> p k n", k=4))

        def ada(j):
            if j >= 2:
                filled(act, "adT", j - 2)
            b = filled(act, "ada", j)
            evac(adr[:, j % 2, :], b[:, 0:P])

        def adT(j):
            b = filled(act, "adT", j)
            evac(mod[:, j // 2, :, 4 * (j % 2):4 * (j % 2) + 4],
                 b[:, 0:P].rearrange("p (q s) -> p s q", q=4)[:, 0:2, :])

        for j in range(4):
            ada(j)
            adT(j)
        act.wait_ge(S["pads_ready"], 2)
        for m in range(4):
            b = filled(act, "pa", m)
            dst = up[:, m, PADP:PADP + NLAT] if m < 2 else yc[:, m - 2, HALO:HALO + NLAT]
            evac(group(dst), ungroup(b[:, :]))
        b = filled(act, "pac")
        four = b[:, :].rearrange("p (m n) -> p m n", m=4)
        evac(up[:, :, CTXP + PADP:CTXP + PADP + NCTX], four[:, 0:2], last=False)
        evac(yc[:, :, CTXC + HALO:CTXC + HALO + NCTX], four[:, 2:4])
        for m in range(2):
            b = filled(act, "g", m)
            evac(group(sg[:, m, 0:NLAT]), ungroup(b[:, :]), ACT.Sigmoid)
        b = filled(act, "gc")
        evac(sg[:, :, NLAT:NTOK], b[:, 0:256].rearrange("p (m n) -> p m n", m=2), ACT.Sigmoid)
        ada(4)
        ada(5)
        for m in range(4):
            b = filled(act, "q", m)
            evac(qT[:, m, 0:NLAT], b[:, :], scale=DH ** -0.5)
        b = filled(act, "qc")
        evac(qT[:, :, NLAT:NTOK], b[:, :].rearrange("p (m n) -> p m n", m=4), scale=DH ** -0.5)
        adT(4)
        adT(5)
        ada(6)
        ada(7)
        for i in range(2):
            b = filled(act, "ck", i)
            evac(kcT[:, :, i * P:(i + 1) * P], b[:, :].rearrange("p (m n) -> p m n", m=4))
        for m in range(4):
            b = filled(act, "k", m)
            evac(kT[:, m, 64:NLAT], b[:, 0:NLAT - 64], last=False)
            evac(kT[:, m, 0:64], b[:, NLAT - 64:NLAT], last=False)
            evac(kT[:, m, NLAT:NLAT + 64], b[:, NLAT - 64:NLAT], last=False)
            evac(kT[:, m, NLAT + 64:NLAT + 128], b[:, 0:64])
        b = filled(act, "kc")
        evac(kpT[:, :, :], b[:, :].rearrange("p (m n) -> p m n", m=4))
        adT(6)
        adT(7)
        ada(8)
        ada(9)
        act.wait_ge(S["ones_ready"], 1)
        emptied(act, "muc")
        sc.activation(sg[:, :, 0:NLAT], acc[:, :, 0:NLAT], ACT.Square)
        sc.activation(sg[:, :, NLAT:NTOK], acc[:, :, CTXC:CTXC + NCTX], ACT.Square).then_inc(S["sq_ready"], 1)
        for j in range(4):
            b = filled(act, "v", j)
            evac(vl[:, j, :, 0:DH], b[:, :].rearrange("p (h e) -> p h e", h=H))
            if j == 2:
                emptied(act, "varc")
                sc.activation(rs, rs, ACT.Sqrt).then_inc(S["sd_ready"], 1)
        b = filled(act, "vc")
        evac(vp[:, :, 0:DH], b[:, :].rearrange("p (h e) -> p h e", h=H))
        adT(8)
        adT(9)
        ada(10)
        ada(11)
        b = filled(act, "ko")
        evac(at, b[:, :])
        for m in range(2):
            b = filled(act, "pl", m)
            evac(ungroup(mT[:, 4 + m, 0:NLAT]), group(b[:, :]), ACT.Identity, scale=V("pool_scale")[:, m:m + 1])
        b = filled(act, "plc")
        for m in range(2):
            evac(mT[:, 4 + m, NLAT:NTOK], b[:, m * P:(m + 1) * P], ACT.Identity, last=m == 1,
                 scale=V("pool_scale")[:, m:m + 1])
        adT(10)
        adT(11)
        act.wait_ge(S["yn_ready"], 1)
        for m in range(2):
            for dst, src in ((sg[:, m, 0:NLAT], acc[:, m, 0:NLAT]), (sg[:, m, NLAT:NTOK], acc[:, m, CTXC:CTXC + NCTX])):
                ins = sc.activation(dst, src, ACT.Silu, scale=V("conv_ln_g")[:, m:m + 1], bias=V("conv_ln_b")[:, m:m + 1])
        ins.then_inc(S["act_ready"], 1)
        for m in range(2):
            b = filled(act, "pw", m)
            evac(ungroup(mT[:, 6 + m, 0:NLAT]), group(b[:, :]), ACT.Identity, bias=V("conv_pw_b")[:, m:m + 1])
        b = filled(act, "pwc")
        for m in range(2):
            evac(mT[:, 6 + m, NLAT:NTOK], b[:, m * P:(m + 1) * P], ACT.Identity, last=m == 1,
                 bias=V("conv_pw_b")[:, m:m + 1])

        def aT(i):
            b = filled(act, "aT", i)
            evac(mT[:, 0:4, i * P:(i + 1) * P], b[:, :].rearrange("p (m n) -> p m n", m=4))

        act.wait_ge(S["zeros_out"], 16 * MAXOV)
        for i in range(PAIRS + 4):
            if i < PAIRS:
                act.wait_ge(S["smax_done"], i + 1)
                b = filled(act, "S", i)
                nmx = st[:, 2, i:i + 1]
                sc.activation(pr[:, i % 4, 0:256], pr[:, i % 4, 0:256], ACT.Exp, bias=nmx)
                evac(pr[:, i % 4, 256:512], b[:, 256:512], ACT.Exp, bias=nmx)
            if 2 <= i < PAIRS + 2:
                s = i - 2
                if s >= 2:
                    act.wait_ge(S["pv_done"], s - 1)
                b = filled(act, "PT", s)
                evac(pts[:, s % 2, :], b[:, :])
            if i == 4:
                b = filled(act, "modT")
                evac(mrow, b[0:64, 0:P])
            if i >= 4 and (i - 4) % 8 == 7:
                aT((i - 4) // 8)
        for j in range(2):
            emptied(act, "Sc", j)
            sc.activation(pr[:, j, :], pr[:, j, :], ACT.Exp).then_inc(S["expc_done"], 1)
        for j in range(2):
            act.wait_ge(S["pv_done"], PAIRS - 1 + j)
            b = filled(act, "PTc", j)
            evac(pts[:, j, :], b[:, :])
        aT(4)

        def rms2(i):
            act.wait_ge(S["x1_ready"], i + 1)
            if i >= 1:
                act.wait_ge(S["ssq2_ready"], i)
            sc.activation(junk2, x[:, i, :], ACT.Square, accum_out=ss[:, 0, i:i + 1]).then_inc(S["ssq2_ready"], 1)
            act.wait_ge(S["ms2_ready"], i + 1)
            sc.activation(ss[:, 1, i:i + 1], ss[:, 0, i:i + 1], ACT.Sqrt).then_inc(S["sqrt2_ready"], 1)

        def logits(i):
            for hf in range(2):
                b = filled(act, "hT", i, hf)
                evac(h2T[:, 4 * hf:4 * hf + 4, i * P:(i + 1) * P], b[:, :].rearrange("p (k n) -> p k n", k=4))
            b = filled(act, "lg", i)
            evac(rw[:, i * NE:(i + 1) * NE], b[:, 0:NE], ACT.Sigmoid)

        for i in range(TT + LAG):
            if i < TT:
                rms2(i)
            if i >= LAG:
                logits(i - LAG)

        def xt_out(i, b):
            act.wait_ge(S["xt_full"], i * 4 + (2 * b + 1))
            ge(act, "gu_full", i * 4 + (2 * b - 2))
            sc.activation(xt[:, b, 0:4, :], bank[0][:, :].rearrange("p (k n) -> p k n", k=4),
                          ACT.Copy).then_inc(S["xt_evac_a"], 1)

        def tiles(i, b):
            for hf in range(2):
                act.wait_ge(S["gu_full"], i * 4 + (2 * b + hf + 1))
                ge(act, "hid_done", i * 4 + (2 * b + hf - 1))
                sc.activation(gs[:, hf, :], bank[2 + hf][:, 0:256], ACT.Silu).then_inc(S["silu_done"], 1)
            xt_out(i + b, 1 - b)
            act.wait_ge(S["y_full"], i * 4 + (2 * b + 1))
            ge(act, y_out[b], i * 16)
            sc.activation(yo[:, b, 0:512], bank[4 + 2 * b][:, :], ACT.Copy).then_inc(S["y_evac_a"], 1)

        xt_out(0, 0)
        over_tiles(act, tiles)

        for c in range(TT):
            act.wait_ge(S["x2_ready"], c + 1)
            sc.activation(fy[:, c, 1, :], x[:, c, :], ACT.Square, accum_out=ss[:, 0, c:c + 1]).then_inc(S["ssq3_ready"], 1)
            act.wait_ge(S["ms3_ready"], c + 1)
            sc.activation(ss[:, 1, c:c + 1], ss[:, 0, c:c + 1], ACT.Sqrt).then_inc(S["sqrt3_ready"], 1)

    @block.vector
    def _(dve):
        link = chained(dve, "dve_chain")
        v = nc.vector

        def evac(out, in_):
            v.tensor_copy(out, in_).then_inc(S["evac_d"], 1)

        b = filled(dve, "vec")
        evac(vecT[:, :], b[:, 0:NVEC])
        b = filled(dve, "cw")
        evac(cwT[:, :], b[:, 0:2 * TAPS])
        emptied(dve, "cw")
        dve.wait_ge(S["ssq_ready"], 1)
        v.tensor_scalar(ss[:, 0, :], ss[:, 0, :], 1.0 / D, EPS, ALU.mult, ALU.add).then_inc(S["ms_ready"], 1)
        dve.wait_ge(S["sqrt_ready"], 1)
        link(v.reciprocal(ss[:, 2, :], ss[:, 1, :]))
        for i in range(TT):
            if i >= 2:
                filled(dve, "xT", i - 2, 1)
            v.tensor_scalar(xn[:, i % 2, :], x[:, i, :], ss[:, 2, i:i + 1], None, ALU.mult).then_inc(S["xn_ready"], 1)
            if i >= 1:
                b = filled(dve, "xT", i - 1, 1)
                evac(hT[:, 4:8, (i - 1) * P:i * P], b[:, :].rearrange("p (k n) -> p k n", k=4))
        b = filled(dve, "xT", TT - 1, 1)
        evac(hT[:, 4:8, (TT - 1) * P:TT * P], b[:, :].rearrange("p (k n) -> p k n", k=4))
        dve.wait_ge(S["mod_ready"], 2)
        emptied(dve, "xT", TT - 1, 0)
        emptied(dve, "xT", TT - 1, 1)
        for k in range(KD):
            for s, (a, n) in ((1, (0, NLAT)), (0, (NLAT, NTOK))):
                ins = v.tensor_scalar(hT[:, k, a:n], hT[:, k, a:n], mod[:, 1, s, k:k + 1], mod[:, 0, s, k:k + 1],
                                      ALU.mult, ALU.add)
            ins.then_inc(S["h_ready"], 1)
        emptied(dve, "gc")
        link(v.tensor_tensor(yc[:, :, HALO:HALO + NLAT], yc[:, :, HALO:HALO + NLAT], sg[:, :, 0:NLAT], ALU.mult))
        link(v.tensor_tensor(yc[:, :, CTXC + HALO:CTXC + HALO + NCTX], yc[:, :, CTXC + HALO:CTXC + HALO + NCTX],
                             sg[:, :, NLAT:NTOK], ALU.mult))
        for m in range(2):
            v.tensor_scalar(acc[:, m, :], yc[:, m, 0:NACC], cwT[:, m:m + 1], V("conv_b")[:, m:m + 1],
                            ALU.mult, ALU.add).then_inc(S["tap_done"], 1)
        with dve.Fori(1, TAPS) as k:
            for m in range(2):
                dve.wait_ge(S["tap_done"], k * 2 + (m - 1))
                v.scalar_tensor_tensor(acc[:, m, :], yc[:, m, bass.ds(k, NACC)], cwT[:, bass.ds(k * 2 + m, 1)],
                                       acc[:, m, :], ALU.mult, ALU.add).then_inc(S["tap_done"], 1)
        dve.wait_ge(S["tap_done"], 2 * TAPS)
        for key, a, w in (("mu", 0, NLAT), ("muc", CTXC, NCTX)):
            b = filled(dve, key)
            for m in range(2):
                ins = v.scalar_tensor_tensor(acc[:, m, a:a + w], b[:, 0:w], -1.0 / 256, acc[:, m, a:a + w], ALU.mult, ALU.add)
            ins.then_inc(S["evac_d"], 1)
        for key, a, w in (("var", 0, NLAT), ("varc", NLAT, NCTX)):
            b = filled(dve, key)
            v.tensor_scalar(rs[:, a:a + w], b[:, 0:w], 1.0 / 256, EPS, ALU.mult, ALU.add).then_inc(S["evac_d"], 1)
        dve.wait_ge(S["sd_ready"], 1)
        link(v.reciprocal(rs, rs))
        for m in range(2):
            v.tensor_tensor(acc[:, m, 0:NLAT], acc[:, m, 0:NLAT], rs[:, 0:NLAT], ALU.mult)
            ins = v.tensor_tensor(acc[:, m, CTXC:CTXC + NCTX], acc[:, m, CTXC:CTXC + NCTX], rs[:, NLAT:NTOK], ALU.mult)
        ins.then_inc(S["yn_ready"], 1)

        def norm(u):
            dve.wait_ge(S["pv_done"], 4 * u + 4 if u < 8 else PAIRS + 4 * (u - 7))
            ob = bank[6 + u % 2][:, 0:260].rearrange("p (h e) -> p h e", h=4)
            link(v.reciprocal(rw[:, 4 * u:4 * u + 4], ob[:, :, DH]))
            if u % 2 == 0 and u >= 2:
                filled(dve, "aT", u // 2 - 1)
            if u == 0:
                dve.wait_ge(S["kcache_out"], 16)
            if u < 8:
                dst = at[:, (u % 2) * 256:(u % 2) * 256 + 256].rearrange("p (h e) -> p h e", h=4)
            else:
                dst = at.rearrange("p (q j e) -> p j q e", q=4, j=2)[:, u - 8]
            v.tensor_tensor(dst, ob[:, :, 0:DH],
                            rw[:, 4 * u:4 * u + 4].unsqueeze(2).to_broadcast([P, 4, DH]), ALU.mult).then_inc(S["o_free"], 1)

        for i in range(PAIRS + 4):
            if i < PAIRS:
                b = filled(dve, "S", i)
                link(v.tensor_reduce(st[:, 0, i:i + 1], b[:, 256:512], AX.X, ALU.max))
                dve.wait_ge(S["bm_ready"], i + 1)
                if i >= 4:
                    filled(dve, "PT", i - 4)
                link(v.tensor_tensor_reduce(pr[:, i % 4, 0:256], b[:, 0:256], bm[:, i % 4, :], 1.0, st[:, 0, i:i + 1],
                                            ALU.add, ALU.max, st[:, 1, i:i + 1]))
                v.tensor_scalar(st[:, 2, i:i + 1], st[:, 1, i:i + 1], -1.0, None, ALU.mult).then_inc(S["smax_done"], 1)
            if i >= 3 and (i - 3) % 4 == 3:
                norm((i - 3) // 4)
        for j in range(2):
            b = filled(dve, "Sc", j)
            four = b[:, :].rearrange("p (h n) -> p h n", h=4)
            link(v.tensor_reduce(st[:, 0, 4 * j:4 * j + 4], four, AX.X, ALU.max))
            filled(dve, "PT", PAIRS - 1)
            v.tensor_tensor(pr[:, j, :].rearrange("p (h n) -> p h n", h=4), four,
                            st[:, 0, 4 * j:4 * j + 4].unsqueeze(2).to_broadcast([P, 4, P]),
                            ALU.subtract).then_inc(S["evac_d"], 1)
        norm(8)
        norm(9)

        for i in range(TT):
            if i == 0:
                dve.wait_ge(S["bc_in"], 16 * 4)
            for hf in range(2):
                b = filled(dve, "wo", i, hf)
                cols = slice(512 * hf, 512 * hf + 512)
                v.tensor_tensor(rtmp, b[:, :], bc[:, 0 if i < 4 else 1, cols], ALU.mult).then_inc(S["evac_d"], 1)
                emptied(dve, "wo", i, hf)
                ins = v.tensor_tensor(x[:, i, cols], x[:, i, cols], rtmp, ALU.add)
                if hf == 0:
                    link(ins)
                else:
                    ins.then_inc(S["x1_ready"], 1)
            dve.wait_ge(S["ssq2_ready"], i + 1)
            v.tensor_scalar(ss[:, 0, i:i + 1], ss[:, 0, i:i + 1], 1.0 / D, EPS, ALU.mult, ALU.add).then_inc(S["ms2_ready"], 1)
            dve.wait_ge(S["sqrt2_ready"], i + 1)
            link(v.reciprocal(ss[:, 2, i:i + 1], ss[:, 1, i:i + 1]))
            if i == 4:
                dve.wait_ge(S["bc2_in"], 16 * 2)
            if i >= 2:
                dve.wait_ge(h2_out[i % 2], 16 * (i // 2))
                filled(dve, "hT", i - 2, 1)
            v.scalar_tensor_tensor(h2[:, i % 2, :], x[:, i, :], ss[:, 2, i:i + 1], bc[:, 2, :] if i < 4 else bc2[:, 0, :],
                                   ALU.mult, ALU.mult).then_inc(S["hn_ready"], 1)

        emptied(dve, "lg", TT - 1)
        dve.wait_ge(S["small_in"], 16 * 3)
        n = TT * NE
        aff = rw[:, 0:n]
        W = ra[:, 4736:5120]
        sel, cnt, hot = W[:, 0:n], W[:, n:2 * n], rw[:, n:3 * n].rearrange("p (k n) -> p k n", k=2)
        sel2, tmp = W[:, 2 * n:3 * n], W[:, 3 * n:4 * n]
        misc = W[:, 4 * n:4 * n + 64]
        gsc, gcnt, ing = misc[:, 0:20], misc[:, 20:40], misc[:, 40:60]

        def three(ap):
            return ap.rearrange("p (i e) -> p i e", i=TT)

        def beats(values, groups, out):
            w = 16 * groups
            mine = values.rearrange("p (g e) -> p g e", g=groups).unsqueeze(3).to_broadcast([P, groups, 4, 4])
            other = values.rearrange("p (g e) -> p g e", g=groups).unsqueeze(2).to_broadcast([P, groups, 4, 4])
            more, same = (z[:, 0:w].rearrange("p (g e f) -> p g e f", g=groups, e=4) for z in (pa_, pb_))
            link(v.tensor_tensor(more, other, mine, ALU.is_gt))
            link(v.tensor_tensor(same, other, mine, ALU.is_equal))
            tie = K("tie").unsqueeze(1).to_broadcast([P, groups, 16])
            sf, mf = (z[:, 0:w].rearrange("p (g f) -> p g f", g=groups) for z in (pb_, pa_))
            link(v.tensor_tensor(sf, sf, tie, ALU.mult))
            link(v.tensor_tensor(mf, mf, sf, ALU.add))
            link(v.tensor_reduce(out, pa_[:, 0:w].rearrange("p (g f) -> p g f", f=4), AX.X, ALU.add))

        link(v.tensor_tensor(three(sel), three(aff), br[:, :].unsqueeze(1).to_broadcast([P, TT, NE]), ALU.add))
        beats(sel, TT * NG, cnt)
        link(v.scalar_tensor_tensor(tmp, cnt, 2.0, sel, ALU.is_lt, ALU.mult))
        link(v.tensor_reduce(gsc, tmp.rearrange("p (g e) -> p g e", e=EPG), AX.X, ALU.add))
        beats(gsc, TT, gcnt)
        link(v.tensor_scalar(ing, gcnt, 0.0, None, ALU.is_equal))
        in_g = ing.unsqueeze(2).to_broadcast([P, TT * NG, EPG])
        for k in range(2):
            link(v.scalar_tensor_tensor(hot[:, k].rearrange("p (g e) -> p g e", e=EPG), cnt.rearrange("p (g e) -> p g e", e=EPG),
                                        float(k), in_g, ALU.is_equal, ALU.mult))
            link(v.tensor_tensor(tmp, aff, hot[:, k], ALU.mult))
            link(v.tensor_reduce(wts[:, k, :], three(tmp), AX.X, ALU.add))
        link(v.tensor_tensor(misc[:, 0:TT], wts[:, 0, :], wts[:, 1, :], ALU.add))
        link(v.reciprocal(misc[:, 8:8 + TT], misc[:, 0:TT]))
        for k in range(2):
            link(v.tensor_tensor(wts[:, k, :], wts[:, k, :], misc[:, 8:8 + TT], ALU.mult))
        v.tensor_tensor(sel2, hot[:, 0], hot[:, 1], ALU.add).then_inc(S["route_ready"], 1)
        b = filled(dve, "rank")
        rank, rows = cnt, misc[:, 0:NE]
        v.tensor_copy(rank, b[:, 0:n])
        evac(rows, b[:, n:n + NE])
        emptied(dve, "rank")
        nov = misc[:, 16:32]
        link(v.tensor_scalar(nov, rows, float(P), None, ALU.is_gt))
        for q in range(2, TT):
            link(v.scalar_tensor_tensor(nov, rows, float(P * q), nov, ALU.is_gt, ALU.add))
        pf = pa_[:, 0:64].rearrange("p (b n) -> p b n", b=2)
        link(v.memset(pa_[:, 0:64], 0.0))
        link(v.tensor_copy(pf[:, 0, 16:32], nov))
        for q, d in enumerate((1, 2, 4, 8)):
            link(v.tensor_tensor(pf[:, 1 - q % 2, 16:32], pf[:, q % 2, 16:32], pf[:, q % 2, 16 - d:32 - d], ALU.add))
        upto = pf[:, 0, 16:32]
        off = misc[:, 32:48]
        link(v.tensor_tensor(off, upto, nov, ALU.subtract))
        q10 = pb_[:, 0:160].rearrange("p (q k i) -> p q k i", q=16, k=2)
        ex, rk, ofs, jt, row, til, ov, tt_, sl = (q10[:, q] for q in range(9))
        for k in range(2):
            for dst, vals in ((ex, K("iota")[:, 0:NE].unsqueeze(1).to_broadcast([P, TT, NE])), (rk, three(rank)),
                              (ofs, off.unsqueeze(1).to_broadcast([P, TT, NE]))):
                link(v.tensor_tensor(three(tmp), three(hot[:, k]), vals, ALU.mult))
                link(v.tensor_reduce(dst[:, k], three(tmp), AX.X, ALU.add))
        link(v.tensor_scalar(jt, rk, float(P), None, ALU.is_ge))
        for q in range(2, TT):
            link(v.scalar_tensor_tensor(jt, rk, float(P * q), jt, ALU.is_ge, ALU.add))
        link(v.scalar_tensor_tensor(row, jt, -float(P), rk, ALU.mult, ALU.add))
        link(v.tensor_scalar(ov, jt, 0.0, None, ALU.is_gt))
        link(v.tensor_tensor(tt_, ofs, ex, ALU.subtract))
        link(v.scalar_tensor_tensor(tt_, tt_, float(NE - 1), jt, ALU.add, ALU.add))
        link(v.tensor_tensor(tt_, tt_, ov, ALU.mult))
        link(v.tensor_tensor(til, ex, tt_, ALU.add))
        link(v.scalar_tensor_tensor(sl, til, float(P), row, ALU.mult, ALU.add))
        link(v.tensor_copy(slot_u[:, :, :], sl))
        for k in range(2):
            for c in range(TT):
                v.tensor_scalar(rowhot[:, k * TT + c, :], K("iota"), row[:, k, c:c + 1], None, ALU.is_equal)
                ins = v.tensor_scalar(tilehot[:, k * TT + c, :], K("iotat"), til[:, k, c:c + 1],
                                      K("tok")[:, c:c + 1], ALU.is_equal, ALU.mult)
        ins.then_inc(S["hot_ready"], 1)
        b = filled(dve, "table")
        evac(ridx[:, :], b[:, 0:NT])
        tv = pa_[:, 64:64 + 160].rearrange("p (j e) -> p j e", j=MAXOV)
        jj = K("iota")[:, 0:MAXOV].unsqueeze(2).to_broadcast([P, MAXOV, NE])

        def row16(ap):
            return ap.unsqueeze(1).to_broadcast([P, MAXOV, NE])

        tu = W[:, 0:160].rearrange("p (j e) -> p j e", j=MAXOV)
        link(v.tensor_tensor(tv, jj, row16(off), ALU.is_ge))
        link(v.tensor_tensor(tu, jj, row16(upto), ALU.is_lt))
        link(v.tensor_tensor(tv, tv, tu, ALU.mult))
        link(v.tensor_tensor(tv, tv, row16(K("iota")[:, 0:NE]), ALU.mult))
        fo = misc[:, 48:64]
        link(v.tensor_reduce(fo[:, 1:1 + MAXOV], tv, AX.X, ALU.add))
        link(v.tensor_copy(fo[:, 0:1], upto[:, 15:16]))
        v.tensor_copy(oi[:, 0:1 + MAXOV], fo[:, 0:1 + MAXOV]).then_inc(S["oi_ready"], 1)

        def xt_out(i, b):
            dve.wait_ge(S["xt_full"], i * 4 + (2 * b + 2))
            ge(dve, "gu_full", i * 4 + (2 * b - 2))
            v.tensor_copy(xt[:, b, 4:8, :], bank[1][:, :].rearrange("p (k n) -> p k n", k=4)).then_inc(S["xt_evac_d"], 1)

        def tiles(i, b):
            for hf in range(2):
                dve.wait_ge(S["silu_done"], i * 4 + (2 * b + hf + 1))
                if hf == 0:
                    ge(dve, "y_full", i * 4 + (2 * b - 2))
                v.tensor_tensor(hid[:, b, 2 * hf:2 * hf + 2, :], gs[:, hf, :].rearrange("p (f n) -> p f n", f=2),
                                bank[2 + hf][:, 256:512].rearrange("p (f n) -> p f n", f=2),
                                ALU.mult).then_inc(S["hid_done"], 1)
            xt_out(i + b, 1 - b)
            dve.wait_ge(S["y_full"], i * 4 + (2 * b + 2))
            ge(dve, y_out[b], i * 16)
            v.tensor_copy(yo[:, b, 512:1024], bank[5 + 2 * b][:, :]).then_inc(S["y_evac_d"], 1)

        xt_out(0, 0)
        over_tiles(dve, tiles)

        for c in range(TT):
            dve.wait_ge(fy_in[c], 32)
            link(v.tensor_scalar(fy[:, c, 0, :], fy[:, c, 0, :], wts[:, 0, c:c + 1], None, ALU.mult))
            v.scalar_tensor_tensor(fy[:, c, 0, :], fy[:, c, 1, :], wts[:, 1, c:c + 1], fy[:, c, 0, :],
                                   ALU.mult, ALU.add).then_inc(S["fsum_ready"], 1)

            def finish(c):
                dve.wait_ge(S["fmul_ready"], c + 1)
                v.tensor_tensor(x[:, c, :], x[:, c, :], fy[:, c, 0, :], ALU.add).then_inc(S["x2_ready"], 1)
                dve.wait_ge(S["ssq3_ready"], c + 1)
                v.tensor_scalar(ss[:, 0, c:c + 1], ss[:, 0, c:c + 1], 1.0 / D, EPS, ALU.mult, ALU.add).then_inc(S["ms3_ready"], 1)
                dve.wait_ge(S["sqrt3_ready"], c + 1)
                link(v.reciprocal(ss[:, 2, c:c + 1], ss[:, 1, c:c + 1]))
                v.scalar_tensor_tensor(fy[:, c, 1, :], x[:, c, :], ss[:, 2, c:c + 1], bc[:, 2, :],
                                       ALU.mult, ALU.mult).then_inc(S["out_ready"], 1)
            if c == 0:
                dve.wait_ge(S["bcend_in"], 16 * 3)
            if c >= 1:
                finish(c - 1)
        finish(TT - 1)

    @block.gpsimd
    def _(pool):
        link = chained(pool, "pool_chain")
        g = nc.gpsimd
        g.memset(cond[:, :, :], 0.0).then_inc(S["cond_zero"], 1)
        link(g.memset(rprow[0:120, :], 0.0))
        pool.dma_start(rprow[0:120, 8:8 + 31], t["rpb"][0].rearrange("h a b -> (h a) b")).then_inc(S["rpb_in"], 16)
        g.memset(poolw[:, :, :], 0.0).then_inc(S["rpad_ready"], 1)
        g.memset(vl[:, :, :, DH:DH + 1], 1.0)
        g.memset(vc[:, :, :, DH:DH + 1], 1.0)
        g.memset(vp[:, :, DH:DH + 1], 1.0).then_inc(S["ones_ready"], 1)
        g.memset(rc[:, 0:2 * LP], 0.0).then_inc(S["pads_ready"], 1)
        g.memset(cuts[11], 0.0).then_inc(S["zeros_ready"], 1)
        pool.wait_ge(S["rpad_ready"], 1)
        for q in range(4):
            a, m = 64 * (q % 2), q // 2
            pool.dma_start(poolw[a:a + 64, m, a:a + 64], t["pool_w"][0, q]).then_inc(S["poolw_in"], 16)
        pool.wait_ge(S["rpb_in"], 16)
        pool.dma_start(t["rpad"], rprow[0:120, :]).then_inc(S["rpad_out"], 16)
        pool.wait_ge(S["rpad_out"], 16)
        rp = t["rpad"].rearrange("(h a) w -> h a w", h=H)
        for qr in range(ROWS):
            pool.dma_start(t["rwin"][qr], rp[:, 7 - qr:15 - qr, :]).then_inc(S["rwin_out"], 16)
        pool.wait_ge(S["rwin_out"], 16 * ROWS)
        for gq in range(2):
            for qc in range(GC):
                a = 15 - 8 * gq - qc
                pool.dma_start(cuts[8][64 * gq + qc:64 * gq + 64:8, :].rearrange("p (n w) -> p n w", w=32),
                               t["rwin"].rearrange("q h a w -> q (h a) w")[:, :, a:a + 32]).then_inc(S["raw_in"], 16)
        filled(pool, "xT", TT - 1, 1)
        g.memset(re[:, 0:e0], 0.0).then_inc(S["pads_ready"], 1)

        def modulation(vec):
            emptied(pool, "adT", 2 * vec + 1)
            m = mod[:, vec, :, :]
            ins = g.tensor_tensor(m, m, V("b_ada")[:, 8 * vec:8 * vec + 8].unsqueeze(1).to_broadcast([P, 2, KD]), ALU.add)
            if vec in (1, 4):
                link(ins)
                link(g.tensor_scalar(m, m, 1.0, None, ALU.add))
                ins = g.tensor_tensor(m, m, V("norm1_g" if vec == 1 else "norm2_g").unsqueeze(1).to_broadcast([P, 2, KD]),
                                      ALU.mult)
            ins.then_inc(S["mod_ready"], 1)

        pool.wait_ge(S["evac_d"], 1)
        modulation(0)
        modulation(1)
        pool.wait_ge(S["h_ready"], KD)
        g.tensor_copy(hT0[:, :, 0:64], hT[:, :, NLAT - 64:NLAT])
        g.tensor_copy(hT0[:, :, 64:128], hT[:, :, 0:64]).then_inc(S["h0_ready"], 1)
        emptied(pool, "pac")
        seg = ((PADP, 0, NLAT), (CTXP + PADP, NLAT, NCTX))

        def mean(src, m, half):
            p = slice(64 * half, 64 * half + 64)
            for a, b, w in seg:
                link(g.tensor_scalar(df[p, m, b:b + w], src[p, m, a:a + w], K("invw")[p, m:m + 1], None, ALU.mult))

        pool.wait_ge(S["cst_in"], 16)
        link(g.tensor_tensor(s1[:, :, 1:LP], up[:, :, 0:LP - 1], up[:, :, 1:LP], ALU.add))
        mean(s1, 0, 0)
        link(g.tensor_tensor(s2[:, :, 2:LP - 1], s1[:, :, 1:LP - 2], s1[:, :, 3:LP], ALU.add))
        mean(s2, 0, 1)
        link(g.tensor_tensor(s1[:, :, 4:LP - 3], s2[:, :, 2:LP - 5], s2[:, :, 6:LP - 1], ALU.add))
        mean(s1, 1, 0)
        link(g.tensor_tensor(s2[:, :, 8:LP - 7], s1[:, :, 4:LP - 11], s1[:, :, 12:LP - 3], ALU.add))
        mean(s2, 1, 1)
        edge = K("edge").rearrange("p (m s n) -> p m s n", m=2, s=2)
        for a, b, w in seg:
            link(g.tensor_tensor(df[:, :, b:b + 8], df[:, :, b:b + 8], edge[:, :, 0, :], ALU.mult))
            link(g.tensor_tensor(df[:, :, b + w - 8:b + w], df[:, :, b + w - 8:b + w], edge[:, :, 1, :], ALU.mult))
            ins = g.tensor_tensor(df[:, :, b:b + w], df[:, :, b:b + w], up[:, :, a:a + w], ALU.subtract)
        ins.then_inc(S["df_ready"], 1)
        for vec in range(2, 6):
            modulation(vec)
        emptied(pool, "vc")
        pool.dma_start(t["new_v"][0, 0], vp[:, :, 0:DH]).then_inc(S["vcache_out"], 16)
        emptied(pool, "ko")
        pool.dma_start(t["new_k"][0, 0].rearrange("n h e -> n (h e)"), at).then_inc(S["kcache_out"], 16)

        def row(vec, who):
            r = (2 * vec + who) * KD
            return t["modr"][r:r + KD, :].rearrange("a b -> (a b)").unsqueeze(0).to_broadcast([P, D])

        pool.wait_ge(S["raw_in"], 16 * 16)
        for s in range(PAIRS):
            if s >= 4:
                pool.wait_ge(S["smax_done"], s - 3)
            tile, h = s // H, s % H
            var = (0, 1, 1, 2)[tile]
            g.tensor_tensor(bm[:, s % 4, :].rearrange("p (g r c) -> p g r c", g=4, r=8),
                            raw[:, h, :, :].rearrange("p r (g c) -> p g r c", g=4),
                            K("mask")[:, 256 * var:256 * var + 256].rearrange("p (g r c) -> p g r c", g=4, r=8),
                            ALU.add).then_inc(S["bm_ready"], 1)
            if s == 7:
                emptied(pool, "modT")
                pool.dma_start(t["modr"], mrow).then_inc(S["mrow_out"], 16)
            if s == 10:
                pool.wait_ge(S["mrow_out"], 16)
                for q, (vec, who) in enumerate(((0, 1), (0, 0), (2, 1), (1, 1))):
                    pool.dma_start(bc[:, q, :], row(vec, who)).then_inc(S["bc_in"], 16)
        emptied(pool, "aT", 4)
        for q, vec in enumerate((2, 1)):
            pool.dma_start(bc2[:, q, :], row(vec, 0)).then_inc(S["bc2_in"], 16)
        for i in range(TT):
            pool.wait_ge(S["hn_ready"], i + 1)
            if i == TT - 1:
                pool.wait_ge(S["bc2_in"], 16 * 2)
            g.tensor_tensor(h2[:, i % 2, :], h2[:, i % 2, :], bc[:, 3, :] if i < 4 else bc2[:, 1, :],
                            ALU.add).then_inc(S["h2_ready"], 1)
            pool.wait_ge(S["h2_ready"], i + 1)
            pool.dma_start(t["h2d"][i * P:(i + 1) * P, :], h2[:, i % 2, :]).then_inc(h2_out[i % 2], 16)
        for q, src in enumerate((row(3, 1), row(3, 0), t["final_g"].rearrange("(a n) -> a n", a=1).to_broadcast([P, D]))):
            pool.dma_start(bc[:, q, :], src).then_inc(S["bcend_in"], 16)

        pool.wait_ge(h2_out[0], 16 * 3)
        pool.wait_ge(h2_out[1], 16 * 2)
        emptied(pool, "table")

        def gather(b, tile):
            g.tensor_copy(gi[:, b:b + 1], ridx[:, bass.ds(tile, 1)]).then_inc(S["gi_ready"], 1)
            pool.wait_ge(S["gi_ready"], tile + 1)
            pool.sem_inc(S["gi_seen"], 1)
            g.indirect_dma_start(xg[:, b, :], None, t["h2d"],
                                 bass.IndirectOffsetOnAxis(ap=gi[:, b:b + 1], axis=0)).then_inc(xg_in[b], 16)

        gather(0, 0)
        gather(1, 1)

        def tiles(i, b):
            pool.wait_ge(S["xt_full"], i * 4 + (2 * b + 2))
            gather(b, i * 2 + (2 + b))

        def overflow(i, b):
            tiles(i, b)
            pool.wait_ge(xg_in[b], i * 16 + 32)
            pool.sem_inc(S["xg_seen"], 1)

        over_tiles(pool, tiles, overflow)
        for b in range(2):
            pool.wait_ge(xg_in[b], 16 * (NE // 2 + 1))
        pool.wait_ge(S["moe_stored"], 1)
        for c in range(TT):
            for k in range(2):
                g.indirect_dma_start(fy[:, c, k, :], None, t["yd"],
                                     bass.IndirectOffsetOnAxis(ap=slot_u[:, k, c:c + 1], axis=0)).then_inc(fy_in[c], 16)
        pool.wait_ge(S["bcend_in"], 48)
        for c in range(TT):
            pool.wait_ge(S["fsum_ready"], c + 1)
            g.tensor_tensor(fy[:, c, 0, :], fy[:, c, 0, :], bc[:, 0 if c < 4 else 1, :], ALU.mult).then_inc(S["fmul_ready"], 1)
        pool.wait_ge(S["vcache_out"], 16)

    @block.tensor
    def _(pe):
        mm = nc.tensor.matmul

        def take(*key):
            n = NTH[key]
            if n >= RING:
                emptied(pe, *PLAN[n - RING][0])
            return bank[n % RING]

        def give(ins):
            ins.then_inc(S["psum_full"], 1)

        def slot(*key):
            n = LOADNO[key]
            pe.wait_ge(w_slot[n % 3], 16 * (n // 3 + 1))
            return slots[:, n % 3, :]

        def transposes(key, tiles):
            b = take(*key)
            for q, ap in enumerate(tiles):
                ins = nc.tensor.transpose(b[:, q * P:(q + 1) * P], ap, ident)
            give(ins)

        pe.wait_ge(S["vec_in"], 16 * (len(VR) + 1))
        pe.wait_ge(S["cst_in"], 16)
        b = take("vec")
        give(nc.tensor.transpose(b[:, 0:NVEC], vrow[0:NVEC, :], ident[0:NVEC, 0:NVEC]))
        b = take("cw")
        give(nc.tensor.transpose(b[:, 0:2 * TAPS], cwrow[0:2 * TAPS, :], ident[0:2 * TAPS, 0:2 * TAPS]))
        for i in range(TT):
            pe.wait_ge(S["xn_ready"], i + 1)
            for hf in range(2):
                transposes(("xT", i, hf), [xn[:, i % 2, (4 * hf + q) * P:(4 * hf + q + 1) * P] for q in range(4)])

        def ada(j):
            w = slot("ada", j).rearrange("p (k n) -> p k n", k=KD)
            if j == 0:
                pe.wait_ge(S["cond_ready"], 1)
            b = take("ada", j)
            for k in range(KD):
                for q in range(4):
                    ins = mm(b[32 * q:32 * q + 32, 0:P], cond[:, k, :], w[:, k, q * P:(q + 1) * P],
                             start=k == 0, stop=k == KD - 1)
            give(ins)

        def adT(j):
            emptied(pe, "ada", j)
            b = take("adT", j)
            give(nc.tensor.transpose(b[:, 0:P], adr[:, j % 2, :], ident))

        def project(load, latent, prompt, width=512):
            w = slot("in", load)[:, 0:KD * width].rearrange("p (k n) -> p k n", k=KD)
            n = width // P
            for m in range(n):
                b = take(latent, m)
                for k in range(KD):
                    if load == 3 and m == 0:
                        pe.wait_ge(S["h_ready"], k + 1)
                    ins = mm(b[:, :], w[:, k, m * P:(m + 1) * P], hT[:, k, 0:NLAT], start=k == 0, stop=k == KD - 1)
                give(ins)
            b = take(prompt)
            for m in range(n):
                for k in range(KD):
                    ins = mm(b[:, m * P:(m + 1) * P], w[:, k, m * P:(m + 1) * P], hT[:, k, NLAT:NTOK],
                             start=k == 0, stop=k == KD - 1)
            give(ins)

        for j in range(4):
            ada(j)
            adT(j)
        project(3, "pa", "pac")
        project(4, "g", "gc", 256)
        ada(4)
        ada(5)
        project(0, "q", "qc")
        adT(4)
        adT(5)
        ada(6)
        ada(7)
        pe.wait_ge(S["cachek_in"], 16)
        for i in range(2):
            transposes(("ck", i), [ckr[:, i, q * P:(q + 1) * P] for q in range(4)])
        project(1, "k", "kc")
        adT(6)
        adT(7)
        ada(8)
        ada(9)

        def channel_sums(key, pieces):
            b = take(key)
            for m, ap in enumerate(pieces):
                ins = mm(b[:, 0:ap.shape[1]], K("ones"), ap, start=m == 0, stop=m == 1)
            give(ins)

        pe.wait_ge(S["tap_done"], 2 * TAPS)
        channel_sums("mu", [acc[:, m, 0:NLAT] for m in range(2)])
        channel_sums("muc", [acc[:, m, CTXC:CTXC + NCTX] for m in range(2)])
        w = slot("in", 2).rearrange("p (k n) -> p k n", k=KD)
        pe.wait_ge(S["h0_ready"], 1)
        for j in range(5):
            b = take("v", j) if j < 4 else take("vc")
            for k in range(KD):
                lhs = hT0[:, k, :] if j == 0 else hT[:, k, P * j - 64:P * j + 64] if j < 4 else hT[:, k, NLAT:NTOK]
                ins = mm(b[:, :], lhs, w[:, k, :], start=k == 0, stop=k == KD - 1)
            give(ins)
            if j == 1:
                pe.wait_ge(S["sq_ready"], 1)
                channel_sums("var", [sg[:, m, 0:NLAT] for m in range(2)])
                channel_sums("varc", [sg[:, m, NLAT:NTOK] for m in range(2)])
        adT(8)
        adT(9)
        ada(10)
        ada(11)
        transposes(("ko",), [kpT[:, m, :] for m in range(4)])
        pe.wait_ge(S["df_ready"], 1)
        pe.wait_ge(S["poolw_in"], 16 * 4)
        pe.wait_ge(S["small_in"], 16 * 3)
        for m in range(2):
            b = take("pl", m)
            give(mm(b[:, :], poolw[:, m, :], df[:, m, 0:NLAT], start=True, stop=True))
        b = take("plc")
        for m in range(2):
            ins = mm(b[:, m * P:(m + 1) * P], poolw[:, m, :], df[:, m, NLAT:NTOK], start=True, stop=True)
        give(ins)

        adT(10)
        adT(11)
        pe.wait_ge(S["act_ready"], 1)
        for m in range(2):
            b = take("pw", m)
            for k in range(2):
                ins = mm(b[:, :], pww[:, k, m * P:(m + 1) * P], sg[:, k, 0:NLAT], start=k == 0, stop=k == 1)
            give(ins)
        b = take("pwc")
        for m in range(2):
            for k in range(2):
                ins = mm(b[:, m * P:(m + 1) * P], pww[:, k, m * P:(m + 1) * P], sg[:, k, NLAT:NTOK], start=k == 0, stop=k == 1)
        give(ins)

        def aT(i):
            pe.wait_ge(S["o_free"], 2 * i + 2)
            transposes(("aT", i), [at[:, m * P:(m + 1) * P] for m in range(4)])

        def o_bank(u):
            if u >= 2:
                pe.wait_ge(S["o_free"], u - 1)
            return bank[6 + u % 2]

        emptied(pe, "k", 3)
        pe.wait_ge(S["cachev_in"], 32)
        for i in range(PAIRS + 4):
            if i < PAIRS:
                tile, h = i // H, i % H
                p = slice(64 * (h % 2), 64 * (h % 2) + 64)
                b = take("S", i)
                q = qT[p, h // 2, tile * P:(tile + 1) * P]
                mm(b[:, 0:256], q, kT[p, h // 2, tile * P:tile * P + 256], start=True, stop=True)
                give(mm(b[:, 256:512], q, kcT[p, h // 2, :], start=True, stop=True))
            if 2 <= i < PAIRS + 2:
                emptied(pe, "S", i - 2)
                transposes(("PT", i - 2), [pr[:, (i - 2) % 4, q * P:(q + 1) * P] for q in range(4)])
            if 3 <= i < PAIRS + 3:
                s = i - 3
                tile, h = s // H, s % H
                ob = o_bank(s // 4) if s % 4 == 0 else bank[6 + (s // 4) % 2]
                emptied(pe, "PT", s)
                vals = [vl[:, tile, h, :], vl[:, (tile + 1) % 4, h, :], vc[:, 0, h, :], vc[:, 1, h, :]]
                for q in range(4):
                    ins = mm(ob[:, 65 * (h % 4):65 * (h % 4) + 65], pts[:, s % 2, q * P:(q + 1) * P], vals[q],
                             start=q == 0, stop=q == 3)
                ins.then_inc(S["pv_done"], 1)
            if i == 4:
                pe.wait_ge(S["mod_ready"], 6)
                b = take("modT")
                give(nc.tensor.transpose(b[0:64, 0:P], mod[:, 2:6, :, :].rearrange("p v s k -> p (v s k)"), ident))
            if i >= 4 and (i - 4) % 8 == 7:
                aT((i - 4) // 8)
        for j in range(2):
            b = take("Sc", j)
            for q in range(4):
                p = slice(64 * j, 64 * j + 64)
                ins = mm(b[:, q * P:(q + 1) * P], qT[p, q, NLAT:NTOK], kpT[p, q, :], start=True, stop=True)
            give(ins)
        for j in range(2):
            pe.wait_ge(S["expc_done"], j + 1)
            transposes(("PTc", j), [pr[:, j, q * P:(q + 1) * P] for q in range(4)])
        for j in range(2):
            emptied(pe, "PTc", j)
            ob = o_bank(8 + j)
            for q in range(4):
                mm(ob[:, 65 * q:65 * q + 65], pts[:, j, q * P:(q + 1) * P], vp[:, 2 * q + j, :],
                   start=True, stop=True).then_inc(S["pv_done"], 1)
        aT(4)

        wo = [slot("out", j).rearrange("p (k n) -> p k n", k=4) for j in range(2)]
        emptied(pe, "aT", 4)
        for i in range(TT + LAG):
            if i < TT:
                for hf in range(2):
                    b = take("wo", i, hf)
                    for k in range(KD):
                        ins = mm(b[:, :], mT[:, k, i * P:(i + 1) * P], wo[k // 4][:, k % 4, 512 * hf:512 * hf + 512],
                                 start=k == 0, stop=k == KD - 1)
                    give(ins)
            if i >= LAG:
                c = i - LAG
                pe.wait_ge(S["h2_ready"], c + 1)
                for hf in range(2):
                    transposes(("hT", c, hf), [h2[:, c % 2, (4 * hf + q) * P:(4 * hf + q + 1) * P] for q in range(4)])
                emptied(pe, "hT", c, 1)
                b = take("lg", c)
                for k in range(KD):
                    ins = mm(b[:, 0:NE], h2T[:, k, c * P:(c + 1) * P], wr[:, k, :], start=k == 0, stop=k == KD - 1)
                give(ins)
        n = TT * NE
        sel2 = ra[:, 4736 + 2 * n:4736 + 3 * n]
        pe.wait_ge(S["route_ready"], 1)
        b = take("rank")
        for c in range(TT):
            for d in range(c + 1):
                mm(b[:, c * NE:(c + 1) * NE], K("tri") if d == c else K("ones"), sel2[:, d * NE:(d + 1) * NE],
                   start=d == 0, stop=d == c)
        for d in range(TT):
            ins = mm(b[:, n:n + NE], K("ones"), sel2[:, d * NE:(d + 1) * NE], start=d == 0, stop=d == TT - 1)
        give(ins)
        pe.wait_ge(S["hot_ready"], 1)
        b = take("table")
        for q in range(10):
            ins = mm(b[:, 0:NT], rowhot[:, q, :], tilehot[:, q, :], start=q == 0, stop=q == 9)
        give(ins)
        emptied(pe, "table")

        def xT(i, b):
            pe.wait_ge(xg_in[b], i * 16 + 16)
            ge(pe, "xt_evac_a", i * 2 + b)
            ge(pe, "xt_evac_d", i * 2 + b)
            for hf in range(2):
                for q in range(4):
                    ins = nc.tensor.transpose(bank[hf][:, q * P:(q + 1) * P], xg[:, b, 4 * hf + q:D:KD], ident)
                ins.then_inc(S["xt_full"], 1)

        def weights(i, b, q):
            if b:
                pe.wait_ge(w_odd[q], i * 16 + 16)
            else:
                pe.wait_ge(w_slot[EVEN[q]], i * 16 + 16 * (EVEN_BASE[q] + 1))
            return wset[b][q].rearrange("p (k n) -> p k n", k=KD if q < 2 else FC)

        def tiles(i, b):
            w = [weights(i, b, 0), weights(i, b, 1)]
            pe.wait_ge(S["xt_evac_a"], i * 2 + (b + 1))
            pe.wait_ge(S["xt_evac_d"], i * 2 + (b + 1))
            for hf in range(2):
                ge(pe, "hid_done", i * 4 + (2 * b + hf - 1))
                for q in range(2):
                    for f in range(2):
                        for k in range(KD):
                            ins = mm(bank[2 + hf][:, (2 * q + f) * P:(2 * q + f + 1) * P],
                                     w[q][:, k, 2 * hf + f:DFF:FC], xt[:, b, k, :], start=k == 0, stop=k == KD - 1)
                ins.then_inc(S["gu_full"], 1)
            xT(i + b, 1 - b)
            wd = weights(i, b, 2)
            pe.wait_ge(S["hid_done"], i * 4 + (2 * b + 2))
            ge(pe, "y_evac_a", i * 2 + (b - 1))
            ge(pe, "y_evac_d", i * 2 + (b - 1))
            for hf in range(2):
                for f in range(FC):
                    ins = mm(bank[4 + 2 * b + hf][:, :], hid[:, b, f, :], wd[:, f, 512 * hf:512 * hf + 512],
                             start=f == 0, stop=f == FC - 1)
                ins.then_inc(S["y_full"], 1)

        xT(0, 0)
        over_tiles(pe, tiles)

    ctx.close()


_INS = ["x_prompt", "x_sample", "cache_k", "cache_v", "c", "c_ctx", "w_ada", "b_ada", "norm1_g", "norm2_g", "w_in",
        "w_out", "rpb", "pool_w", "pool_scale", "conv_w", "conv_b", "conv_ln_g", "conv_ln_b", "conv_pw_w",
        "conv_pw_b", "w_router", "b_router", "moe_w_gate", "moe_w_up", "moe_w_down", "final_g"]
_OUTS = [("y_prompt", (1, NCTX, D)), ("y_sample", (1, NLAT, D)), ("new_k", (1, 1, NCTX, H, DH)),
         ("new_v", (1, 1, NCTX, H, DH))]
_SCRATCH = [("h2d", (NTOK, D)), ("yd", (BIG * P, D)), ("modr", (64, P)), ("rpad", (120, 48)), ("rwin", (8, H, 8, 48))]


def kernel(**inputs):
    import numpy as _np
    import concourse.bacc as _bacc
    from concourse.bass_utils import run_bass_kernel_spmd as _run

    nc = _bacc.Bacc("TRN2", target_bir_lowering=False, num_devices=1)
    arrays, t = {}, {}
    for name in _INS + ["consts"]:
        a = shape_constants() if name == "consts" else _np.ascontiguousarray(inputs[name])
        arrays[f"in_{name}"] = a
        t[name] = nc.dram_tensor(f"in_{name}", a.shape, F32, kind="ExternalInput").ap()
    for name, shape in _OUTS:
        t[name] = nc.dram_tensor(f"out_{name}", shape, F32, kind="ExternalOutput").ap()
    for name, shape in _SCRATCH:
        t[name] = nc.dram_tensor(f"scratch_{name}", shape, F32, kind="Internal").ap()
    build(nc, t)
    r = _run(nc, [arrays], core_ids=[0])
    return tuple(r.results[0][f"out_{name}"] for name, _ in _OUTS)
```

```python
from contextlib import ExitStack

import numpy as np

import concourse.bass as bass
from concourse import mybir
from concourse.alu_op_type import AluOpType as ALU

ACT = mybir.ActivationFunctionType
F32 = mybir.dt.float32
U32 = mybir.dt.uint32
I32 = mybir.dt.int32
AX = mybir.AxisListType

P = 128
D = 1024
KD = D // P
NCTX = 128
NLAT = 512
NTOK = NLAT + NCTX
TT = NTOK // P
ROWS, COLS = 8, 64
G, GC = 8, 8
H, DH = 8, 64
DA = H * DH
PAST = 256
WR, WC = 8, 16
NE, NG, EPG = 16, 4, 4
DFF = 512
FC = DFF // P
TAPS = 31
HALO = TAPS // 2
EPS = 1e-6
NEG = -1e30
PADP = 8
LP = NLAT + 2 * PADP + NCTX + 2 * PADP
LC = NLAT + 2 * HALO + NCTX + 2 * HALO
CTXP = NLAT + 2 * PADP
CTXC = NLAT + 2 * HALO
NACC = LC - 2 * HALO
MAXOV = (2 * NTOK - (P + 1)) // P + 1
MAXOV += MAXOV % 2
NT = NE + MAXOV + 2
BIG = NE + MAXOV
RING = 6

CW = [("ident", P), ("tri", P), ("ones", P), ("iota", P), ("iotat", NT), ("tok", TT), ("tie", 16),
      ("edge", 32), ("invw", 2), ("cols2", 2), ("mask", 3 * 256)]
CO, _o = {}, 0
for _n, _w in CW:
    CO[_n] = (_o, _o + _w)
    _o += _w
CWID = _o

VR = [("c_ctx", 8), ("c", 8), ("norm1_g", 8), ("b_ada", 48)]
VR2 = [("norm2_g", 8), ("pool_scale", 2), ("conv_b", 2), ("conv_ln_g", 2), ("conv_ln_b", 2), ("conv_pw_b", 2)]
VO, _o = {}, 0
for _n, _w in VR:
    VO[_n] = (_o, _w)
    _o += _w
NVEC = _o
_o = 2 * TAPS
for _n, _w in VR2:
    VO[_n] = (_o, _w)
    _o += _w
NCW = _o


def shape_constants():
    c = np.zeros((P, CWID), np.float32)

    def put(name, v):
        c[:, CO[name][0]:CO[name][1]] = v

    p = np.arange(P)
    put("ident", np.eye(P))
    put("tri", p[:, None] < p[None, :])
    put("ones", 1.0)
    put("iota", p[None, :])
    put("iotat", np.arange(NT)[None, :])
    put("tok", p[:, None] + P * np.arange(TT)[None, :])
    put("tie", (np.arange(4)[None, :] < np.arange(4)[:, None]).reshape(1, 16))
    e = np.ones((P, 2, 2, 8))
    w_of = np.array([[2, 4], [8, 16]])
    for ch in range(2):
        for half in range(2):
            w = w_of[ch, half]
            for i in range(8):
                e[64 * half:64 * half + 64, ch, 0, i] = w / min(w, i + w // 2)
                e[64 * half:64 * half + 64, ch, 1, i] = w / min(w, 8 - i + w // 2)
    put("edge", e.reshape(P, 32))
    put("invw", 1.0 / w_of.T[p // 64])
    put("cols2", 0.0)
    gq, qc = p // 64, p % 8
    k = np.arange(256)
    gk, kc = k // 64, k % 8
    m = np.zeros((P, 3, 256))
    for v, t in enumerate((0, 1, 3)):
        qcol = (2 * t + gq) * 8 + qc
        kcol = (2 * t - 1 + gk) * 8 + kc
        cs = np.clip(qcol - WC // 2, 0, COLS - WC)
        ok = (kcol[None] >= cs[:, None]) & (kcol[None] < cs[:, None] + WC) & (kcol[None] >= 0) & (kcol[None] < COLS)
        m[:, v] = np.where(ok, 0.0, NEG)
    put("mask", m.reshape(P, 768))
    return c


def fill_plan():
    plan = [(("vec",), "D")]
    for j in range(2):
        plan += [(("ada", j), "A"), (("adT", j), "A")]
    plan += [(("xT", i, h), "AD"[h]) for i in range(TT) for h in range(2)] + [(("cw",), "D")]
    for j in range(2, 4):
        plan += [(("ada", j), "A"), (("adT", j), "A")]
    plan += [(("pa", m), "A") for m in range(4)] + [(("pac",), "A"), (("ada", 4), "A")]
    plan += [(("g", m), "A") for m in range(2)] + [(("gc",), "A"), (("adT", 4), "A"), (("ada", 5), "A")]
    plan += [(("q", m), "A") for m in range(4)] + [(("qc",), "A"), (("adT", 5), "A"), (("ada", 6), "A")]
    plan += [(("ck", i), "A") for i in range(2)]
    plan += [(("k", m), "A") for m in range(4)] + [(("kc",), "A"), (("adT", 6), "A"), (("ada", 7), "A")]
    plan += [(("mu",), "D"), (("muc",), "D")]
    plan += [(("v", m), "A") for m in range(2)] + [(("var",), "D"), (("varc",), "D")]
    plan += [(("v", m), "A") for m in range(2, 4)] + [(("vc",), "A"), (("adT", 7), "A"), (("ada", 8), "A")]
    plan += [(("ko",), "A"), (("pl", 0), "A"), (("pl", 1), "A"), (("plc",), "A"), (("adT", 8), "A")]
    for i in range(PAIRS + 4):
        if i < PAIRS:
            plan.append((("S", i), "A"))
        if i in BESIDE:
            plan.append((BESIDE[i], "D" if BESIDE[i][0] in ("Sc", "wo") else "A"))
        if 2 <= i < PAIRS + 2:
            plan.append((("PT", i - 2), "A"))
        if i >= 4 and (i - 4) % 8 == 7:
            plan.append((("aT", (i - 4) // 8), "A"))
    plan += [(("PTc", 0), "A"), (("PTc", 1), "A"), (("wo", 0, 1), "D"), (("wo", 1, 0), "D"), (("aT", 4), "A")]
    for i in range(1, TT + LAG):
        if 1 < i < TT:
            plan.append((("wo", i, 0), "D"))
        if i >= LAG:
            plan += [(("hT", i - LAG, 0), "A"), (("hT", i - LAG, 1), "A")]
        if i < TT:
            plan.append((("wo", i, 1), "D"))
        if i >= LAG:
            plan.append((("lg", i - LAG), "A"))
    plan += [(("rank",), "D"), (("table",), "D")]
    return plan


LAG = 2
PAIRS = 4 * H
BESIDE = {1: ("pw", 0), 2: ("pw", 1), 3: ("pwc",), 4: ("ada", 9), 5: ("adT", 9), 7: ("ada", 10), 8: ("adT", 10),
          10: ("ada", 11), 11: ("adT", 11), 18: ("modT",), PAIRS: ("Sc", 0), PAIRS + 1: ("Sc", 1), PAIRS + 3: ("wo", 0, 0)}
PLAN = fill_plan()
NTH = {key: n for n, (key, _) in enumerate(PLAN)}
WHO = {key: who for key, who in PLAN}
TURN = {key: sum(1 for k, w in PLAN[:n + 1] if w == who) for n, (key, who) in enumerate(PLAN)}

LOADS = [(("ada", j), ("ada", j)) for j in range(4)]
LOADS += [(("in", 3), ("pac",)), (("ada", 4), ("ada", 4)), (("in", 4), ("gc",)), (("ada", 5), ("ada", 5)),
          (("in", 0), ("qc",)), (("ada", 6), ("ada", 6)), (("in", 1), ("kc",)), (("in", 2), ("vc",))]
LOADS += [(("ada", j), ("ada", j)) for j in range(7, 12)]
LOADS += [(("out", 0), ("wo", TT - 1, 1)), (("out", 1), ("wo", TT - 1, 1))]
LOADNO = {key: n for n, (key, _) in enumerate(LOADS)}
NLOAD = len(LOADS)
EVEN = [(NLOAD + q) % 3 for q in range(3)]
EVEN_BASE = [len([n for n in range(NLOAD) if n % 3 == s]) for s in EVEN]


def build(nc, t):
    ctx = ExitStack()

    def sb(name, shape, dt=F32):
        return ctx.enter_context(nc.sbuf_tensor(name, shape, dt))

    def sem(name):
        return ctx.enter_context(nc.semaphore(name))

    bank = [ctx.enter_context(nc.psum_tensor(f"bank{i}", [P, 512], F32)) for i in range(8)]

    slots = sb("slots", [P, 3, 4096])
    x = sb("x", [P, TT, D])
    ra = sb("ra", [P, KD * NTOK])
    rb = sb("rb", [P, 16984])
    rc = sb("rc", [P, KD * NTOK])
    re = sb("re", [P, 5440])
    cst = sb("cst", [P, CWID])
    vecT = sb("vecT", [P, NVEC])
    cwT = sb("cwT", [P, NCW])
    cond = sb("cond", [P, KD, 32])
    adr = sb("adr", [P, P])
    mod = sb("mod", [P, 6, 2, KD])
    poolw = sb("poolw", [P, 2, P])
    pww = sb("pww", [P, 2, 256])
    wr = sb("wr", [P, KD, NE])
    br = sb("br", [P, NE])
    st = sb("st", [P, 3, 32])
    ss = sb("ss", [P, 3, TT])
    ridx = sb("ridx", [P, NT], U32)
    gi = sb("gi", [P, 2], U32)
    slot_u = sb("slot_u", [P, 2, TT], U32)
    wts = sb("wts", [P, 2, TT])
    oi = sb("oi", [P, 16], I32)

    def K(name):
        return cst[:, CO[name][0]:CO[name][1]]

    def V(name):
        return (vecT if name in dict(VR) else cwT)[:, VO[name][0]:VO[name][0] + VO[name][1]]

    ident = K("ident")
    hT = ra[:, :].rearrange("p (k n) -> p k n", k=KD)
    bc = ra[:, 0:4096].rearrange("p (b n) -> p b n", b=4)
    cuts, o = [], 0
    for n in (4 * NTOK, 4 * 640, 4 * PAST, 4 * NCTX, 4 * 520, 520, 2 * 520, 512, H * 256, 1024, 2048, 1024):
        cuts.append(rb[:, o:o + n])
        o += n
    assert o <= 16984
    qT, kT, kcT, kpT = (v.rearrange("p (m n) -> p m n", m=4) for v in cuts[0:4])
    vl = cuts[4].rearrange("p (j h e) -> p j h e", j=4, h=H)
    vp = cuts[5].rearrange("p (h e) -> p h e", h=H)
    vc = cuts[6].rearrange("p (j h e) -> p j h e", j=2, h=H)
    at = cuts[7]
    raw = cuts[8].rearrange("p (h r w) -> p h r w", h=H, r=8)
    bm = cuts[9].rearrange("p (b n) -> p b n", b=4)
    pr = cuts[10].rearrange("p (b n) -> p b n", b=4)
    pts = cuts[11].rearrange("p (b n) -> p b n", b=2)
    hT0 = cuts[9].rearrange("p (k n) -> p k n", k=KD)
    ckr = cuts[10][:, 0:1024].rearrange("p (j n) -> p j n", j=2)
    odd = rb[:, 0:12288].rearrange("p (q n) -> p q n", q=3)
    bc2 = rb[:, 12288:14336].rearrange("p (b n) -> p b n", b=2)
    h2 = rb[:, 14336:16384].rearrange("p (b n) -> p b n", b=2)
    rowhot = rb[:, 12288:12288 + 10 * P].rearrange("p (b n) -> p b n", b=10)
    tilehot = rb[:, 13568:13568 + 10 * NT].rearrange("p (b n) -> p b n", b=10)
    up, s1, s2 = (rc[:, i * 2 * LP:(i + 1) * 2 * LP].rearrange("p (m n) -> p m n", m=2) for i in range(3))
    mT = rc[:, :].rearrange("p (k n) -> p k n", k=KD)
    xn = re[:, 0:2048].rearrange("p (b n) -> p b n", b=2)
    junk = re[:, 2048:3072]
    junk2 = ra[:, 4096:5120]
    e0, e1, e2, e3 = 2 * LC, 2 * LC + 2 * NTOK, 2 * LC + 2 * NTOK + 2 * NACC, 2 * LC + 4 * NTOK + 2 * NACC
    yc = re[:, 0:e0].rearrange("p (m n) -> p m n", m=2)
    sg = re[:, e0:e1].rearrange("p (m n) -> p m n", m=2)
    acc = re[:, e1:e2].rearrange("p (m n) -> p m n", m=2)
    df = re[:, e2:e3].rearrange("p (m n) -> p m n", m=2)
    rs = re[:, 0:NTOK]
    mrow = re[0:64, 5312:5440]
    vrow, cwrow, rprow = re[:, 5000:5128], re[:, 5128:5256], re[:, 5256:5304]
    h2T = re[:, 0:5120].rearrange("p (k n) -> p k n", k=KD)
    xg = rc[:, 0:2048].rearrange("p (b n) -> p b n", b=2)
    xt = rc[:, 2048:4096].rearrange("p (b k n) -> p b k n", b=2, k=KD)
    hid = rc[:, 4096:5120].rearrange("p (b f n) -> p b f n", b=2, f=FC)
    yo = re[:, 0:2048].rearrange("p (b n) -> p b n", b=2)
    gs = re[:, 2048:2560].rearrange("p (b n) -> p b n", b=2)
    wset = [[slots[:, s, :] for s in EVEN], [odd[:, q, :] for q in range(3)]]
    fy = slots[:, :, :].rearrange("p a b -> p (a b)")[:, 0:2 * TT * D].rearrange("p (c k n) -> p c k n", c=TT, k=2)
    pa_, pb_ = ra[:, 4096:4416], ra[:, 4416:4736]
    rw = re[:, 5120:5440]

    S = {n: sem(n) for n in """cst_in vec_in cw_in small_in poolw_in cachek_in cachev_in rpb_in rpad_out rwin_out raw_in bc_in bc2_in
        psum_full evac_a evac_d cond_zero cond_ready ssq_ready ms_ready sqrt_ready xn_ready mod_ready h_ready h0_ready
        pads_ready rpad_ready ones_ready tap_done df_ready sq_ready sd_ready yn_ready
        act_ready bm_ready smax_done pv_done o_free expc_done mrow_out kcache_out vcache_out
        ssq2_ready ms2_ready sqrt2_ready hn_ready h2_ready route_ready hot_ready ridx_ready oi_ready
        xt_full xt_evac_a xt_evac_d gu_full silu_done hid_done y_full y_evac_a y_evac_d bcend_in
        first_ready x2_ready ssq3_ready ms3_ready sqrt3_ready rms3_ready xn3_ready out_ready last_ready out_done
        zeros_ready zeros_out moe_stored over_stored gi_seen xg_seen gi_ready dve_chain pool_chain act_chain""".split()}
    w_slot = [sem(f"w_slot{i}") for i in range(3)]
    w_odd = [sem(f"w_odd{i}") for i in range(3)]
    x_in = [sem(f"x_in{i}") for i in range(TT)]
    h2_out = [sem(f"h2_out{i}") for i in range(2)]
    xg_in = [sem(f"xg_in{i}") for i in range(2)]
    y_out = [sem(f"y_out{i}") for i in range(2)]
    fy_in = [sem(f"fy_in{i}") for i in range(TT)]

    def chained(eng, name):
        n = [0]

        def link(ins):
            n[0] += 1
            ins.then_inc(S[name], 1)
            eng.wait_ge(S[name], n[0])
        return link

    def filled(eng, *key):
        eng.wait_ge(S["psum_full"], NTH[key] + 1)
        return bank[NTH[key] % RING]

    def emptied(eng, *key):
        eng.wait_ge(S["evac_a" if WHO[key] == "A" else "evac_d"], TURN[key])

    def group(ap):
        return ap.rearrange("p (r g c) -> p g r c", r=ROWS, g=G)

    def ungroup(ap):
        return ap.rearrange("p (g r c) -> p g r c", r=ROWS, g=G)

    def ge(eng, s, n):
        if not (isinstance(n, int) and n <= 0):
            eng.wait_ge(S[s] if isinstance(s, str) else s, n)

    def over_tiles(eng, body, over_body=None):
        for b in range(2):
            body(0, b)
        with eng.Fori(1, NE // 2) as i:
            for b in range(2):
                body(i, b)
        eng.wait_ge(S["oi_ready"], 1)
        more = eng.value_load(oi[0:1, 0:1], min_val=0, max_val=MAXOV)
        for b in range(2):
            with eng.If(more > b):
                (over_body or body)(NE // 2, b)
        with eng.If(more > 2):
            with eng.Fori(NE // 2 + 1, NE // 2 + MAXOV // 2) as i:
                for b in range(2):
                    with eng.If(more > i * 2 + (b - NE)):
                        (over_body or body)(i, b)
                eng.nop()

    block = ctx.enter_context(nc.Block())

    @block.sync
    def _(sp):
        sp.dma_start(cst[:, :], t["consts"]).then_inc(S["cst_in"], 16)
        for n, (key, _) in enumerate(LOADS):
            for i in ((0, 1), (2, 3, 4))[n] if n < 2 else ():
                if i < 4:
                    for g in range(2):
                        sp.dma_start(x[64 * g:64 * g + 64, i, :],
                                     t["x_sample"][0].rearrange("(r g c) d -> g r c d", r=ROWS, g=G)[2 * i + g]).then_inc(x_in[i], 16)
                else:
                    sp.dma_start(x[:, 4, :], t["x_prompt"][0]).then_inc(x_in[4], 16)
            if n == 3:
                sp.dma_start(pww[:, :, :], t["conv_pw_w"][0].rearrange("(k p) n -> p k n", p=P)).then_inc(S["small_in"], 16)
                sp.dma_start(wr[:, :, :], t["w_router"].rearrange("(k p) n -> p k n", p=P)).then_inc(S["small_in"], 16)
                sp.dma_start(br[:, :], t["b_router"].rearrange("(a n) -> a n", a=1).to_broadcast([P, NE])).then_inc(S["small_in"], 16)
            if n == 5:
                sp.dma_start(ckr[:, :, :], t["cache_k"][0, 0].rearrange("(j p) h e -> p j (h e)", p=P)).then_inc(S["cachek_in"], 16)
                for j in range(2):
                    sp.dma_start(vc[:, j, :, 0:DH], t["cache_v"][0, 0, j * P:(j + 1) * P]).then_inc(S["cachev_in"], 16)
            if n >= 3:
                sp.wait_ge(S["psum_full"], NTH[LOADS[n - 3][1]] + 1)
            kind, j = key
            if kind == "ada":
                src = t["w_ada"][0].rearrange("(k p) n -> p k n", p=P)[:, :, 512 * j:512 * j + 512]
            elif kind == "in":
                src = t["w_in"][0].rearrange("(k p) n -> p k n", p=P)[:, :, 512 * j:min(512 * j + 512, 2304)]
            else:
                src = t["w_out"][0].rearrange("(k p) n -> p k n", p=P)[:, 4 * j:4 * j + 4, :]
            if n == 9:
                sp.wait_ge(S["zeros_ready"], 1)
                for q in range(NE, BIG):
                    sp.dma_start(t["yd"][q * P:(q + 1) * P, :], cuts[11]).then_inc(S["zeros_out"], 16)
            k, w = src.shape[1], src.shape[2]
            sp.dma_start(slots[:, n % 3, 0:k * w].rearrange("p (k n) -> p k n", k=k), src).then_inc(w_slot[n % 3], 16)

        def expert(q, e):
            if q < 2:
                return t["moe_w_gate" if q == 0 else "moe_w_up"][0, e].rearrange("(p k) n -> p (k n)", k=KD)
            return t["moe_w_down"][0, e].rearrange("(p k) n -> p (k n)", k=FC)

        def load(b, q, e):
            s = w_odd[q] if b else w_slot[EVEN[q]]
            sp.dma_start(wset[b][q], expert(q, e)).then_inc(s, 16)

        for q in range(3):
            sp.wait_ge(S["psum_full"], NTH[LOADS[NLOAD - 3 + q][1]] + 1)
            load(0, q, 0)
            if q == 0:
                emptied(sp, "aT", 4)
                for r in range(3):
                    load(1, r, 1)

        def store(b, tile):
            sp.wait_ge(S["y_evac_a"], tile + 1)
            sp.wait_ge(S["y_evac_d"], tile + 1)
            sp.dma_start(t["yd"][bass.ds(tile * P, P), :], yo[:, b, :]).then_inc(y_out[b], 16)

        with sp.Fori(0, NE // 2 - 1) as i:
            for b in range(2):
                tile = i * 2 + b
                sp.wait_ge(S["gu_full"], tile * 2 + 2)
                load(b, 0, tile + 2)
                load(b, 1, tile + 2)
                sp.wait_ge(S["y_full"], tile * 2 + 2)
                load(b, 2, tile + 2)
                store(b, tile)
        sp.wait_ge(S["oi_ready"], 1)
        more = sp.value_load(oi[0:1, 0:1], min_val=0, max_val=MAXOV)

        def load_more(b, tile, n):
            at_n = slice(n + 1, n + 2) if isinstance(n, int) else bass.ds(n + 1, 1)
            e = sp.value_load(oi[0:1, at_n], min_val=0, max_val=NE - 1)
            sp.wait_ge(S["gu_full"], tile * 2 + 2)
            load(b, 0, e)
            load(b, 1, e)
            sp.wait_ge(S["y_full"], tile * 2 + 2)
            load(b, 2, e)

        for b in range(2):
            with sp.If(more > b):
                load_more(b, NE - 2 + b, b)
            store(b, NE - 2 + b)

        def over_pair(i):
            for b in range(2):
                with sp.If(more > i * 2 + (2 + b)):
                    load_more(b, i * 2 + (NE + b), i * 2 + (2 + b))
                with sp.If(more > i * 2 + b):
                    store(b, i * 2 + (NE + b))
                    sp.wait_ge(y_out[b], i * 16 + 16 * (NE // 2 + 1))
                    sp.sem_inc(S["over_stored"], 1)

        over_pair(0)
        with sp.If(more > 2):
            with sp.Fori(1, MAXOV // 2) as i:
                over_pair(i)
                sp.nop()
        for b in range(2):
            sp.wait_ge(y_out[b], 16 * (NE // 2))
        sp.sem_inc(S["moe_stored"], 1)

        for c in range(TT):
            if c < TT - 1:
                sp.wait_ge(S["out_ready"], c + 1)
            else:
                sp.wait_ge(S["last_ready"], 1)
            if c < 4:
                for g in range(2):
                    sp.dma_start(t["y_sample"][0].rearrange("(r g c) d -> g r c d", r=ROWS, g=G)[2 * c + g],
                                 fy[64 * g:64 * g + 64, c, 1, :]).then_inc(S["out_done"], 16)
            else:
                sp.dma_start(t["y_prompt"][0], fy[:, c, 1, :]).then_inc(S["out_done"], 16)
        sp.wait_ge(S["out_done"], 16 * 9)

    @block.scalar
    def _(act):
        link = chained(act, "act_chain")
        sc = nc.scalar

        def evac(out, in_, func=ACT.Copy, last=True, **kw):
            ins = sc.activation(out, in_, func, **kw)
            if last:
                ins.then_inc(S["evac_a"], 1)

        o = 0
        for name, rows in VR:
            src = t[name]
            if len(src.shape) == 2:
                src = src[0]
            act.dma_start(vrow[o:o + rows, :], src.rearrange("(a p) -> a p", p=P)).then_inc(S["vec_in"], 16)
            o += rows

        emptied(act, "vec")
        act.wait_ge(S["cond_zero"], 1)
        sc.activation(cond[:, :, 0], V("c_ctx"), ACT.Silu)
        sc.activation(cond[:, :, 1], V("c"), ACT.Silu).then_inc(S["cond_ready"], 1)

        def ada(j):
            if j >= 1:
                filled(act, "adT", j - 1)
            b = filled(act, "ada", j)
            evac(adr[:, :], b[:, 0:P])

        def adT(j):
            b = filled(act, "adT", j)
            evac(mod[:, j // 2, :, 4 * (j % 2):4 * (j % 2) + 4],
                 b[:, 0:P].rearrange("p (q s) -> p s q", q=4)[:, 0:2, :])

        for i in range(TT):
            act.wait_ge(x_in[i], 32 if i < 4 else 16)
            ins = sc.activation(junk, x[:, i, :], ACT.Square, accum_out=ss[:, 0, i:i + 1])
            if i < TT - 1:
                link(ins)
            if i == 1:
                ada(0)
                adT(0)
        ins.then_inc(S["ssq_ready"], 1)
        act.wait_ge(S["ms_ready"], 1)
        sc.activation(ss[:, 1, :], ss[:, 0, :], ACT.Sqrt).then_inc(S["sqrt_ready"], 1)
        ada(1)
        adT(1)
        for i in range(TT):
            b = filled(act, "xT", i, 0)
            evac(hT[:, 0:4, i * P:(i + 1) * P], b[:, :].rearrange("p (k n) -> p k n", k=4))

        for j in range(2, 4):
            ada(j)
            adT(j)
        act.wait_ge(S["pads_ready"], 2)
        for m in range(4):
            b = filled(act, "pa", m)
            dst = up[:, m, PADP:PADP + NLAT] if m < 2 else yc[:, m - 2, HALO:HALO + NLAT]
            evac(group(dst), ungroup(b[:, :]))
        b = filled(act, "pac")
        four = b[:, :].rearrange("p (m n) -> p m n", m=4)
        evac(up[:, :, CTXP + PADP:CTXP + PADP + NCTX], four[:, 0:2], last=False)
        evac(yc[:, :, CTXC + HALO:CTXC + HALO + NCTX], four[:, 2:4])
        ada(4)
        for m in range(2):
            b = filled(act, "g", m)
            evac(group(sg[:, m, 0:NLAT]), ungroup(b[:, :]), ACT.Sigmoid)
        b = filled(act, "gc")
        evac(sg[:, :, NLAT:NTOK], b[:, 0:256].rearrange("p (m n) -> p m n", m=2), ACT.Sigmoid)
        adT(4)
        ada(5)
        for m in range(4):
            b = filled(act, "q", m)
            evac(qT[:, m, 0:NLAT], b[:, :], scale=DH ** -0.5)
        b = filled(act, "qc")
        evac(qT[:, :, NLAT:NTOK], b[:, :].rearrange("p (m n) -> p m n", m=4), scale=DH ** -0.5)
        adT(5)
        ada(6)
        for i in range(2):
            b = filled(act, "ck", i)
            evac(kcT[:, :, i * P:(i + 1) * P], b[:, :].rearrange("p (m n) -> p m n", m=4))
        for m in range(4):
            b = filled(act, "k", m)
            evac(kT[:, m, 64:NLAT], b[:, 0:NLAT - 64], last=False)
            evac(kT[:, m, 0:64], b[:, NLAT - 64:NLAT], last=False)
            evac(kT[:, m, NLAT:NLAT + 64], b[:, NLAT - 64:NLAT], last=False)
            evac(kT[:, m, NLAT + 64:NLAT + 128], b[:, 0:64])
        b = filled(act, "kc")
        evac(kpT[:, :, :], b[:, :].rearrange("p (m n) -> p m n", m=4))
        adT(6)
        ada(7)
        act.wait_ge(S["ones_ready"], 1)

        def swish():
            act.wait_ge(S["yn_ready"], 1)
            for m in range(2):
                for dst, src in ((sg[:, m, 0:NLAT], acc[:, m, 0:NLAT]),
                                 (sg[:, m, NLAT:NTOK], acc[:, m, CTXC:CTXC + NCTX])):
                    ins = sc.activation(dst, src, ACT.Silu, scale=V("conv_ln_g")[:, m:m + 1], bias=V("conv_ln_b")[:, m:m + 1])
            ins.then_inc(S["act_ready"], 1)

        emptied(act, "muc")
        sc.activation(sg[:, :, 0:NLAT], acc[:, :, 0:NLAT], ACT.Square)
        sc.activation(sg[:, :, NLAT:NTOK], acc[:, :, CTXC:CTXC + NCTX], ACT.Square).then_inc(S["sq_ready"], 1)
        for j in range(4):
            b = filled(act, "v", j)
            evac(vl[:, j, :, 0:DH], b[:, :].rearrange("p (h e) -> p h e", h=H))
            if j == 2:
                emptied(act, "varc")
                sc.activation(rs, rs, ACT.Sqrt).then_inc(S["sd_ready"], 1)
        swish()
        b = filled(act, "vc")
        evac(vp[:, :, 0:DH], b[:, :].rearrange("p (h e) -> p h e", h=H))
        adT(7)
        ada(8)
        b = filled(act, "ko")
        evac(at, b[:, :])
        for m in range(2):
            b = filled(act, "pl", m)
            evac(ungroup(mT[:, 4 + m, 0:NLAT]), group(b[:, :]), ACT.Identity, scale=V("pool_scale")[:, m:m + 1])
        b = filled(act, "plc")
        for m in range(2):
            evac(mT[:, 4 + m, NLAT:NTOK], b[:, m * P:(m + 1) * P], ACT.Identity, last=m == 1,
                 scale=V("pool_scale")[:, m:m + 1])
        adT(8)

        def pw(m):
            b = filled(act, "pw", m)
            evac(ungroup(mT[:, 6 + m, 0:NLAT]), group(b[:, :]), ACT.Identity, bias=V("conv_pw_b")[:, m:m + 1])

        def pwc():
            b = filled(act, "pwc")
            for m in range(2):
                evac(mT[:, 6 + m, NLAT:NTOK], b[:, m * P:(m + 1) * P], ACT.Identity, last=m == 1,
                     bias=V("conv_pw_b")[:, m:m + 1])

        def modT():
            b = filled(act, "modT")
            evac(mrow, b[0:64, 0:P])

        beside = {"pw": pw, "pwc": pwc, "ada": ada, "adT": adT, "modT": modT}

        def aT(i):
            b = filled(act, "aT", i)
            evac(mT[:, 0:4, i * P:(i + 1) * P], b[:, :].rearrange("p (m n) -> p m n", m=4))

        act.wait_ge(S["zeros_out"], 16 * MAXOV)
        for i in range(PAIRS + 4):
            if i < PAIRS:
                act.wait_ge(S["smax_done"], i + 1)
                b = filled(act, "S", i)
                nmx = st[:, 2, i:i + 1]
                sc.activation(pr[:, i % 4, 0:256], pr[:, i % 4, 0:256], ACT.Exp, bias=nmx)
                evac(pr[:, i % 4, 256:512], b[:, 256:512], ACT.Exp, bias=nmx)
            if i in BESIDE and BESIDE[i][0] in beside:
                beside[BESIDE[i][0]](*BESIDE[i][1:])
            if 2 <= i < PAIRS + 2:
                s = i - 2
                if s >= 2:
                    act.wait_ge(S["pv_done"], s - 1)
                b = filled(act, "PT", s)
                evac(pts[:, s % 2, :], b[:, :])
            if i > PAIRS and BESIDE.get(i - 1, "-")[0] == "Sc":
                j = BESIDE[i - 1][1]
                emptied(act, "Sc", j)
                sc.activation(pr[:, j, :], pr[:, j, :], ACT.Exp).then_inc(S["expc_done"], 1)
            if i >= 4 and (i - 4) % 8 == 7:
                aT((i - 4) // 8)
        for j in range(2):
            act.wait_ge(S["pv_done"], PAIRS - 1 + j)
            b = filled(act, "PTc", j)
            evac(pts[:, j, :], b[:, :])

        def rms2(i):
            emptied(act, "wo", i, 1)
            if i >= 1:
                act.wait_ge(S["ssq2_ready"], i)
            sc.activation(junk2, x[:, i, :], ACT.Square, accum_out=ss[:, 0, i:i + 1]).then_inc(S["ssq2_ready"], 1)
            act.wait_ge(S["ms2_ready"], i + 1)
            sc.activation(ss[:, 1, i:i + 1], ss[:, 0, i:i + 1], ACT.Sqrt).then_inc(S["sqrt2_ready"], 1)

        def h2_out_of_psum(i):
            for hf in range(2):
                b = filled(act, "hT", i, hf)
                evac(h2T[:, 4 * hf:4 * hf + 4, i * P:(i + 1) * P], b[:, :].rearrange("p (k n) -> p k n", k=4))

        rms2(0)
        aT(4)
        for i in range(1, TT + LAG):
            if i >= LAG:
                h2_out_of_psum(i - LAG)
            if i < TT:
                rms2(i)
            if i >= LAG:
                b = filled(act, "lg", i - LAG)
                evac(rw[:, (i - LAG) * NE:(i - LAG + 1) * NE], b[:, 0:NE], ACT.Sigmoid)

        def xt_out(i, b):
            act.wait_ge(S["xt_full"], i * 4 + (2 * b + 1))
            ge(act, "gu_full", i * 4 + (2 * b - 2))
            sc.activation(xt[:, b, 0:4, :], bank[0][:, :].rearrange("p (k n) -> p k n", k=4),
                          ACT.Copy).then_inc(S["xt_evac_a"], 1)

        def tiles(i, b):
            for hf in range(2):
                act.wait_ge(S["gu_full"], i * 4 + (2 * b + hf + 1))
                ge(act, "hid_done", i * 4 + (2 * b + hf - 1))
                sc.activation(gs[:, hf, :], bank[2 + hf][:, 0:256], ACT.Silu).then_inc(S["silu_done"], 1)
            xt_out(i + b, 1 - b)
            act.wait_ge(S["y_full"], i * 4 + (2 * b + 1))
            ge(act, y_out[b], i * 16)
            sc.activation(yo[:, b, 0:512], bank[4 + 2 * b][:, :], ACT.Copy).then_inc(S["y_evac_a"], 1)

        xt_out(0, 0)
        over_tiles(act, tiles)

        for c in range(TT + 2):
            if c < TT:
                act.wait_ge(fy_in[c], 32)
                sc.activation(fy[:, c, 0, :], fy[:, c, 0, :], ACT.Copy, scale=wts[:, 0, c:c + 1]).then_inc(S["first_ready"], 1)
            if c >= 2:
                d = c - 2
                act.wait_ge(S["x2_ready"], d + 1)
                sc.activation(fy[:, d, 1, :], x[:, d, :], ACT.Square, accum_out=ss[:, 0, d:d + 1]).then_inc(S["ssq3_ready"], 1)
                act.wait_ge(S["ms3_ready"], d + 1)
                sc.activation(ss[:, 1, d:d + 1], ss[:, 0, d:d + 1], ACT.Sqrt).then_inc(S["sqrt3_ready"], 1)
                if d < TT - 1:
                    act.wait_ge(S["rms3_ready"], d + 1)
                    sc.activation(fy[:, d, 1, :], x[:, d, :], ACT.Copy, scale=ss[:, 2, d:d + 1]).then_inc(S["xn3_ready"], 1)

    @block.vector
    def _(dve):
        link = chained(dve, "dve_chain")
        v = nc.vector

        def evac(out, in_):
            v.tensor_copy(out, in_).then_inc(S["evac_d"], 1)

        b = filled(dve, "vec")
        evac(vecT[:, :], b[:, 0:NVEC])
        dve.wait_ge(S["ssq_ready"], 1)
        v.tensor_scalar(ss[:, 0, :], ss[:, 0, :], 1.0 / D, EPS, ALU.mult, ALU.add).then_inc(S["ms_ready"], 1)
        dve.wait_ge(S["sqrt_ready"], 1)
        link(v.reciprocal(ss[:, 2, :], ss[:, 1, :]))
        for i in range(TT):
            if i >= 2:
                filled(dve, "xT", i - 2, 1)
            v.tensor_scalar(xn[:, i % 2, :], x[:, i, :], ss[:, 2, i:i + 1], None, ALU.mult).then_inc(S["xn_ready"], 1)
            if i >= 1:
                b = filled(dve, "xT", i - 1, 1)
                evac(hT[:, 4:8, (i - 1) * P:i * P], b[:, :].rearrange("p (k n) -> p k n", k=4))
        b = filled(dve, "xT", TT - 1, 1)
        evac(hT[:, 4:8, (TT - 1) * P:TT * P], b[:, :].rearrange("p (k n) -> p k n", k=4))
        b = filled(dve, "cw")
        evac(cwT[:, :], b[:, 0:NCW])
        dve.wait_ge(S["mod_ready"], 2)
        emptied(dve, "xT", TT - 1, 0)
        emptied(dve, "xT", TT - 1, 1)
        for k in range(KD):
            for s, (a, n) in ((1, (0, NLAT)), (0, (NLAT, NTOK))):
                ins = v.tensor_scalar(hT[:, k, a:n], hT[:, k, a:n], mod[:, 1, s, k:k + 1], mod[:, 0, s, k:k + 1],
                                      ALU.mult, ALU.add)
            ins.then_inc(S["h_ready"], 1)
        emptied(dve, "cw")
        emptied(dve, "gc")
        link(v.tensor_tensor(yc[:, :, HALO:HALO + NLAT], yc[:, :, HALO:HALO + NLAT], sg[:, :, 0:NLAT], ALU.mult))
        link(v.tensor_tensor(yc[:, :, CTXC + HALO:CTXC + HALO + NCTX], yc[:, :, CTXC + HALO:CTXC + HALO + NCTX],
                             sg[:, :, NLAT:NTOK], ALU.mult))
        for m in range(2):
            v.tensor_scalar(acc[:, m, :], yc[:, m, 0:NACC], cwT[:, m:m + 1], V("conv_b")[:, m:m + 1],
                            ALU.mult, ALU.add).then_inc(S["tap_done"], 1)
        with dve.Fori(1, TAPS) as k:
            for m in range(2):
                dve.wait_ge(S["tap_done"], k * 2 + (m - 1))
                v.scalar_tensor_tensor(acc[:, m, :], yc[:, m, bass.ds(k, NACC)], cwT[:, bass.ds(k * 2 + m, 1)],
                                       acc[:, m, :], ALU.mult, ALU.add).then_inc(S["tap_done"], 1)
        dve.wait_ge(S["tap_done"], 2 * TAPS)
        for key, a, w in (("mu", 0, NLAT), ("muc", CTXC, NCTX)):
            b = filled(dve, key)
            for m in range(2):
                ins = v.scalar_tensor_tensor(acc[:, m, a:a + w], b[:, 0:w], -1.0 / 256, acc[:, m, a:a + w], ALU.mult, ALU.add)
            ins.then_inc(S["evac_d"], 1)
        for key, a, w in (("var", 0, NLAT), ("varc", NLAT, NCTX)):
            b = filled(dve, key)
            v.tensor_scalar(rs[:, a:a + w], b[:, 0:w], 1.0 / 256, EPS, ALU.mult, ALU.add).then_inc(S["evac_d"], 1)
        dve.wait_ge(S["sd_ready"], 1)
        link(v.reciprocal(rs, rs))
        for m in range(2):
            v.tensor_tensor(acc[:, m, 0:NLAT], acc[:, m, 0:NLAT], rs[:, 0:NLAT], ALU.mult)
            ins = v.tensor_tensor(acc[:, m, CTXC:CTXC + NCTX], acc[:, m, CTXC:CTXC + NCTX], rs[:, NLAT:NTOK], ALU.mult)
        ins.then_inc(S["yn_ready"], 1)

        def norm(u):
            dve.wait_ge(S["pv_done"], 4 * u + 4 if u < 8 else PAIRS + 4 * (u - 7))
            ob = bank[6 + u % 2][:, 0:260].rearrange("p (h e) -> p h e", h=4)
            link(v.reciprocal(rw[:, 4 * u:4 * u + 4], ob[:, :, DH]))
            if u % 2 == 0 and u >= 2:
                filled(dve, "aT", u // 2 - 1)
            if u == 0:
                dve.wait_ge(S["kcache_out"], 16)
            if u < 8:
                dst = at[:, (u % 2) * 256:(u % 2) * 256 + 256].rearrange("p (h e) -> p h e", h=4)
            else:
                dst = at.rearrange("p (q j e) -> p j q e", q=4, j=2)[:, u - 8]
            v.tensor_tensor(dst, ob[:, :, 0:DH],
                            rw[:, 4 * u:4 * u + 4].unsqueeze(2).to_broadcast([P, 4, DH]), ALU.mult).then_inc(S["o_free"], 1)

        def prompt_scores(j):
            b = filled(dve, "Sc", j)
            four = b[:, :].rearrange("p (h n) -> p h n", h=4)
            link(v.tensor_reduce(st[:, 0, 4 * j:4 * j + 4], four, AX.X, ALU.max))
            filled(dve, "PT", PAIRS - 4 + j)
            v.tensor_tensor(pr[:, j, :].rearrange("p (h n) -> p h n", h=4), four,
                            st[:, 0, 4 * j:4 * j + 4].unsqueeze(2).to_broadcast([P, 4, P]),
                            ALU.subtract).then_inc(S["evac_d"], 1)

        def add_mixed(i, hf):
            if (i, hf) == (0, 0):
                dve.wait_ge(S["bc_in"], 16 * 4)
            b = filled(dve, "wo", i, hf)
            cols = slice(512 * hf, 512 * hf + 512)
            link(v.tensor_tensor(b[:, :], b[:, :], bc[:, 0 if i < 4 else 1, cols], ALU.mult))
            v.tensor_tensor(x[:, i, cols], x[:, i, cols], b[:, :], ALU.add).then_inc(S["evac_d"], 1)

        beside = {"Sc": prompt_scores, "wo": add_mixed}
        for i in range(PAIRS + 4):
            if i < PAIRS:
                b = filled(dve, "S", i)
                link(v.tensor_reduce(st[:, 0, i:i + 1], b[:, 256:512], AX.X, ALU.max))
                dve.wait_ge(S["bm_ready"], i + 1)
                if i >= 4:
                    filled(dve, "PT", i - 4)
                link(v.tensor_tensor_reduce(pr[:, i % 4, 0:256], b[:, 0:256], bm[:, i % 4, :], 1.0, st[:, 0, i:i + 1],
                                            ALU.add, ALU.max, st[:, 1, i:i + 1]))
                v.tensor_scalar(st[:, 2, i:i + 1], st[:, 1, i:i + 1], -1.0, None, ALU.mult).then_inc(S["smax_done"], 1)
            if i in BESIDE and BESIDE[i][0] in beside:
                beside[BESIDE[i][0]](*BESIDE[i][1:])
            if i >= 3 and (i - 3) % 4 == 3:
                norm((i - 3) // 4)

        for i in range(TT):
            if i:
                add_mixed(i, 0)
            add_mixed(i, 1)
            if i == 0:
                norm(8)
                norm(9)
            dve.wait_ge(S["ssq2_ready"], i + 1)
            v.tensor_scalar(ss[:, 0, i:i + 1], ss[:, 0, i:i + 1], 1.0 / D, EPS, ALU.mult, ALU.add).then_inc(S["ms2_ready"], 1)
            dve.wait_ge(S["sqrt2_ready"], i + 1)
            link(v.reciprocal(ss[:, 2, i:i + 1], ss[:, 1, i:i + 1]))
            if i == 0:
                filled(dve, "aT", 4)
            if i == 4:
                dve.wait_ge(S["bc2_in"], 16 * 2)
            if i >= 2:
                dve.wait_ge(h2_out[i % 2], 16 * (i // 2))
                filled(dve, "hT", i - 2, 1)
            v.scalar_tensor_tensor(h2[:, i % 2, :], x[:, i, :], ss[:, 2, i:i + 1], bc[:, 2, :] if i < 4 else bc2[:, 0, :],
                                   ALU.mult, ALU.mult).then_inc(S["hn_ready"], 1)

        emptied(dve, "lg", TT - 1)
        dve.wait_ge(S["small_in"], 16 * 3)
        n = TT * NE
        aff = rw[:, 0:n]
        W = ra[:, 4736:5120]
        sel, cnt, hot = W[:, 0:n], W[:, n:2 * n], rw[:, n:3 * n].rearrange("p (k n) -> p k n", k=2)
        sel2, tmp = W[:, 2 * n:3 * n], W[:, 3 * n:4 * n]
        misc = W[:, 4 * n:4 * n + 64]
        gsc, gcnt, ing = misc[:, 0:20], misc[:, 20:40], misc[:, 40:60]

        def three(ap):
            return ap.rearrange("p (i e) -> p i e", i=TT)

        def beats(values, groups, out):
            w = 16 * groups
            mine = values.rearrange("p (g e) -> p g e", g=groups).unsqueeze(3).to_broadcast([P, groups, 4, 4])
            other = values.rearrange("p (g e) -> p g e", g=groups).unsqueeze(2).to_broadcast([P, groups, 4, 4])
            more, same = (z[:, 0:w].rearrange("p (g e f) -> p g e f", g=groups, e=4) for z in (pa_, pb_))
            link(v.tensor_tensor(more, other, mine, ALU.is_gt))
            link(v.tensor_tensor(same, other, mine, ALU.is_equal))
            tie = K("tie").unsqueeze(1).to_broadcast([P, groups, 16])
            sf, mf = (z[:, 0:w].rearrange("p (g f) -> p g f", g=groups) for z in (pb_, pa_))
            link(v.tensor_tensor(sf, sf, tie, ALU.mult))
            link(v.tensor_tensor(mf, mf, sf, ALU.add))
            link(v.tensor_reduce(out, pa_[:, 0:w].rearrange("p (g f) -> p g f", f=4), AX.X, ALU.add))

        link(v.tensor_tensor(three(sel), three(aff), br[:, :].unsqueeze(1).to_broadcast([P, TT, NE]), ALU.add))
        beats(sel, TT * NG, cnt)
        link(v.scalar_tensor_tensor(tmp, cnt, 2.0, sel, ALU.is_lt, ALU.mult))
        link(v.tensor_reduce(gsc, tmp.rearrange("p (g e) -> p g e", e=EPG), AX.X, ALU.add))
        beats(gsc, TT, gcnt)
        link(v.tensor_scalar(ing, gcnt, 0.0, None, ALU.is_equal))
        in_g = ing.unsqueeze(2).to_broadcast([P, TT * NG, EPG])
        for k in range(2):
            link(v.scalar_tensor_tensor(hot[:, k].rearrange("p (g e) -> p g e", e=EPG), cnt.rearrange("p (g e) -> p g e", e=EPG),
                                        float(k), in_g, ALU.is_equal, ALU.mult))
            link(v.tensor_tensor(tmp, aff, hot[:, k], ALU.mult))
            link(v.tensor_reduce(wts[:, k, :], three(tmp), AX.X, ALU.add))
        link(v.tensor_tensor(misc[:, 0:TT], wts[:, 0, :], wts[:, 1, :], ALU.add))
        link(v.reciprocal(misc[:, 8:8 + TT], misc[:, 0:TT]))
        for k in range(2):
            link(v.tensor_tensor(wts[:, k, :], wts[:, k, :], misc[:, 8:8 + TT], ALU.mult))
        v.tensor_tensor(sel2, hot[:, 0], hot[:, 1], ALU.add).then_inc(S["route_ready"], 1)
        b = filled(dve, "rank")
        rank, rows = cnt, misc[:, 0:NE]
        v.tensor_copy(rank, b[:, 0:n])
        evac(rows, b[:, n:n + NE])
        emptied(dve, "rank")
        nov = misc[:, 16:32]
        link(v.tensor_scalar(nov, rows, float(P), None, ALU.is_gt))
        for q in range(2, TT):
            link(v.scalar_tensor_tensor(nov, rows, float(P * q), nov, ALU.is_gt, ALU.add))
        pf = pa_[:, 0:64].rearrange("p (b n) -> p b n", b=2)
        link(v.memset(pa_[:, 0:64], 0.0))
        link(v.tensor_copy(pf[:, 0, 16:32], nov))
        for q, d in enumerate((1, 2, 4, 8)):
            link(v.tensor_tensor(pf[:, 1 - q % 2, 16:32], pf[:, q % 2, 16:32], pf[:, q % 2, 16 - d:32 - d], ALU.add))
        upto = pf[:, 0, 16:32]
        off = misc[:, 32:48]
        link(v.tensor_tensor(off, upto, nov, ALU.subtract))
        q10 = pb_[:, 0:160].rearrange("p (q k i) -> p q k i", q=16, k=2)
        ex, rk, ofs, jt, row, til, ov, tt_, sl = (q10[:, q] for q in range(9))
        for k in range(2):
            for dst, vals in ((ex, K("iota")[:, 0:NE].unsqueeze(1).to_broadcast([P, TT, NE])), (rk, three(rank)),
                              (ofs, off.unsqueeze(1).to_broadcast([P, TT, NE]))):
                link(v.tensor_tensor(three(tmp), three(hot[:, k]), vals, ALU.mult))
                link(v.tensor_reduce(dst[:, k], three(tmp), AX.X, ALU.add))
        link(v.tensor_scalar(jt, rk, float(P), None, ALU.is_ge))
        for q in range(2, TT):
            link(v.scalar_tensor_tensor(jt, rk, float(P * q), jt, ALU.is_ge, ALU.add))
        link(v.scalar_tensor_tensor(row, jt, -float(P), rk, ALU.mult, ALU.add))
        link(v.tensor_scalar(ov, jt, 0.0, None, ALU.is_gt))
        link(v.tensor_tensor(tt_, ofs, ex, ALU.subtract))
        link(v.scalar_tensor_tensor(tt_, tt_, float(NE - 1), jt, ALU.add, ALU.add))
        link(v.tensor_tensor(tt_, tt_, ov, ALU.mult))
        link(v.tensor_tensor(til, ex, tt_, ALU.add))
        link(v.scalar_tensor_tensor(sl, til, float(P), row, ALU.mult, ALU.add))
        link(v.tensor_copy(slot_u[:, :, :], sl))
        for k in range(2):
            for c in range(TT):
                v.tensor_scalar(rowhot[:, k * TT + c, :], K("iota"), row[:, k, c:c + 1], None, ALU.is_equal)
                ins = v.tensor_scalar(tilehot[:, k * TT + c, :], K("iotat"), til[:, k, c:c + 1],
                                      K("tok")[:, c:c + 1], ALU.is_equal, ALU.mult)
        ins.then_inc(S["hot_ready"], 1)
        b = filled(dve, "table")
        evac(ridx[:, :], b[:, 0:NT])
        tv = pa_[:, 64:64 + 160].rearrange("p (j e) -> p j e", j=MAXOV)
        jj = K("iota")[:, 0:MAXOV].unsqueeze(2).to_broadcast([P, MAXOV, NE])

        def row16(ap):
            return ap.unsqueeze(1).to_broadcast([P, MAXOV, NE])

        tu = W[:, 0:160].rearrange("p (j e) -> p j e", j=MAXOV)
        link(v.tensor_tensor(tv, jj, row16(off), ALU.is_ge))
        link(v.tensor_tensor(tu, jj, row16(upto), ALU.is_lt))
        link(v.tensor_tensor(tv, tv, tu, ALU.mult))
        link(v.tensor_tensor(tv, tv, row16(K("iota")[:, 0:NE]), ALU.mult))
        fo = misc[:, 48:64]
        link(v.tensor_reduce(fo[:, 1:1 + MAXOV], tv, AX.X, ALU.add))
        link(v.tensor_copy(fo[:, 0:1], upto[:, 15:16]))
        v.tensor_copy(oi[:, 0:1 + MAXOV], fo[:, 0:1 + MAXOV]).then_inc(S["oi_ready"], 1)

        def xt_out(i, b):
            dve.wait_ge(S["xt_full"], i * 4 + (2 * b + 2))
            ge(dve, "gu_full", i * 4 + (2 * b - 2))
            v.tensor_copy(xt[:, b, 4:8, :], bank[1][:, :].rearrange("p (k n) -> p k n", k=4)).then_inc(S["xt_evac_d"], 1)

        def tiles(i, b):
            for hf in range(2):
                dve.wait_ge(S["silu_done"], i * 4 + (2 * b + hf + 1))
                if hf == 0:
                    ge(dve, "y_full", i * 4 + (2 * b - 2))
                v.tensor_tensor(hid[:, b, 2 * hf:2 * hf + 2, :], gs[:, hf, :].rearrange("p (f n) -> p f n", f=2),
                                bank[2 + hf][:, 256:512].rearrange("p (f n) -> p f n", f=2),
                                ALU.mult).then_inc(S["hid_done"], 1)
            xt_out(i + b, 1 - b)
            dve.wait_ge(S["y_full"], i * 4 + (2 * b + 2))
            ge(dve, y_out[b], i * 16)
            v.tensor_copy(yo[:, b, 512:1024], bank[5 + 2 * b][:, :]).then_inc(S["y_evac_d"], 1)

        xt_out(0, 0)
        over_tiles(dve, tiles)

        def mean_square(c):
            dve.wait_ge(S["ssq3_ready"], c + 1)
            v.tensor_scalar(ss[:, 0, c:c + 1], ss[:, 0, c:c + 1], 1.0 / D, EPS, ALU.mult, ALU.add).then_inc(S["ms3_ready"], 1)

        def inverse(c):
            dve.wait_ge(S["sqrt3_ready"], c + 1)
            v.reciprocal(ss[:, 2, c:c + 1], ss[:, 1, c:c + 1]).then_inc(S["rms3_ready"], 1)

        dve.wait_ge(S["bcend_in"], 16 * 3)
        for c in range(TT):
            dve.wait_ge(S["first_ready"], c + 1)
            link(v.scalar_tensor_tensor(fy[:, c, 0, :], fy[:, c, 1, :], wts[:, 1, c:c + 1], fy[:, c, 0, :],
                                        ALU.mult, ALU.add))
            if c >= 1:
                mean_square(c - 1)
            link(v.tensor_tensor(fy[:, c, 0, :], fy[:, c, 0, :], bc[:, 0 if c < 4 else 1, :], ALU.mult))
            if c >= 1:
                inverse(c - 1)
            v.tensor_tensor(x[:, c, :], x[:, c, :], fy[:, c, 0, :], ALU.add).then_inc(S["x2_ready"], 1)
        mean_square(TT - 1)
        inverse(TT - 1)
        dve.wait_ge(S["rms3_ready"], TT)
        v.scalar_tensor_tensor(fy[:, TT - 1, 1, :], x[:, TT - 1, :], ss[:, 2, TT - 1:TT], bc[:, 2, :],
                               ALU.mult, ALU.mult).then_inc(S["last_ready"], 1)

    @block.gpsimd
    def _(pool):
        link = chained(pool, "pool_chain")
        g = nc.gpsimd
        g.memset(cond[:, :, :], 0.0).then_inc(S["cond_zero"], 1)
        link(g.memset(rprow[0:120, :], 0.0))
        pool.dma_start(rprow[0:120, 8:8 + 31], t["rpb"][0].rearrange("h a b -> (h a) b")).then_inc(S["rpb_in"], 16)
        pool.dma_start(cwrow[0:2 * TAPS, :], t["conv_w"][0].rearrange("k (m p) -> (k m) p", p=P)).then_inc(S["cw_in"], 16)
        for name, rows in VR2:
            src = t[name]
            if len(src.shape) == 2:
                src = src[0]
            o = VO[name][0]
            pool.dma_start(cwrow[o:o + rows, :], src.rearrange("(a p) -> a p", p=P)).then_inc(S["cw_in"], 16)
        g.memset(poolw[:, :, :], 0.0).then_inc(S["rpad_ready"], 1)
        g.memset(vl[:, :, :, DH:DH + 1], 1.0)
        g.memset(vc[:, :, :, DH:DH + 1], 1.0)
        g.memset(vp[:, :, DH:DH + 1], 1.0).then_inc(S["ones_ready"], 1)
        g.memset(rc[:, 0:2 * LP], 0.0).then_inc(S["pads_ready"], 1)
        g.memset(cuts[11], 0.0).then_inc(S["zeros_ready"], 1)
        pool.wait_ge(S["rpad_ready"], 1)
        for q in range(4):
            a, m = 64 * (q % 2), q // 2
            pool.dma_start(poolw[a:a + 64, m, a:a + 64], t["pool_w"][0, q]).then_inc(S["poolw_in"], 16)
        pool.wait_ge(S["rpb_in"], 16)
        pool.dma_start(t["rpad"], rprow[0:120, :]).then_inc(S["rpad_out"], 16)
        filled(pool, "xT", TT - 1, 1)
        g.memset(re[:, 0:e0], 0.0).then_inc(S["pads_ready"], 1)

        def modulation(vec):
            emptied(pool, "adT", 2 * vec + 1)
            m = mod[:, vec, :, :]
            ins = g.tensor_tensor(m, m, V("b_ada")[:, 8 * vec:8 * vec + 8].unsqueeze(1).to_broadcast([P, 2, KD]), ALU.add)
            if vec in (1, 4):
                link(ins)
                link(g.tensor_scalar(m, m, 1.0, None, ALU.add))
                ins = g.tensor_tensor(m, m, V("norm1_g" if vec == 1 else "norm2_g").unsqueeze(1).to_broadcast([P, 2, KD]),
                                      ALU.mult)
            ins.then_inc(S["mod_ready"], 1)

        pool.wait_ge(S["evac_d"], 1)
        modulation(0)
        modulation(1)
        pool.wait_ge(S["h_ready"], KD)
        g.tensor_copy(hT0[:, :, 0:64], hT[:, :, NLAT - 64:NLAT])
        g.tensor_copy(hT0[:, :, 64:128], hT[:, :, 0:64]).then_inc(S["h0_ready"], 1)
        pool.wait_ge(S["rpad_out"], 16)
        rp = t["rpad"].rearrange("(h a) w -> h a w", h=H)
        for qr in range(ROWS):
            pool.dma_start(t["rwin"][qr], rp[:, 7 - qr:15 - qr, :]).then_inc(S["rwin_out"], 16)
        pool.wait_ge(S["rwin_out"], 16 * ROWS)
        for gq in range(2):
            for qc in range(GC):
                a = 15 - 8 * gq - qc
                pool.dma_start(cuts[8][64 * gq + qc:64 * gq + 64:8, :].rearrange("p (n w) -> p n w", w=32),
                               t["rwin"].rearrange("q h a w -> q (h a) w")[:, :, a:a + 32]).then_inc(S["raw_in"], 16)
        emptied(pool, "pac")
        seg = ((PADP, 0, NLAT), (CTXP + PADP, NLAT, NCTX))

        def mean(src, m, half):
            p = slice(64 * half, 64 * half + 64)
            for a, b, w in seg:
                link(g.tensor_scalar(df[p, m, b:b + w], src[p, m, a:a + w], K("invw")[p, m:m + 1], None, ALU.mult))

        pool.wait_ge(S["cst_in"], 16)
        link(g.tensor_tensor(s1[:, :, 1:LP], up[:, :, 0:LP - 1], up[:, :, 1:LP], ALU.add))
        mean(s1, 0, 0)
        link(g.tensor_tensor(s2[:, :, 2:LP - 1], s1[:, :, 1:LP - 2], s1[:, :, 3:LP], ALU.add))
        mean(s2, 0, 1)
        link(g.tensor_tensor(s1[:, :, 4:LP - 3], s2[:, :, 2:LP - 5], s2[:, :, 6:LP - 1], ALU.add))
        mean(s1, 1, 0)
        link(g.tensor_tensor(s2[:, :, 8:LP - 7], s1[:, :, 4:LP - 11], s1[:, :, 12:LP - 3], ALU.add))
        mean(s2, 1, 1)
        edge = K("edge").rearrange("p (m s n) -> p m s n", m=2, s=2)
        for a, b, w in seg:
            link(g.tensor_tensor(df[:, :, b:b + 8], df[:, :, b:b + 8], edge[:, :, 0, :], ALU.mult))
            link(g.tensor_tensor(df[:, :, b + w - 8:b + w], df[:, :, b + w - 8:b + w], edge[:, :, 1, :], ALU.mult))
            ins = g.tensor_tensor(df[:, :, b:b + w], df[:, :, b:b + w], up[:, :, a:a + w], ALU.subtract)
        ins.then_inc(S["df_ready"], 1)
        modulation(2)
        modulation(3)
        emptied(pool, "vc")
        pool.dma_start(t["new_v"][0, 0], vp[:, :, 0:DH]).then_inc(S["vcache_out"], 16)
        emptied(pool, "ko")
        pool.dma_start(t["new_k"][0, 0].rearrange("n h e -> n (h e)"), at).then_inc(S["kcache_out"], 16)

        def row(vec, who):
            r = (2 * vec + who) * KD
            return t["modr"][r:r + KD, :].rearrange("a b -> (a b)").unsqueeze(0).to_broadcast([P, D])

        pool.wait_ge(S["raw_in"], 16 * 16)
        for s in range(PAIRS):
            if s >= 4:
                pool.wait_ge(S["smax_done"], s - 3)
            tile, h = s // H, s % H
            var = (0, 1, 1, 2)[tile]
            g.tensor_tensor(bm[:, s % 4, :].rearrange("p (g r c) -> p g r c", g=4, r=8),
                            raw[:, h, :, :].rearrange("p r (g c) -> p g r c", g=4),
                            K("mask")[:, 256 * var:256 * var + 256].rearrange("p (g r c) -> p g r c", g=4, r=8),
                            ALU.add).then_inc(S["bm_ready"], 1)
            if s == 11:
                modulation(4)
            if s == 16:
                modulation(5)
            if s == 22:
                emptied(pool, "modT")
                pool.dma_start(t["modr"], mrow).then_inc(S["mrow_out"], 16)
            if s == 25:
                pool.wait_ge(S["mrow_out"], 16)
                for q, (vec, who) in enumerate(((0, 1), (0, 0), (2, 1), (1, 1))):
                    pool.dma_start(bc[:, q, :], row(vec, who)).then_inc(S["bc_in"], 16)
        emptied(pool, "aT", 4)
        for q, vec in enumerate((2, 1)):
            pool.dma_start(bc2[:, q, :], row(vec, 0)).then_inc(S["bc2_in"], 16)
        for i in range(TT):
            pool.wait_ge(S["hn_ready"], i + 1)
            if i == TT - 1:
                pool.wait_ge(S["bc2_in"], 16 * 2)
            g.tensor_tensor(h2[:, i % 2, :], h2[:, i % 2, :], bc[:, 3, :] if i < 4 else bc2[:, 1, :],
                            ALU.add).then_inc(S["h2_ready"], 1)
            pool.wait_ge(S["h2_ready"], i + 1)
            pool.dma_start(t["h2d"][i * P:(i + 1) * P, :], h2[:, i % 2, :]).then_inc(h2_out[i % 2], 16)
        for q, src in enumerate((row(3, 1), row(3, 0), t["final_g"].rearrange("(a n) -> a n", a=1).to_broadcast([P, D]))):
            pool.dma_start(bc[:, q, :], src).then_inc(S["bcend_in"], 16)

        pool.wait_ge(h2_out[0], 16 * 3)
        pool.wait_ge(h2_out[1], 16 * 2)
        emptied(pool, "table")

        def gather(b, tile):
            g.tensor_copy(gi[:, b:b + 1], ridx[:, bass.ds(tile, 1)]).then_inc(S["gi_ready"], 1)
            pool.wait_ge(S["gi_ready"], tile + 1)
            pool.sem_inc(S["gi_seen"], 1)
            g.indirect_dma_start(xg[:, b, :], None, t["h2d"],
                                 bass.IndirectOffsetOnAxis(ap=gi[:, b:b + 1], axis=0)).then_inc(xg_in[b], 16)

        gather(0, 0)
        gather(1, 1)

        def tiles(i, b):
            pool.wait_ge(S["xt_full"], i * 4 + (2 * b + 2))
            gather(b, i * 2 + (2 + b))

        def overflow(i, b):
            tiles(i, b)
            pool.wait_ge(xg_in[b], i * 16 + 32)
            pool.sem_inc(S["xg_seen"], 1)

        over_tiles(pool, tiles, overflow)
        for b in range(2):
            pool.wait_ge(xg_in[b], 16 * (NE // 2 + 1))
        pool.wait_ge(S["moe_stored"], 1)
        for c in range(TT):
            for k in range(2):
                g.indirect_dma_start(fy[:, c, k, :], None, t["yd"],
                                     bass.IndirectOffsetOnAxis(ap=slot_u[:, k, c:c + 1], axis=0)).then_inc(fy_in[c], 16)
        pool.wait_ge(S["bcend_in"], 48)
        for c in range(TT - 1):
            pool.wait_ge(S["xn3_ready"], c + 1)
            g.tensor_tensor(fy[:, c, 1, :], fy[:, c, 1, :], bc[:, 2, :], ALU.mult).then_inc(S["out_ready"], 1)
        pool.wait_ge(S["vcache_out"], 16)

    @block.tensor
    def _(pe):
        mm = nc.tensor.matmul

        def take(*key):
            n = NTH[key]
            if n >= RING:
                emptied(pe, *PLAN[n - RING][0])
            return bank[n % RING]

        def give(ins):
            ins.then_inc(S["psum_full"], 1)

        def slot(*key):
            n = LOADNO[key]
            pe.wait_ge(w_slot[n % 3], 16 * (n // 3 + 1))
            return slots[:, n % 3, :]

        def transposes(key, tiles):
            b = take(*key)
            for q, ap in enumerate(tiles):
                ins = nc.tensor.transpose(b[:, q * P:(q + 1) * P], ap, ident)
            give(ins)

        pe.wait_ge(S["vec_in"], 16 * len(VR))
        pe.wait_ge(S["cst_in"], 16)
        b = take("vec")
        give(nc.tensor.transpose(b[:, 0:NVEC], vrow[0:NVEC, :], ident[0:NVEC, 0:NVEC]))

        def ada(j):
            w = slot("ada", j).rearrange("p (k n) -> p k n", k=KD)
            if j == 0:
                pe.wait_ge(S["cond_ready"], 1)
            b = take("ada", j)
            for k in range(KD):
                for q in range(4):
                    ins = mm(b[32 * q:32 * q + 32, 0:P], cond[:, k, :], w[:, k, q * P:(q + 1) * P],
                             start=k == 0, stop=k == KD - 1)
            give(ins)

        def adT(j):
            emptied(pe, "ada", j)
            b = take("adT", j)
            give(nc.tensor.transpose(b[:, 0:P], adr[:, :], ident))

        for j in range(2):
            ada(j)
            adT(j)
        for i in range(TT):
            pe.wait_ge(S["xn_ready"], i + 1)
            for hf in range(2):
                transposes(("xT", i, hf), [xn[:, i % 2, (4 * hf + q) * P:(4 * hf + q + 1) * P] for q in range(4)])

        pe.wait_ge(S["cw_in"], 16 * (len(VR2) + 1))
        b = take("cw")
        give(nc.tensor.transpose(b[:, 0:NCW], cwrow[0:NCW, :], ident[0:NCW, 0:NCW]))

        def project(load, latent, prompt, width=512):
            w = slot("in", load)[:, 0:KD * width].rearrange("p (k n) -> p k n", k=KD)
            n = width // P
            for m in range(n):
                b = take(latent, m)
                for k in range(KD):
                    if load == 3 and m == 0:
                        pe.wait_ge(S["h_ready"], k + 1)
                    ins = mm(b[:, :], w[:, k, m * P:(m + 1) * P], hT[:, k, 0:NLAT], start=k == 0, stop=k == KD - 1)
                give(ins)
            b = take(prompt)
            for m in range(n):
                for k in range(KD):
                    ins = mm(b[:, m * P:(m + 1) * P], w[:, k, m * P:(m + 1) * P], hT[:, k, NLAT:NTOK],
                             start=k == 0, stop=k == KD - 1)
            give(ins)

        for j in range(2, 4):
            ada(j)
            adT(j)
        project(3, "pa", "pac")
        ada(4)
        project(4, "g", "gc", 256)
        adT(4)
        ada(5)
        project(0, "q", "qc")
        adT(5)
        ada(6)
        pe.wait_ge(S["cachek_in"], 16)
        for i in range(2):
            transposes(("ck", i), [ckr[:, i, q * P:(q + 1) * P] for q in range(4)])
        project(1, "k", "kc")
        adT(6)
        ada(7)

        def channel_sums(key, pieces):
            b = take(key)
            for m, ap in enumerate(pieces):
                ins = mm(b[:, 0:ap.shape[1]], K("ones"), ap, start=m == 0, stop=m == 1)
            give(ins)

        pe.wait_ge(S["tap_done"], 2 * TAPS)
        channel_sums("mu", [acc[:, m, 0:NLAT] for m in range(2)])
        channel_sums("muc", [acc[:, m, CTXC:CTXC + NCTX] for m in range(2)])
        w = slot("in", 2).rearrange("p (k n) -> p k n", k=KD)
        pe.wait_ge(S["h0_ready"], 1)
        for j in range(5):
            b = take("v", j) if j < 4 else take("vc")
            for k in range(KD):
                lhs = hT0[:, k, :] if j == 0 else hT[:, k, P * j - 64:P * j + 64] if j < 4 else hT[:, k, NLAT:NTOK]
                ins = mm(b[:, :], lhs, w[:, k, :], start=k == 0, stop=k == KD - 1)
            give(ins)
            if j == 1:
                pe.wait_ge(S["sq_ready"], 1)
                channel_sums("var", [sg[:, m, 0:NLAT] for m in range(2)])
                channel_sums("varc", [sg[:, m, NLAT:NTOK] for m in range(2)])
        adT(7)
        ada(8)
        transposes(("ko",), [kpT[:, m, :] for m in range(4)])
        pe.wait_ge(S["df_ready"], 1)
        pe.wait_ge(S["poolw_in"], 16 * 4)
        pe.wait_ge(S["small_in"], 16 * 3)
        for m in range(2):
            b = take("pl", m)
            give(mm(b[:, :], poolw[:, m, :], df[:, m, 0:NLAT], start=True, stop=True))
        b = take("plc")
        for m in range(2):
            ins = mm(b[:, m * P:(m + 1) * P], poolw[:, m, :], df[:, m, NLAT:NTOK], start=True, stop=True)
        give(ins)

        adT(8)

        def pw(m):
            pe.wait_ge(S["act_ready"], 1)
            b = take("pw", m)
            for k in range(2):
                ins = mm(b[:, :], pww[:, k, m * P:(m + 1) * P], sg[:, k, 0:NLAT], start=k == 0, stop=k == 1)
            give(ins)

        def pwc():
            b = take("pwc")
            for m in range(2):
                for k in range(2):
                    ins = mm(b[:, m * P:(m + 1) * P], pww[:, k, m * P:(m + 1) * P], sg[:, k, NLAT:NTOK],
                             start=k == 0, stop=k == 1)
            give(ins)

        def modT():
            pe.wait_ge(S["mod_ready"], 6)
            b = take("modT")
            give(nc.tensor.transpose(b[0:64, 0:P], mod[:, 2:6, :, :].rearrange("p v s k -> p (v s k)"), ident))

        def prompt_scores(j):
            b = take("Sc", j)
            for q in range(4):
                p = slice(64 * j, 64 * j + 64)
                ins = mm(b[:, q * P:(q + 1) * P], qT[p, q, NLAT:NTOK], kpT[p, q, :], start=True, stop=True)
            give(ins)

        wo = []

        def project_out(i, hf):
            if not wo:
                wo.extend(slot("out", j).rearrange("p (k n) -> p k n", k=4) for j in range(2))
            if hf == 0:
                emptied(pe, "aT", i)
            b = take("wo", i, hf)
            for k in range(KD):
                ins = mm(b[:, :], mT[:, k, i * P:(i + 1) * P], wo[k // 4][:, k % 4, 512 * hf:512 * hf + 512],
                         start=k == 0, stop=k == KD - 1)
            give(ins)

        beside = {"pw": pw, "pwc": pwc, "ada": ada, "adT": adT, "modT": modT, "Sc": prompt_scores, "wo": project_out}

        def aT(i):
            pe.wait_ge(S["o_free"], 2 * i + 2)
            transposes(("aT", i), [at[:, m * P:(m + 1) * P] for m in range(4)])

        def o_bank(u):
            if u >= 2:
                pe.wait_ge(S["o_free"], u - 1)
            return bank[6 + u % 2]

        emptied(pe, "k", 3)
        pe.wait_ge(S["cachev_in"], 32)
        for i in range(PAIRS + 4):
            if i < PAIRS:
                tile, h = i // H, i % H
                p = slice(64 * (h % 2), 64 * (h % 2) + 64)
                b = take("S", i)
                q = qT[p, h // 2, tile * P:(tile + 1) * P]
                mm(b[:, 0:256], q, kT[p, h // 2, tile * P:tile * P + 256], start=True, stop=True)
                give(mm(b[:, 256:512], q, kcT[p, h // 2, :], start=True, stop=True))
            if i in BESIDE:
                beside[BESIDE[i][0]](*BESIDE[i][1:])
            if 2 <= i < PAIRS + 2:
                emptied(pe, "S", i - 2)
                transposes(("PT", i - 2), [pr[:, (i - 2) % 4, q * P:(q + 1) * P] for q in range(4)])
            if 3 <= i < PAIRS + 3:
                s = i - 3
                tile, h = s // H, s % H
                ob = o_bank(s // 4) if s % 4 == 0 else bank[6 + (s // 4) % 2]
                emptied(pe, "PT", s)
                vals = [vl[:, tile, h, :], vl[:, (tile + 1) % 4, h, :], vc[:, 0, h, :], vc[:, 1, h, :]]
                for q in range(4):
                    ins = mm(ob[:, 65 * (h % 4):65 * (h % 4) + 65], pts[:, s % 2, q * P:(q + 1) * P], vals[q],
                             start=q == 0, stop=q == 3)
                ins.then_inc(S["pv_done"], 1)
            if i >= 4 and (i - 4) % 8 == 7:
                aT((i - 4) // 8)
        for j in range(2):
            pe.wait_ge(S["expc_done"], j + 1)
            transposes(("PTc", j), [pr[:, j, q * P:(q + 1) * P] for q in range(4)])
        project_out(0, 1)
        for j in range(2):
            emptied(pe, "PTc", j)
            ob = o_bank(8 + j)
            for q in range(4):
                mm(ob[:, 65 * q:65 * q + 65], pts[:, j, q * P:(q + 1) * P], vp[:, 2 * q + j, :],
                   start=True, stop=True).then_inc(S["pv_done"], 1)
        project_out(1, 0)
        aT(4)

        for i in range(1, TT + LAG):
            c = i - LAG
            if 1 < i < TT:
                project_out(i, 0)
            if c >= 0:
                pe.wait_ge(S["h2_ready"], c + 1)
                for hf in range(2):
                    transposes(("hT", c, hf), [h2[:, c % 2, (4 * hf + q) * P:(4 * hf + q + 1) * P] for q in range(4)])
            if i < TT:
                project_out(i, 1)
            if c >= 0:
                emptied(pe, "hT", c, 1)
                b = take("lg", c)
                for k in range(KD):
                    ins = mm(b[:, 0:NE], h2T[:, k, c * P:(c + 1) * P], wr[:, k, :], start=k == 0, stop=k == KD - 1)
                give(ins)
        n = TT * NE
        sel2 = ra[:, 4736 + 2 * n:4736 + 3 * n]
        pe.wait_ge(S["route_ready"], 1)
        b = take("rank")
        for c in range(TT):
            for d in range(c + 1):
                mm(b[:, c * NE:(c + 1) * NE], K("tri") if d == c else K("ones"), sel2[:, d * NE:(d + 1) * NE],
                   start=d == 0, stop=d == c)
        for d in range(TT):
            ins = mm(b[:, n:n + NE], K("ones"), sel2[:, d * NE:(d + 1) * NE], start=d == 0, stop=d == TT - 1)
        give(ins)
        pe.wait_ge(S["hot_ready"], 1)
        b = take("table")
        for q in range(10):
            ins = mm(b[:, 0:NT], rowhot[:, q, :], tilehot[:, q, :], start=q == 0, stop=q == 9)
        give(ins)
        emptied(pe, "table")

        def xT(i, b):
            pe.wait_ge(xg_in[b], i * 16 + 16)
            ge(pe, "xt_evac_a", i * 2 + b)
            ge(pe, "xt_evac_d", i * 2 + b)
            for hf in range(2):
                for q in range(4):
                    ins = nc.tensor.transpose(bank[hf][:, q * P:(q + 1) * P], xg[:, b, 4 * hf + q:D:KD], ident)
                ins.then_inc(S["xt_full"], 1)

        def weights(i, b, q):
            if b:
                pe.wait_ge(w_odd[q], i * 16 + 16)
            else:
                pe.wait_ge(w_slot[EVEN[q]], i * 16 + 16 * (EVEN_BASE[q] + 1))
            return wset[b][q].rearrange("p (k n) -> p k n", k=KD if q < 2 else FC)

        def tiles(i, b):
            w = [weights(i, b, 0), weights(i, b, 1)]
            pe.wait_ge(S["xt_evac_a"], i * 2 + (b + 1))
            pe.wait_ge(S["xt_evac_d"], i * 2 + (b + 1))
            for hf in range(2):
                ge(pe, "hid_done", i * 4 + (2 * b + hf - 1))
                for q in range(2):
                    for f in range(2):
                        for k in range(KD):
                            ins = mm(bank[2 + hf][:, (2 * q + f) * P:(2 * q + f + 1) * P],
                                     w[q][:, k, 2 * hf + f:DFF:FC], xt[:, b, k, :], start=k == 0, stop=k == KD - 1)
                ins.then_inc(S["gu_full"], 1)
            xT(i + b, 1 - b)
            wd = weights(i, b, 2)
            pe.wait_ge(S["hid_done"], i * 4 + (2 * b + 2))
            ge(pe, "y_evac_a", i * 2 + (b - 1))
            ge(pe, "y_evac_d", i * 2 + (b - 1))
            for hf in range(2):
                for f in range(FC):
                    ins = mm(bank[4 + 2 * b + hf][:, :], hid[:, b, f, :], wd[:, f, 512 * hf:512 * hf + 512],
                             start=f == 0, stop=f == FC - 1)
                ins.then_inc(S["y_full"], 1)

        xT(0, 0)
        over_tiles(pe, tiles)

    ctx.close()


_INS = ["x_prompt", "x_sample", "cache_k", "cache_v", "c", "c_ctx", "w_ada", "b_ada", "norm1_g", "norm2_g", "w_in",
        "w_out", "rpb", "pool_w", "pool_scale", "conv_w", "conv_b", "conv_ln_g", "conv_ln_b", "conv_pw_w",
        "conv_pw_b", "w_router", "b_router", "moe_w_gate", "moe_w_up", "moe_w_down", "final_g"]
_OUTS = [("y_prompt", (1, NCTX, D)), ("y_sample", (1, NLAT, D)), ("new_k", (1, 1, NCTX, H, DH)),
         ("new_v", (1, 1, NCTX, H, DH))]
_SCRATCH = [("h2d", (NTOK, D)), ("yd", (BIG * P, D)), ("modr", (64, P)), ("rpad", (120, 48)), ("rwin", (8, H, 8, 48))]


def kernel(**inputs):
    import numpy as _np
    import concourse.bacc as _bacc
    from concourse.bass_utils import run_bass_kernel_spmd as _run

    nc = _bacc.Bacc("TRN2", target_bir_lowering=False, num_devices=1)
    arrays, t = {}, {}
    for name in _INS + ["consts"]:
        a = shape_constants() if name == "consts" else _np.ascontiguousarray(inputs[name])
        arrays[f"in_{name}"] = a
        t[name] = nc.dram_tensor(f"in_{name}", a.shape, F32, kind="ExternalInput").ap()
    for name, shape in _OUTS:
        t[name] = nc.dram_tensor(f"out_{name}", shape, F32, kind="ExternalOutput").ap()
    for name, shape in _SCRATCH:
        t[name] = nc.dram_tensor(f"scratch_{name}", shape, F32, kind="Internal").ap()
    build(nc, t)
    r = _run(nc, [arrays], core_ids=[0])
    return tuple(r.results[0][f"out_{name}"] for name, _ in _OUTS)
```

```python
from contextlib import ExitStack

import numpy as np

import concourse.bass as bass
from concourse import mybir
from concourse.alu_op_type import AluOpType as ALU

ACT = mybir.ActivationFunctionType
F32 = mybir.dt.float32
U32 = mybir.dt.uint32
I32 = mybir.dt.int32
AX = mybir.AxisListType

P = 128
D = 1024
KD = D // P
NCTX = 128
NLAT = 512
NTOK = NLAT + NCTX
TT = NTOK // P
ROWS, COLS = 8, 64
G, GC = 8, 8
H, DH = 8, 64
DA = H * DH
PAST = 256
WR, WC = 8, 16
NE, NG, EPG = 16, 4, 4
DFF = 512
FC = DFF // P
TAPS = 31
HALO = TAPS // 2
EPS = 1e-6
NEG = -1e30
PADP = 8
LP = NLAT + 2 * PADP + NCTX + 2 * PADP
LC = NLAT + 2 * HALO + NCTX + 2 * HALO
CTXP = NLAT + 2 * PADP
CTXC = NLAT + 2 * HALO
NACC = LC - 2 * HALO
MAXOV = (2 * NTOK - (P + 1)) // P + 1
MAXOV += MAXOV % 2
NT = NE + MAXOV + 2
BIG = NE + MAXOV
RING = 6

CW = [("ident", P), ("tri", P), ("ones", P), ("iota", P), ("iotat", NT), ("tok", TT), ("tie", 16),
      ("edge", 32), ("invw", 2), ("cols2", 2), ("mask", 3 * 256)]
CO, _o = {}, 0
for _n, _w in CW:
    CO[_n] = (_o, _o + _w)
    _o += _w
CWID = _o

VR = [("c_ctx", 8), ("c", 8), ("norm1_g", 8), ("b_ada", 48)]
VR2 = [("norm2_g", 8), ("pool_scale", 2), ("conv_b", 2), ("conv_ln_g", 2), ("conv_ln_b", 2), ("conv_pw_b", 2)]
VO, _o = {}, 0
for _n, _w in VR:
    VO[_n] = (_o, _w)
    _o += _w
NVEC = _o
_o = 2 * TAPS
for _n, _w in VR2:
    VO[_n] = (_o, _w)
    _o += _w
NCW = _o


def shape_constants():
    c = np.zeros((P, CWID), np.float32)

    def put(name, v):
        c[:, CO[name][0]:CO[name][1]] = v

    p = np.arange(P)
    put("ident", np.eye(P))
    put("tri", p[:, None] < p[None, :])
    put("ones", 1.0)
    put("iota", p[None, :])
    put("iotat", np.arange(NT)[None, :])
    put("tok", p[:, None] + P * np.arange(TT)[None, :])
    put("tie", (np.arange(4)[None, :] < np.arange(4)[:, None]).reshape(1, 16))
    e = np.ones((P, 2, 2, 8))
    w_of = np.array([[2, 4], [8, 16]])
    for ch in range(2):
        for half in range(2):
            w = w_of[ch, half]
            for i in range(8):
                e[64 * half:64 * half + 64, ch, 0, i] = w / min(w, i + w // 2)
                e[64 * half:64 * half + 64, ch, 1, i] = w / min(w, 8 - i + w // 2)
    put("edge", e.reshape(P, 32))
    put("invw", 1.0 / w_of.T[p // 64])
    put("cols2", 0.0)
    gq, qc = p // 64, p % 8
    k = np.arange(256)
    gk, kc = k // 64, k % 8
    m = np.zeros((P, 3, 256))
    for v, t in enumerate((0, 1, 3)):
        qcol = (2 * t + gq) * 8 + qc
        kcol = (2 * t - 1 + gk) * 8 + kc
        cs = np.clip(qcol - WC // 2, 0, COLS - WC)
        ok = (kcol[None] >= cs[:, None]) & (kcol[None] < cs[:, None] + WC) & (kcol[None] >= 0) & (kcol[None] < COLS)
        m[:, v] = np.where(ok, 0.0, NEG)
    put("mask", m.reshape(P, 768))
    return c


def fill_plan():
    plan = [(("vec",), "D")]
    plan += [(("xT", i, h), "AD"[h]) for i in range(TT) for h in range(2)]
    for j in (0, 2):
        plan += [(("ada", j), "A"), (("adT", j), "A")]
    plan += [(("cw",), "D")]
    for j in (1, 3):
        plan += [(("ada", j), "A"), (("adT", j), "A")]
    plan += [(("pa", m), "A") for m in range(4)] + [(("pac",), "A"), (("ada", 4), "A")]
    plan += [(("g", m), "A") for m in range(2)] + [(("gc",), "A"), (("adT", 4), "A"), (("ada", 5), "A")]
    plan += [(("q", m), "A") for m in range(4)] + [(("qc",), "A"), (("adT", 5), "A"), (("ada", 6), "A")]
    plan += [(("ck", i), "A") for i in range(2)]
    plan += [(("k", m), "A") for m in range(4)] + [(("kc",), "A"), (("adT", 6), "A"), (("ada", 7), "A")]
    plan += [(("mu",), "D"), (("muc",), "D")]
    plan += [(("v", m), "A") for m in range(2)] + [(("var",), "D"), (("varc",), "D")]
    plan += [(("v", m), "A") for m in range(2, 4)] + [(("vc",), "A"), (("adT", 7), "A"), (("ada", 8), "A")]
    plan += [(("ko",), "A"), (("pl", 0), "A"), (("pl", 1), "A"), (("plc",), "A"), (("adT", 8), "A")]
    for i in range(STEPS):
        if i < PAIRS and i % 2 == 0:
            plan += [(("S", i), "A"), (("S", i + 1), "A")]
        if i in BESIDE:
            plan.append((BESIDE[i], "D" if BESIDE[i][0] in ("Sc", "wo") else "A"))
        if 2 <= i < PAIRS + 2:
            plan.append((("PT", i - 2), "A"))
        if i >= 5 and (i - 5) % 8 == 7:
            plan.append((("aT", (i - 5) // 8), "A"))
    plan += [(("PTc", 0), "A"), (("PTc", 1), "A"), (("wo", 0, 1), "D"), (("wo", 1, 0), "D"), (("aT", 4), "A")]
    for i in range(1, TT + LAG):
        if 1 < i < TT:
            plan.append((("wo", i, 0), "D"))
        if i >= LAG:
            plan += [(("hT", i - LAG, 0), "A"), (("hT", i - LAG, 1), "A")]
        if i < TT:
            plan.append((("wo", i, 1), "D"))
        if i >= LAG:
            plan.append((("lg", i - LAG), "A"))
    plan += [(("rank",), "D"), (("table",), "D")]
    return plan


LAG = 2
PAIRS = 4 * H
STEPS = PAIRS + 6
BESIDE = {1: ("pw", 0), 2: ("pw", 1), 3: ("pwc",), 4: ("ada", 9), 5: ("adT", 9), 7: ("ada", 10), 8: ("adT", 10),
          10: ("ada", 11), 11: ("adT", 11), 18: ("modT",), PAIRS: ("Sc", 0), PAIRS + 1: ("Sc", 1), PAIRS + 4: ("wo", 0, 0)}
PLAN = fill_plan()
NTH = {key: n for n, (key, _) in enumerate(PLAN)}
ASIDE = {("ada", 1): 6, ("adT", 1): 7, ("ada", 3): 6, ("adT", 3): 7}
BANK = {key: ASIDE.get(key, n % RING) for key, n in NTH.items()}
WHO = {key: who for key, who in PLAN}
TURN = {key: sum(1 for k, w in PLAN[:n + 1] if w == who) for n, (key, who) in enumerate(PLAN)}

LAST = {3: ("pac",), 4: ("gc",), 0: ("qc",), 1: ("kc",), 2: ("vc",)}
ORDER = [("ada", 0), ("ada", 2), ("in", 3), ("ada", 1), ("ada", 3), ("in", 4), ("ada", 4), ("ada", 5), ("in", 0),
         ("ada", 6), ("in", 1), ("in", 2), ("ada", 7), ("ada", 8), ("ada", 9), ("ada", 10), ("ada", 11), ("out", 0),
         ("out", 1)]
SLOT = [0, 1, 2, 0, 1, 0, 1, 2, 1, 0, 2, 1, 0, 2, 1, 0, 2, 1, 0]
LOADS = [(key, key if key[0] == "ada" else LAST[key[1]] if key[0] == "in" else ("wo", TT - 1, 1)) for key in ORDER]
LOADNO = {key: n for n, (key, _) in enumerate(LOADS)}
NLOAD = len(LOADS)
BEFORE = [max([p for p in range(n) if SLOT[p] == SLOT[n]], default=None) for n in range(NLOAD)]
EVEN = SLOT[-3:]
EVEN_BASE = [SLOT.count(s) for s in EVEN]


def build(nc, t):
    ctx = ExitStack()

    def sb(name, shape, dt=F32):
        return ctx.enter_context(nc.sbuf_tensor(name, shape, dt))

    def sem(name):
        return ctx.enter_context(nc.semaphore(name))

    bank = [ctx.enter_context(nc.psum_tensor(f"bank{i}", [P, 512], F32)) for i in range(8)]

    slots = sb("slots", [P, 3, 4096])
    x = sb("x", [P, TT, D])
    ra = sb("ra", [P, KD * NTOK])
    rb = sb("rb", [P, 16984])
    rc = sb("rc", [P, KD * NTOK])
    re = sb("re", [P, 5440])
    cst = sb("cst", [P, CWID])
    vecT = sb("vecT", [P, NVEC])
    cwT = sb("cwT", [P, NCW])
    cond = sb("cond", [P, KD, 32])
    adr = sb("adr", [P, P])
    mod = sb("mod", [P, 6, 2, KD])
    poolw = sb("poolw", [P, 2, P])
    pww = sb("pww", [P, 2, 256])
    wr = sb("wr", [P, KD, NE])
    br = sb("br", [P, NE])
    st = sb("st", [P, 3, 32])
    ss = sb("ss", [P, 3, TT])
    ridx = sb("ridx", [P, NT], U32)
    gi = sb("gi", [P, 2], U32)
    slot_u = sb("slot_u", [P, 2, TT], U32)
    wts = sb("wts", [P, 2, TT])
    oi = sb("oi", [P, 16], I32)

    def K(name):
        return cst[:, CO[name][0]:CO[name][1]]

    def V(name):
        return (vecT if name in dict(VR) else cwT)[:, VO[name][0]:VO[name][0] + VO[name][1]]

    ident = K("ident")
    hT = ra[:, :].rearrange("p (k n) -> p k n", k=KD)
    bc = ra[:, 0:4096].rearrange("p (b n) -> p b n", b=4)
    cuts, o = [], 0
    for n in (4 * NTOK, 4 * 640, 4 * PAST, 4 * NCTX, 4 * 520, 520, 2 * 520, 512, H * 256, 1024, 2048, 1024):
        cuts.append(rb[:, o:o + n])
        o += n
    assert o <= 16984
    qT, kT, kcT, kpT = (v.rearrange("p (m n) -> p m n", m=4) for v in cuts[0:4])
    vl = cuts[4].rearrange("p (j h e) -> p j h e", j=4, h=H)
    vp = cuts[5].rearrange("p (h e) -> p h e", h=H)
    vc = cuts[6].rearrange("p (j h e) -> p j h e", j=2, h=H)
    at = cuts[7]
    raw = cuts[8].rearrange("p (h r w) -> p h r w", h=H, r=8)
    bm = cuts[9].rearrange("p (b n) -> p b n", b=4)
    pr = cuts[10].rearrange("p (b n) -> p b n", b=4)
    pts = cuts[11].rearrange("p (b n) -> p b n", b=2)
    hT0 = cuts[9].rearrange("p (k n) -> p k n", k=KD)
    ckr = cuts[10][:, 0:1024].rearrange("p (j n) -> p j n", j=2)
    odd = rb[:, 0:12288].rearrange("p (q n) -> p q n", q=3)
    bc2 = rb[:, 12288:14336].rearrange("p (b n) -> p b n", b=2)
    h2 = rb[:, 14336:16384].rearrange("p (b n) -> p b n", b=2)
    rowhot = rb[:, 12288:12288 + 10 * P].rearrange("p (b n) -> p b n", b=10)
    tilehot = rb[:, 13568:13568 + 10 * NT].rearrange("p (b n) -> p b n", b=10)
    before = rb[:, 13568 + 10 * NT:13568 + 10 * NT + (TT + 1) * NE]
    up, s1, s2 = (rc[:, i * 2 * LP:(i + 1) * 2 * LP].rearrange("p (m n) -> p m n", m=2) for i in range(3))
    mT = rc[:, :].rearrange("p (k n) -> p k n", k=KD)
    xn = re[:, 0:2048].rearrange("p (b n) -> p b n", b=2)
    junk = re[:, 2048:3072]
    junk2 = ra[:, 4096:5120]
    e0, e1, e2, e3 = 2 * LC, 2 * LC + 2 * NTOK, 2 * LC + 2 * NTOK + 2 * NACC, 2 * LC + 4 * NTOK + 2 * NACC
    yc = re[:, 0:e0].rearrange("p (m n) -> p m n", m=2)
    sg = re[:, e0:e1].rearrange("p (m n) -> p m n", m=2)
    acc = re[:, e1:e2].rearrange("p (m n) -> p m n", m=2)
    df = re[:, e2:e3].rearrange("p (m n) -> p m n", m=2)
    rs = re[:, 0:NTOK]
    mrow = re[0:64, 5312:5440]
    vrow, cwrow, rprow = re[:, 5000:5128], re[:, 5128:5256], re[:, 5256:5304]
    h2T = re[:, 0:5120].rearrange("p (k n) -> p k n", k=KD)
    xg = rc[:, 0:2048].rearrange("p (b n) -> p b n", b=2)
    xt = rc[:, 2048:4096].rearrange("p (b k n) -> p b k n", b=2, k=KD)
    hid = rc[:, 4096:5120].rearrange("p (b f n) -> p b f n", b=2, f=FC)
    yo = re[:, 0:2048].rearrange("p (b n) -> p b n", b=2)
    gs = re[:, 2048:2560].rearrange("p (b n) -> p b n", b=2)
    wset = [[slots[:, s, :] for s in EVEN], [odd[:, q, :] for q in range(3)]]
    fy = slots[:, :, :].rearrange("p a b -> p (a b)")[:, 0:2 * TT * D].rearrange("p (c k n) -> p c k n", c=TT, k=2)
    pa_, pb_ = ra[:, 4096:4416], ra[:, 4416:4736]
    rw = re[:, 5120:5440]

    S = {n: sem(n) for n in """cst_in vec_in cw_in small_in poolw_in cachek_in cachev_in rpb_in rpad_out rwin_out raw_in bc_in bc2_in
        psum_full evac_a evac_d cond_zero cond_ready ssq_ready ms_ready sqrt_ready xn_ready mod_ready h_ready h0_ready
        pads_ready rpad_ready ones_ready tap_done df_ready sq_ready sd_ready yn_ready
        act_ready bm_ready smax_done pv_done o_free expc_done mrow_out kcache_out vcache_out
        ssq2_ready ms2_ready sqrt2_ready hn_ready h2_ready h2_last aff_ready off_ready tiles_hot rows_hot route_ready ridx_ready oi_ready
        xt_full xt_evac_a xt_evac_d gu_full silu_done hid_done y_full y_evac_a y_evac_d bcend_in
        first_ready x2_ready ssq3_ready ms3_ready sqrt3_ready rms3_ready xn3_ready out_ready last_ready out_done
        zeros_ready zeros_out moe_stored over_stored gi_seen xg_seen gi_ready dve_chain pool_chain act_chain""".split()}
    w_slot = [sem(f"w_slot{i}") for i in range(3)]
    w_odd = [sem(f"w_odd{i}") for i in range(3)]
    x_in = [sem(f"x_in{i}") for i in range(TT)]
    h2_out = [sem(f"h2_out{i}") for i in range(2)]
    xg_in = [sem(f"xg_in{i}") for i in range(2)]
    y_out = [sem(f"y_out{i}") for i in range(2)]
    fy_in = [sem(f"fy_in{i}") for i in range(TT)]

    def chained(eng, name):
        n = [0]

        def link(ins):
            n[0] += 1
            ins.then_inc(S[name], 1)
            eng.wait_ge(S[name], n[0])
        return link

    def filled(eng, *key):
        eng.wait_ge(S["psum_full"], NTH[key] + 1)
        return bank[BANK[key]]

    def emptied(eng, *key):
        eng.wait_ge(S["evac_a" if WHO[key] == "A" else "evac_d"], TURN[key])

    def group(ap):
        return ap.rearrange("p (r g c) -> p g r c", r=ROWS, g=G)

    def ungroup(ap):
        return ap.rearrange("p (g r c) -> p g r c", r=ROWS, g=G)

    def ge(eng, s, n):
        if not (isinstance(n, int) and n <= 0):
            eng.wait_ge(S[s] if isinstance(s, str) else s, n)

    def over_tiles(eng, body, over_body=None):
        for b in range(2):
            body(0, b)
        with eng.Fori(1, NE // 2) as i:
            for b in range(2):
                body(i, b)
        eng.wait_ge(S["oi_ready"], 1)
        more = eng.value_load(oi[0:1, 0:1], min_val=0, max_val=MAXOV)
        for b in range(2):
            with eng.If(more > b):
                (over_body or body)(NE // 2, b)
        with eng.If(more > 2):
            with eng.Fori(NE // 2 + 1, NE // 2 + MAXOV // 2) as i:
                for b in range(2):
                    with eng.If(more > i * 2 + (b - NE)):
                        (over_body or body)(i, b)
                eng.nop()

    def tile_sums():
        misc, pf = ra[:, 4736 + 4 * TT * NE:4736 + 4 * TT * NE + 64], ra[:, 4096:4160].rearrange("p (b n) -> p b n", b=2)
        return pf[:, 0, 16:32], misc[:, 32:48], pf

    block = ctx.enter_context(nc.Block())

    @block.sync
    def _(sp):
        sp.dma_start(cst[:, :], t["consts"]).then_inc(S["cst_in"], 16)
        for n, (key, _) in enumerate(LOADS):
            for i in range(TT) if n == 0 else ():
                if i < 4:
                    for g in range(2):
                        sp.dma_start(x[64 * g:64 * g + 64, i, :],
                                     t["x_sample"][0].rearrange("(r g c) d -> g r c d", r=ROWS, g=G)[2 * i + g]).then_inc(x_in[i], 16)
                else:
                    sp.dma_start(x[:, 4, :], t["x_prompt"][0]).then_inc(x_in[4], 16)
            if n == 6:
                sp.dma_start(pww[:, :, :], t["conv_pw_w"][0].rearrange("(k p) n -> p k n", p=P)).then_inc(S["small_in"], 16)
                sp.dma_start(wr[:, :, :], t["w_router"].rearrange("(k p) n -> p k n", p=P)).then_inc(S["small_in"], 16)
                sp.dma_start(br[:, :], t["b_router"].rearrange("(a n) -> a n", a=1).to_broadcast([P, NE])).then_inc(S["small_in"], 16)
            if n == 7:
                sp.dma_start(ckr[:, :, :], t["cache_k"][0, 0].rearrange("(j p) h e -> p j (h e)", p=P)).then_inc(S["cachek_in"], 16)
                for j in range(2):
                    sp.dma_start(vc[:, j, :, 0:DH], t["cache_v"][0, 0, j * P:(j + 1) * P]).then_inc(S["cachev_in"], 16)
            if BEFORE[n] is not None:
                sp.wait_ge(S["psum_full"], NTH[LOADS[BEFORE[n]][1]] + 1)
            kind, j = key
            if kind == "ada":
                src = t["w_ada"][0].rearrange("(k p) n -> p k n", p=P)[:, :, 512 * j:512 * j + 512]
            elif kind == "in":
                src = t["w_in"][0].rearrange("(k p) n -> p k n", p=P)[:, :, 512 * j:min(512 * j + 512, 2304)]
            else:
                src = t["w_out"][0].rearrange("(k p) n -> p k n", p=P)[:, 4 * j:4 * j + 4, :]
            if n == 9:
                sp.wait_ge(S["zeros_ready"], 1)
                for q in range(NE, BIG):
                    sp.dma_start(t["yd"][q * P:(q + 1) * P, :], cuts[11]).then_inc(S["zeros_out"], 16)
            k, w = src.shape[1], src.shape[2]
            sp.dma_start(slots[:, SLOT[n], 0:k * w].rearrange("p (k n) -> p k n", k=k), src).then_inc(w_slot[SLOT[n]], 16)

        def expert(q, e):
            if q < 2:
                return t["moe_w_gate" if q == 0 else "moe_w_up"][0, e].rearrange("(p k) n -> p (k n)", k=KD)
            return t["moe_w_down"][0, e].rearrange("(p k) n -> p (k n)", k=FC)

        def load(b, q, e):
            s = w_odd[q] if b else w_slot[EVEN[q]]
            sp.dma_start(wset[b][q], expert(q, e)).then_inc(s, 16)

        for q in range(3):
            sp.wait_ge(S["psum_full"], NTH[LOADS[NLOAD - 3 + q][1]] + 1)
            load(0, q, 0)
            if q == 0:
                emptied(sp, "aT", 4)
                for r in range(3):
                    load(1, r, 1)

        def store(b, tile):
            sp.wait_ge(S["y_evac_a"], tile + 1)
            sp.wait_ge(S["y_evac_d"], tile + 1)
            sp.dma_start(t["yd"][bass.ds(tile * P, P), :], yo[:, b, :]).then_inc(y_out[b], 16)

        with sp.Fori(0, NE // 2 - 1) as i:
            for b in range(2):
                tile = i * 2 + b
                sp.wait_ge(S["gu_full"], tile * 2 + 2)
                load(b, 0, tile + 2)
                load(b, 1, tile + 2)
                sp.wait_ge(S["y_full"], tile * 2 + 2)
                load(b, 2, tile + 2)
                store(b, tile)
        sp.wait_ge(S["oi_ready"], 1)
        more = sp.value_load(oi[0:1, 0:1], min_val=0, max_val=MAXOV)

        def load_more(b, tile, n):
            at_n = slice(n + 1, n + 2) if isinstance(n, int) else bass.ds(n + 1, 1)
            e = sp.value_load(oi[0:1, at_n], min_val=0, max_val=NE - 1)
            sp.wait_ge(S["gu_full"], tile * 2 + 2)
            load(b, 0, e)
            load(b, 1, e)
            sp.wait_ge(S["y_full"], tile * 2 + 2)
            load(b, 2, e)

        for b in range(2):
            with sp.If(more > b):
                load_more(b, NE - 2 + b, b)
            store(b, NE - 2 + b)

        def over_pair(i):
            for b in range(2):
                with sp.If(more > i * 2 + (2 + b)):
                    load_more(b, i * 2 + (NE + b), i * 2 + (2 + b))
                with sp.If(more > i * 2 + b):
                    store(b, i * 2 + (NE + b))
                    sp.wait_ge(y_out[b], i * 16 + 16 * (NE // 2 + 1))
                    sp.sem_inc(S["over_stored"], 1)

        over_pair(0)
        with sp.If(more > 2):
            with sp.Fori(1, MAXOV // 2) as i:
                over_pair(i)
                sp.nop()
        for b in range(2):
            sp.wait_ge(y_out[b], 16 * (NE // 2))
        sp.sem_inc(S["moe_stored"], 1)

        for c in range(TT):
            if c < TT - 1:
                sp.wait_ge(S["out_ready"], c + 1)
            else:
                sp.wait_ge(S["last_ready"], 1)
            if c < 4:
                for g in range(2):
                    sp.dma_start(t["y_sample"][0].rearrange("(r g c) d -> g r c d", r=ROWS, g=G)[2 * c + g],
                                 fy[64 * g:64 * g + 64, c, 1, :]).then_inc(S["out_done"], 16)
            else:
                sp.dma_start(t["y_prompt"][0], fy[:, c, 1, :]).then_inc(S["out_done"], 16)
        sp.wait_ge(S["out_done"], 16 * 9)

    @block.scalar
    def _(act):
        link = chained(act, "act_chain")
        sc = nc.scalar

        def evac(out, in_, func=ACT.Copy, last=True, **kw):
            ins = sc.activation(out, in_, func, **kw)
            if last:
                ins.then_inc(S["evac_a"], 1)

        o = 0
        for name, rows in VR:
            src = t[name]
            if len(src.shape) == 2:
                src = src[0]
            act.dma_start(vrow[o:o + rows, :], src.rearrange("(a p) -> a p", p=P)).then_inc(S["vec_in"], 16)
            o += rows

        emptied(act, "vec")
        act.wait_ge(S["cond_zero"], 1)
        sc.activation(cond[:, :, 0], V("c_ctx"), ACT.Silu)
        sc.activation(cond[:, :, 1], V("c"), ACT.Silu).then_inc(S["cond_ready"], 1)

        def ada(j):
            if j:
                filled(act, "adT", {2: 0, 1: 2, 3: 1}.get(j, j - 1))
            b = filled(act, "ada", j)
            evac(adr[:, :], b[:, 0:P])

        def adT(j):
            b = filled(act, "adT", j)
            evac(mod[:, j // 2, :, 4 * (j % 2):4 * (j % 2) + 4],
                 b[:, 0:P].rearrange("p (q s) -> p s q", q=4)[:, 0:2, :])

        for i in range(TT):
            act.wait_ge(x_in[i], 32 if i < 4 else 16)
            ins = sc.activation(junk, x[:, i, :], ACT.Square, accum_out=ss[:, 0, i:i + 1])
            if i < TT - 1:
                link(ins)
        ins.then_inc(S["ssq_ready"], 1)
        act.wait_ge(S["ms_ready"], 1)
        sc.activation(ss[:, 1, :], ss[:, 0, :], ACT.Sqrt).then_inc(S["sqrt_ready"], 1)
        for i in range(TT):
            b = filled(act, "xT", i, 0)
            evac(hT[:, 0:4, i * P:(i + 1) * P], b[:, :].rearrange("p (k n) -> p k n", k=4))

        for j in (0, 2, 1, 3):
            ada(j)
            adT(j)
        act.wait_ge(S["pads_ready"], 2)
        for m in range(4):
            b = filled(act, "pa", m)
            dst = up[:, m, PADP:PADP + NLAT] if m < 2 else yc[:, m - 2, HALO:HALO + NLAT]
            evac(group(dst), ungroup(b[:, :]))
        b = filled(act, "pac")
        four = b[:, :].rearrange("p (m n) -> p m n", m=4)
        evac(up[:, :, CTXP + PADP:CTXP + PADP + NCTX], four[:, 0:2], last=False)
        evac(yc[:, :, CTXC + HALO:CTXC + HALO + NCTX], four[:, 2:4])
        ada(4)
        for m in range(2):
            b = filled(act, "g", m)
            evac(group(sg[:, m, 0:NLAT]), ungroup(b[:, :]), ACT.Sigmoid)
        b = filled(act, "gc")
        evac(sg[:, :, NLAT:NTOK], b[:, 0:256].rearrange("p (m n) -> p m n", m=2), ACT.Sigmoid)
        adT(4)
        ada(5)
        for m in range(4):
            b = filled(act, "q", m)
            evac(qT[:, m, 0:NLAT], b[:, :], scale=DH ** -0.5)
        b = filled(act, "qc")
        evac(qT[:, :, NLAT:NTOK], b[:, :].rearrange("p (m n) -> p m n", m=4), scale=DH ** -0.5)
        adT(5)
        ada(6)
        for i in range(2):
            b = filled(act, "ck", i)
            evac(kcT[:, :, i * P:(i + 1) * P], b[:, :].rearrange("p (m n) -> p m n", m=4))
        for m in range(4):
            b = filled(act, "k", m)
            evac(kT[:, m, 64:NLAT], b[:, 0:NLAT - 64], last=False)
            evac(kT[:, m, 0:64], b[:, NLAT - 64:NLAT], last=False)
            evac(kT[:, m, NLAT:NLAT + 64], b[:, NLAT - 64:NLAT], last=False)
            evac(kT[:, m, NLAT + 64:NLAT + 128], b[:, 0:64])
        b = filled(act, "kc")
        evac(kpT[:, :, :], b[:, :].rearrange("p (m n) -> p m n", m=4))
        adT(6)
        ada(7)
        act.wait_ge(S["ones_ready"], 1)

        def swish():
            act.wait_ge(S["yn_ready"], 1)
            for m in range(2):
                for dst, src in ((sg[:, m, 0:NLAT], acc[:, m, 0:NLAT]),
                                 (sg[:, m, NLAT:NTOK], acc[:, m, CTXC:CTXC + NCTX])):
                    ins = sc.activation(dst, src, ACT.Silu, scale=V("conv_ln_g")[:, m:m + 1], bias=V("conv_ln_b")[:, m:m + 1])
            ins.then_inc(S["act_ready"], 1)

        emptied(act, "muc")
        sc.activation(sg[:, :, 0:NLAT], acc[:, :, 0:NLAT], ACT.Square)
        sc.activation(sg[:, :, NLAT:NTOK], acc[:, :, CTXC:CTXC + NCTX], ACT.Square).then_inc(S["sq_ready"], 1)
        for j in range(4):
            b = filled(act, "v", j)
            evac(vl[:, j, :, 0:DH], b[:, :].rearrange("p (h e) -> p h e", h=H))
            if j == 2:
                emptied(act, "varc")
                sc.activation(rs, rs, ACT.Sqrt).then_inc(S["sd_ready"], 1)
        swish()
        b = filled(act, "vc")
        evac(vp[:, :, 0:DH], b[:, :].rearrange("p (h e) -> p h e", h=H))
        adT(7)
        ada(8)
        b = filled(act, "ko")
        evac(at, b[:, :])
        for m in range(2):
            b = filled(act, "pl", m)
            evac(ungroup(mT[:, 4 + m, 0:NLAT]), group(b[:, :]), ACT.Identity, scale=V("pool_scale")[:, m:m + 1])
        b = filled(act, "plc")
        for m in range(2):
            evac(mT[:, 4 + m, NLAT:NTOK], b[:, m * P:(m + 1) * P], ACT.Identity, last=m == 1,
                 scale=V("pool_scale")[:, m:m + 1])
        adT(8)

        def pw(m):
            b = filled(act, "pw", m)
            evac(ungroup(mT[:, 6 + m, 0:NLAT]), group(b[:, :]), ACT.Identity, bias=V("conv_pw_b")[:, m:m + 1])

        def pwc():
            b = filled(act, "pwc")
            for m in range(2):
                evac(mT[:, 6 + m, NLAT:NTOK], b[:, m * P:(m + 1) * P], ACT.Identity, last=m == 1,
                     bias=V("conv_pw_b")[:, m:m + 1])

        def modT():
            b = filled(act, "modT")
            evac(mrow, b[0:64, 0:P])

        beside = {"pw": pw, "pwc": pwc, "ada": ada, "adT": adT, "modT": modT}

        def aT(i):
            b = filled(act, "aT", i)
            evac(mT[:, 0:4, i * P:(i + 1) * P], b[:, :].rearrange("p (m n) -> p m n", m=4))

        act.wait_ge(S["zeros_out"], 16 * MAXOV)
        for i in range(STEPS):
            for u in (i, i + 1) if i < PAIRS and i % 2 == 0 else ():
                act.wait_ge(S["smax_done"], u + 1)
                b = filled(act, "S", u)
                nmx = st[:, 2, u:u + 1]
                sc.activation(pr[:, u % 4, 0:256], pr[:, u % 4, 0:256], ACT.Exp, bias=nmx)
                evac(pr[:, u % 4, 256:512], b[:, 256:512], ACT.Exp, bias=nmx)
            if i in BESIDE and BESIDE[i][0] in beside:
                beside[BESIDE[i][0]](*BESIDE[i][1:])
            if 2 <= i < PAIRS + 2:
                s = i - 2
                if s >= 2:
                    act.wait_ge(S["pv_done"], s - 1)
                b = filled(act, "PT", s)
                evac(pts[:, s % 2, :], b[:, :])
            if i > PAIRS and BESIDE.get(i - 1, "-")[0] == "Sc":
                j = BESIDE[i - 1][1]
                emptied(act, "Sc", j)
                sc.activation(pr[:, j, :], pr[:, j, :], ACT.Exp).then_inc(S["expc_done"], 1)
            if i >= 5 and (i - 5) % 8 == 7:
                aT((i - 5) // 8)
        for j in range(2):
            act.wait_ge(S["pv_done"], PAIRS - 1 + j)
            b = filled(act, "PTc", j)
            evac(pts[:, j, :], b[:, :])

        def rms2(i):
            emptied(act, "wo", i, 1)
            if i >= 1:
                act.wait_ge(S["ssq2_ready"], i)
            sc.activation(junk2, x[:, i, :], ACT.Square, accum_out=ss[:, 0, i:i + 1]).then_inc(S["ssq2_ready"], 1)
            act.wait_ge(S["ms2_ready"], i + 1)
            sc.activation(ss[:, 1, i:i + 1], ss[:, 0, i:i + 1], ACT.Sqrt).then_inc(S["sqrt2_ready"], 1)

        def h2_out_of_psum(i):
            for hf in range(2):
                b = filled(act, "hT", i, hf)
                evac(h2T[:, 4 * hf:4 * hf + 4, i * P:(i + 1) * P], b[:, :].rearrange("p (k n) -> p k n", k=4))

        rms2(0)
        aT(4)
        for i in range(1, TT + LAG):
            if i >= LAG:
                h2_out_of_psum(i - LAG)
            if i < TT:
                rms2(i)
            if i >= LAG:
                c = i - LAG
                if c == TT - LAG:
                    emptied(act, "lg", c - 1)
                    sc.activation(rw[:, 0:c * NE], rw[:, 0:c * NE], ACT.Sigmoid).then_inc(S["aff_ready"], 1)
                b = filled(act, "lg", c)
                evac(rw[:, c * NE:(c + 1) * NE], b[:, 0:NE], ACT.Copy if c < TT - LAG else ACT.Sigmoid)

        def xt_out(i, b):
            act.wait_ge(S["xt_full"], i * 4 + (2 * b + 1))
            ge(act, "gu_full", i * 4 + (2 * b - 2))
            sc.activation(xt[:, b, 0:4, :], bank[0][:, :].rearrange("p (k n) -> p k n", k=4),
                          ACT.Copy).then_inc(S["xt_evac_a"], 1)

        def tiles(i, b):
            for hf in range(2):
                act.wait_ge(S["gu_full"], i * 4 + (2 * b + hf + 1))
                ge(act, "hid_done", i * 4 + (2 * b + hf - 1))
                sc.activation(gs[:, hf, :], bank[2 + hf][:, 0:256], ACT.Silu).then_inc(S["silu_done"], 1)
            xt_out(i + b, 1 - b)
            act.wait_ge(S["y_full"], i * 4 + (2 * b + 1))
            ge(act, y_out[b], i * 16)
            sc.activation(yo[:, b, 0:512], bank[4 + 2 * b][:, :], ACT.Copy).then_inc(S["y_evac_a"], 1)

        xt_out(0, 0)
        over_tiles(act, tiles)

        def gate(c):
            act.wait_ge(fy_in[c], 32)
            sc.activation(fy[:, c, 0, :], fy[:, c, 0, :], ACT.Copy, scale=wts[:, 0, c:c + 1]).then_inc(S["first_ready"], 1)

        gate(0)
        gate(1)
        for d in range(TT):
            act.wait_ge(S["x2_ready"], d + 1)
            sc.activation(fy[:, d, 1, :], x[:, d, :], ACT.Square, accum_out=ss[:, 0, d:d + 1]).then_inc(S["ssq3_ready"], 1)
            if d + 2 < TT:
                gate(d + 2)
            act.wait_ge(S["ms3_ready"], d + 1)
            sc.activation(ss[:, 1, d:d + 1], ss[:, 0, d:d + 1], ACT.Sqrt).then_inc(S["sqrt3_ready"], 1)
            if d < TT - 1:
                act.wait_ge(S["rms3_ready"], d + 1)
                sc.activation(fy[:, d, 1, :], x[:, d, :], ACT.Copy, scale=ss[:, 2, d:d + 1]).then_inc(S["xn3_ready"], 1)

    @block.vector
    def _(dve):
        link = chained(dve, "dve_chain")
        v = nc.vector

        def evac(out, in_):
            v.tensor_copy(out, in_).then_inc(S["evac_d"], 1)

        b = filled(dve, "vec")
        evac(vecT[:, :], b[:, 0:NVEC])
        dve.wait_ge(S["ssq_ready"], 1)
        v.tensor_scalar(ss[:, 0, :], ss[:, 0, :], 1.0 / D, EPS, ALU.mult, ALU.add).then_inc(S["ms_ready"], 1)
        dve.wait_ge(S["sqrt_ready"], 1)
        link(v.reciprocal(ss[:, 2, :], ss[:, 1, :]))
        for i in range(TT):
            if i >= 2:
                filled(dve, "xT", i - 2, 1)
            v.tensor_scalar(xn[:, i % 2, :], x[:, i, :], ss[:, 2, i:i + 1], None, ALU.mult).then_inc(S["xn_ready"], 1)
            if i >= 1:
                b = filled(dve, "xT", i - 1, 1)
                evac(hT[:, 4:8, (i - 1) * P:i * P], b[:, :].rearrange("p (k n) -> p k n", k=4))
        b = filled(dve, "xT", TT - 1, 1)
        evac(hT[:, 4:8, (TT - 1) * P:TT * P], b[:, :].rearrange("p (k n) -> p k n", k=4))
        b = filled(dve, "cw")
        evac(cwT[:, :], b[:, 0:NCW])
        emptied(dve, "xT", TT - 1, 0)
        emptied(dve, "xT", TT - 1, 1)
        for k in range(KD):
            if k % 4 == 0:
                dve.wait_ge(S["mod_ready"], k // 2 + 2)
            for s, (a, n) in ((1, (0, NLAT)), (0, (NLAT, NTOK))):
                ins = v.tensor_scalar(hT[:, k, a:n], hT[:, k, a:n], mod[:, 1, s, k:k + 1], mod[:, 0, s, k:k + 1],
                                      ALU.mult, ALU.add)
            ins.then_inc(S["h_ready"], 1)
        emptied(dve, "cw")
        emptied(dve, "gc")
        link(v.tensor_tensor(yc[:, :, HALO:HALO + NLAT], yc[:, :, HALO:HALO + NLAT], sg[:, :, 0:NLAT], ALU.mult))
        link(v.tensor_tensor(yc[:, :, CTXC + HALO:CTXC + HALO + NCTX], yc[:, :, CTXC + HALO:CTXC + HALO + NCTX],
                             sg[:, :, NLAT:NTOK], ALU.mult))
        for m in range(2):
            v.tensor_scalar(acc[:, m, :], yc[:, m, 0:NACC], cwT[:, m:m + 1], V("conv_b")[:, m:m + 1],
                            ALU.mult, ALU.add).then_inc(S["tap_done"], 1)
        with dve.Fori(1, TAPS) as k:
            for m in range(2):
                dve.wait_ge(S["tap_done"], k * 2 + (m - 1))
                v.scalar_tensor_tensor(acc[:, m, :], yc[:, m, bass.ds(k, NACC)], cwT[:, bass.ds(k * 2 + m, 1)],
                                       acc[:, m, :], ALU.mult, ALU.add).then_inc(S["tap_done"], 1)
        dve.wait_ge(S["tap_done"], 2 * TAPS)
        for key, a, w in (("mu", 0, NLAT), ("muc", CTXC, NCTX)):
            b = filled(dve, key)
            for m in range(2):
                ins = v.scalar_tensor_tensor(acc[:, m, a:a + w], b[:, 0:w], -1.0 / 256, acc[:, m, a:a + w], ALU.mult, ALU.add)
            ins.then_inc(S["evac_d"], 1)
        for key, a, w in (("var", 0, NLAT), ("varc", NLAT, NCTX)):
            b = filled(dve, key)
            v.tensor_scalar(rs[:, a:a + w], b[:, 0:w], 1.0 / 256, EPS, ALU.mult, ALU.add).then_inc(S["evac_d"], 1)
        dve.wait_ge(S["sd_ready"], 1)
        link(v.reciprocal(rs, rs))
        for m in range(2):
            v.tensor_tensor(acc[:, m, 0:NLAT], acc[:, m, 0:NLAT], rs[:, 0:NLAT], ALU.mult)
            ins = v.tensor_tensor(acc[:, m, CTXC:CTXC + NCTX], acc[:, m, CTXC:CTXC + NCTX], rs[:, NLAT:NTOK], ALU.mult)
        ins.then_inc(S["yn_ready"], 1)

        def norm(u):
            dve.wait_ge(S["pv_done"], 4 * u + 4 if u < 8 else PAIRS + 4 * (u - 7))
            ob = bank[6 + u % 2][:, 0:260].rearrange("p (h e) -> p h e", h=4)
            link(v.reciprocal(rw[:, 4 * u:4 * u + 4], ob[:, :, DH]))
            if u % 2 == 0 and u >= 2:
                filled(dve, "aT", u // 2 - 1)
            if u == 0:
                dve.wait_ge(S["kcache_out"], 16)
            if u < 8:
                dst = at[:, (u % 2) * 256:(u % 2) * 256 + 256].rearrange("p (h e) -> p h e", h=4)
            else:
                dst = at.rearrange("p (q j e) -> p j q e", q=4, j=2)[:, u - 8]
            v.tensor_tensor(dst, ob[:, :, 0:DH],
                            rw[:, 4 * u:4 * u + 4].unsqueeze(2).to_broadcast([P, 4, DH]), ALU.mult).then_inc(S["o_free"], 1)

        def prompt_scores(j):
            b = filled(dve, "Sc", j)
            four = b[:, :].rearrange("p (h n) -> p h n", h=4)
            link(v.tensor_reduce(st[:, 0, 4 * j:4 * j + 4], four, AX.X, ALU.max))
            filled(dve, "PT", PAIRS - 4 + j)
            v.tensor_tensor(pr[:, j, :].rearrange("p (h n) -> p h n", h=4), four,
                            st[:, 0, 4 * j:4 * j + 4].unsqueeze(2).to_broadcast([P, 4, P]),
                            ALU.subtract).then_inc(S["evac_d"], 1)

        def add_mixed(i, hf):
            if (i, hf) == (0, 0):
                dve.wait_ge(S["bc_in"], 16 * 4)
            b = filled(dve, "wo", i, hf)
            cols = slice(512 * hf, 512 * hf + 512)
            link(v.tensor_tensor(b[:, :], b[:, :], bc[:, 0 if i < 4 else 1, cols], ALU.mult))
            v.tensor_tensor(x[:, i, cols], x[:, i, cols], b[:, :], ALU.add).then_inc(S["evac_d"], 1)

        beside = {"Sc": prompt_scores, "wo": add_mixed}
        for i in range(STEPS):
            if i < PAIRS:
                b = filled(dve, "S", i)
                link(v.tensor_reduce(st[:, 0, i:i + 1], b[:, 256:512], AX.X, ALU.max))
                dve.wait_ge(S["bm_ready"], i + 1)
                if i >= 4:
                    filled(dve, "PT", i - 4)
                link(v.tensor_tensor_reduce(pr[:, i % 4, 0:256], b[:, 0:256], bm[:, i % 4, :], 1.0, st[:, 0, i:i + 1],
                                            ALU.add, ALU.max, st[:, 1, i:i + 1]))
                v.tensor_scalar(st[:, 2, i:i + 1], st[:, 1, i:i + 1], -1.0, None, ALU.mult).then_inc(S["smax_done"], 1)
            if i in BESIDE and BESIDE[i][0] in beside:
                beside[BESIDE[i][0]](*BESIDE[i][1:])
            if i >= 4 and (i - 4) % 4 == 3:
                norm((i - 4) // 4)

        for i in range(TT):
            if i:
                add_mixed(i, 0)
            add_mixed(i, 1)
            if i == 0:
                norm(8)
                norm(9)
            dve.wait_ge(S["ssq2_ready"], i + 1)
            v.tensor_scalar(ss[:, 0, i:i + 1], ss[:, 0, i:i + 1], 1.0 / D, EPS, ALU.mult, ALU.add).then_inc(S["ms2_ready"], 1)
            dve.wait_ge(S["sqrt2_ready"], i + 1)
            link(v.reciprocal(ss[:, 2, i:i + 1], ss[:, 1, i:i + 1]))
            if i == 0:
                filled(dve, "aT", 4)
            if i == 4:
                dve.wait_ge(S["bc2_in"], 16 * 2)
            if i >= 2:
                dve.wait_ge(h2_out[i % 2], 16 * (i // 2))
                filled(dve, "hT", i - 2, 1)
            ins = v.scalar_tensor_tensor(h2[:, i % 2, :], x[:, i, :], ss[:, 2, i:i + 1],
                                         bc[:, 2, :] if i < 4 else bc2[:, 0, :], ALU.mult, ALU.mult)
            if i < TT - 1:
                ins.then_inc(S["hn_ready"], 1)
            else:
                link(ins)
                v.tensor_tensor(h2[:, i % 2, :], h2[:, i % 2, :], bc2[:, 1, :], ALU.add).then_inc(S["h2_last"], 1)

        dve.wait_ge(S["small_in"], 16 * 3)
        n = TT * NE
        aff = rw[:, 0:n]
        W = ra[:, 4736:5120]
        sel, cnt, hot = W[:, 0:n], W[:, n:2 * n], rw[:, n:3 * n].rearrange("p (k n) -> p k n", k=2)
        sel2, tmp = W[:, 2 * n:3 * n], W[:, 3 * n:4 * n]
        misc = W[:, 4 * n:4 * n + 64]
        gsc, gcnt, ing = misc[:, 0:20], misc[:, 20:40], misc[:, 40:60]

        def three(ap):
            return ap.rearrange("p (i e) -> p i e", i=TT)

        def beats(values, groups, out):
            w = 16 * groups
            mine = values.rearrange("p (g e) -> p g e", g=groups).unsqueeze(3).to_broadcast([P, groups, 4, 4])
            other = values.rearrange("p (g e) -> p g e", g=groups).unsqueeze(2).to_broadcast([P, groups, 4, 4])
            more, same = (z[:, 0:w].rearrange("p (g e f) -> p g e f", g=groups, e=4) for z in (pa_, pb_))
            link(v.tensor_tensor(more, other, mine, ALU.is_gt))
            link(v.tensor_tensor(same, other, mine, ALU.is_equal))
            tie = K("tie").unsqueeze(1).to_broadcast([P, groups, 16])
            sf, mf = (z[:, 0:w].rearrange("p (g f) -> p g f", g=groups) for z in (pb_, pa_))
            link(v.tensor_tensor(sf, sf, tie, ALU.mult))
            link(v.tensor_tensor(mf, mf, sf, ALU.add))
            link(v.tensor_reduce(out, pa_[:, 0:w].rearrange("p (g f) -> p g f", f=4), AX.X, ALU.add))

        early = (TT - 1) * NE
        dve.wait_ge(S["aff_ready"], 1)
        emptied(dve, "lg", TT - 2)
        link(v.tensor_tensor(sel[:, 0:early].rearrange("p (i e) -> p i e", i=TT - 1),
                             aff[:, 0:early].rearrange("p (i e) -> p i e", i=TT - 1),
                             br[:, :].unsqueeze(1).to_broadcast([P, TT - 1, NE]), ALU.add))
        beats(sel[:, 0:early], (TT - 1) * NG, cnt[:, 0:early])
        emptied(dve, "lg", TT - 1)
        link(v.tensor_tensor(sel[:, early:n], aff[:, early:n], br[:, :], ALU.add))
        beats(sel[:, early:n], NG, cnt[:, early:n])
        link(v.scalar_tensor_tensor(tmp, cnt, 2.0, sel, ALU.is_lt, ALU.mult))
        link(v.tensor_reduce(gsc, tmp.rearrange("p (g e) -> p g e", e=EPG), AX.X, ALU.add))
        beats(gsc, TT, gcnt)
        link(v.tensor_scalar(ing, gcnt, 0.0, None, ALU.is_equal))
        in_g = ing.unsqueeze(2).to_broadcast([P, TT * NG, EPG])
        for k in range(2):
            link(v.scalar_tensor_tensor(hot[:, k].rearrange("p (g e) -> p g e", e=EPG), cnt.rearrange("p (g e) -> p g e", e=EPG),
                                        float(k), in_g, ALU.is_equal, ALU.mult))
        link(v.tensor_tensor(sel2, hot[:, 0], hot[:, 1], ALU.add))
        v.memset(before[:, 0:NE], 0.0)
        link(v.tensor_copy(before[:, NE:2 * NE], sel2[:, 0:NE]))
        for c in range(1, TT):
            ins = v.tensor_tensor(before[:, (c + 1) * NE:(c + 2) * NE], before[:, c * NE:(c + 1) * NE],
                                  sel2[:, c * NE:(c + 1) * NE], ALU.add)
            if c < TT - 1:
                link(ins)
        ins.then_inc(S["route_ready"], 1)
        two = pa_[:, 64:64 + 2 * n]

        def pick(dst, vals):
            w = two.rearrange("p (k i e) -> p k i e", k=2, i=TT)
            link(v.tensor_tensor(w, hot.rearrange("p k (i e) -> p k i e", i=TT),
                                 vals.unsqueeze(1).to_broadcast([P, 2, TT, NE]), ALU.mult))
            link(v.tensor_reduce(dst, w, AX.X, ALU.add))

        q10 = pb_[:, 0:160].rearrange("p (q k i) -> p q k i", q=16, k=2)
        ex, rk, ofs, jt, row, til, ov, tt_, sl = (q10[:, q] for q in range(9))
        pick(ex, K("iota")[:, 0:NE].unsqueeze(1).to_broadcast([P, TT, NE]))
        b = filled(dve, "rank")
        rank, rows = cnt, misc[:, 0:NE]
        v.tensor_copy(rows, b[:, 2 * n:2 * n + NE])
        link(v.tensor_copy(rank, b[:, 0:n]))
        v.tensor_tensor(rank, rank, b[:, n:2 * n], ALU.add).then_inc(S["evac_d"], 1)
        emptied(dve, "rank")
        upto, off, pf = tile_sums()
        pick(rk, three(rank))
        link(v.tensor_scalar(jt, rk, float(P), None, ALU.is_ge))
        for q in range(2, TT):
            link(v.scalar_tensor_tensor(jt, rk, float(P * q), jt, ALU.is_ge, ALU.add))
        link(v.scalar_tensor_tensor(row, jt, -float(P), rk, ALU.mult, ALU.add))
        link(v.tensor_scalar(ov, jt, 0.0, None, ALU.is_gt))
        dve.wait_ge(S["off_ready"], 1)
        pick(ofs, off.unsqueeze(1).to_broadcast([P, TT, NE]))
        link(v.tensor_tensor(tt_, ofs, ex, ALU.subtract))
        link(v.scalar_tensor_tensor(tt_, tt_, float(NE - 1), jt, ALU.add, ALU.add))
        link(v.tensor_tensor(tt_, tt_, ov, ALU.mult))
        link(v.tensor_tensor(til, ex, tt_, ALU.add))
        link(v.scalar_tensor_tensor(sl, til, float(P), row, ALU.mult, ALU.add))
        link(v.tensor_copy(slot_u[:, :, :], sl))
        th = tilehot.rearrange("p (k c) n -> p k c n", k=2)
        link(v.tensor_tensor(th, K("iotat").unsqueeze(1).unsqueeze(1).to_broadcast([P, 2, TT, NT]),
                             til.unsqueeze(3).to_broadcast([P, 2, TT, NT]), ALU.is_equal))
        v.tensor_tensor(th, th, K("tok").unsqueeze(1).unsqueeze(3).to_broadcast([P, 2, TT, NT]),
                        ALU.mult).then_inc(S["tiles_hot"], 1)
        for k in range(2):
            v.tensor_tensor(rowhot[:, k * TT:(k + 1) * TT, :], K("iota").unsqueeze(1).to_broadcast([P, TT, P]),
                            row[:, k].unsqueeze(2).to_broadcast([P, TT, P]), ALU.is_equal).then_inc(S["rows_hot"], 1)
        b = filled(dve, "table")
        evac(ridx[:, :], b[:, 0:NT])
        tv = pa_[:, 64:64 + 160].rearrange("p (j e) -> p j e", j=MAXOV)
        jj = K("iota")[:, 0:MAXOV].unsqueeze(2).to_broadcast([P, MAXOV, NE])

        def row16(ap):
            return ap.unsqueeze(1).to_broadcast([P, MAXOV, NE])

        tu = W[:, 0:160].rearrange("p (j e) -> p j e", j=MAXOV)
        link(v.tensor_tensor(tv, jj, row16(off), ALU.is_ge))
        link(v.tensor_tensor(tu, jj, row16(upto), ALU.is_lt))
        link(v.tensor_tensor(tv, tv, tu, ALU.mult))
        link(v.tensor_tensor(tv, tv, row16(K("iota")[:, 0:NE]), ALU.mult))
        fo = misc[:, 48:64]
        link(v.tensor_reduce(fo[:, 1:1 + MAXOV], tv, AX.X, ALU.add))
        link(v.tensor_copy(fo[:, 0:1], upto[:, 15:16]))
        v.tensor_copy(oi[:, 0:1 + MAXOV], fo[:, 0:1 + MAXOV]).then_inc(S["oi_ready"], 1)
        for k in range(2):
            link(v.tensor_tensor(tmp, aff, hot[:, k], ALU.mult))
            link(v.tensor_reduce(wts[:, k, :], three(tmp), AX.X, ALU.add))
        link(v.tensor_tensor(pf[:, 1, 0:TT], wts[:, 0, :], wts[:, 1, :], ALU.add))
        link(v.reciprocal(pf[:, 1, 8:8 + TT], pf[:, 1, 0:TT]))
        for k in range(2):
            link(v.tensor_tensor(wts[:, k, :], wts[:, k, :], pf[:, 1, 8:8 + TT], ALU.mult))

        def xt_out(i, b):
            dve.wait_ge(S["xt_full"], i * 4 + (2 * b + 2))
            ge(dve, "gu_full", i * 4 + (2 * b - 2))
            v.tensor_copy(xt[:, b, 4:8, :], bank[1][:, :].rearrange("p (k n) -> p k n", k=4)).then_inc(S["xt_evac_d"], 1)

        def tiles(i, b):
            for hf in range(2):
                dve.wait_ge(S["silu_done"], i * 4 + (2 * b + hf + 1))
                if hf == 0:
                    ge(dve, "y_full", i * 4 + (2 * b - 2))
                v.tensor_tensor(hid[:, b, 2 * hf:2 * hf + 2, :], gs[:, hf, :].rearrange("p (f n) -> p f n", f=2),
                                bank[2 + hf][:, 256:512].rearrange("p (f n) -> p f n", f=2),
                                ALU.mult).then_inc(S["hid_done"], 1)
            xt_out(i + b, 1 - b)
            dve.wait_ge(S["y_full"], i * 4 + (2 * b + 2))
            ge(dve, y_out[b], i * 16)
            v.tensor_copy(yo[:, b, 512:1024], bank[5 + 2 * b][:, :]).then_inc(S["y_evac_d"], 1)

        xt_out(0, 0)
        over_tiles(dve, tiles)

        def mean_square(c):
            dve.wait_ge(S["ssq3_ready"], c + 1)
            v.tensor_scalar(ss[:, 0, c:c + 1], ss[:, 0, c:c + 1], 1.0 / D, EPS, ALU.mult, ALU.add).then_inc(S["ms3_ready"], 1)

        def inverse(c):
            dve.wait_ge(S["sqrt3_ready"], c + 1)
            v.reciprocal(ss[:, 2, c:c + 1], ss[:, 1, c:c + 1]).then_inc(S["rms3_ready"], 1)

        dve.wait_ge(S["bcend_in"], 16 * 3)
        for c in range(TT):
            dve.wait_ge(S["first_ready"], c + 1)
            link(v.scalar_tensor_tensor(fy[:, c, 0, :], fy[:, c, 1, :], wts[:, 1, c:c + 1], fy[:, c, 0, :],
                                        ALU.mult, ALU.add))
            if c >= 1:
                mean_square(c - 1)
            link(v.tensor_tensor(fy[:, c, 0, :], fy[:, c, 0, :], bc[:, 0 if c < 4 else 1, :], ALU.mult))
            if c >= 1:
                inverse(c - 1)
            v.tensor_tensor(x[:, c, :], x[:, c, :], fy[:, c, 0, :], ALU.add).then_inc(S["x2_ready"], 1)
        mean_square(TT - 1)
        inverse(TT - 1)
        dve.wait_ge(S["rms3_ready"], TT)
        v.scalar_tensor_tensor(fy[:, TT - 1, 1, :], x[:, TT - 1, :], ss[:, 2, TT - 1:TT], bc[:, 2, :],
                               ALU.mult, ALU.mult).then_inc(S["last_ready"], 1)

    @block.gpsimd
    def _(pool):
        link = chained(pool, "pool_chain")
        g = nc.gpsimd
        g.memset(cond[:, :, :], 0.0).then_inc(S["cond_zero"], 1)
        link(g.memset(rprow[0:120, :], 0.0))
        pool.dma_start(rprow[0:120, 8:8 + 31], t["rpb"][0].rearrange("h a b -> (h a) b")).then_inc(S["rpb_in"], 16)
        pool.dma_start(cwrow[0:2 * TAPS, :], t["conv_w"][0].rearrange("k (m p) -> (k m) p", p=P)).then_inc(S["cw_in"], 16)
        for name, rows in VR2:
            src = t[name]
            if len(src.shape) == 2:
                src = src[0]
            o = VO[name][0]
            pool.dma_start(cwrow[o:o + rows, :], src.rearrange("(a p) -> a p", p=P)).then_inc(S["cw_in"], 16)
        g.memset(poolw[:, :, :], 0.0).then_inc(S["rpad_ready"], 1)
        g.memset(vl[:, :, :, DH:DH + 1], 1.0)
        g.memset(vc[:, :, :, DH:DH + 1], 1.0)
        g.memset(vp[:, :, DH:DH + 1], 1.0).then_inc(S["ones_ready"], 1)
        g.memset(rc[:, 0:2 * LP], 0.0).then_inc(S["pads_ready"], 1)
        g.memset(cuts[11], 0.0).then_inc(S["zeros_ready"], 1)
        pool.wait_ge(S["rpad_ready"], 1)
        for q in range(4):
            a, m = 64 * (q % 2), q // 2
            pool.dma_start(poolw[a:a + 64, m, a:a + 64], t["pool_w"][0, q]).then_inc(S["poolw_in"], 16)
        pool.wait_ge(S["rpb_in"], 16)
        pool.dma_start(t["rpad"], rprow[0:120, :]).then_inc(S["rpad_out"], 16)
        filled(pool, "xT", TT - 1, 1)
        g.memset(re[:, 0:e0], 0.0).then_inc(S["pads_ready"], 1)

        def modulation(vec, a=0, n=KD):
            emptied(pool, "adT", 2 * vec + (a + n) // 4 - 1)
            m = mod[:, vec, :, a:a + n]

            def both(rows):
                return rows.unsqueeze(1).to_broadcast([P, 2, n])
            ins = g.tensor_tensor(m, m, both(V("b_ada")[:, 8 * vec + a:8 * vec + a + n]), ALU.add)
            if vec in (1, 4):
                link(ins)
                link(g.tensor_scalar(m, m, 1.0, None, ALU.add))
                ins = g.tensor_tensor(m, m, both(V("norm1_g" if vec == 1 else "norm2_g")[:, a:a + n]), ALU.mult)
            ins.then_inc(S["mod_ready"], 1)

        pool.wait_ge(S["evac_d"], 1)
        for a in (0, 4):
            modulation(0, a, 4)
            modulation(1, a, 4)
        pool.wait_ge(S["h_ready"], KD)
        g.tensor_copy(hT0[:, :, 0:64], hT[:, :, NLAT - 64:NLAT])
        g.tensor_copy(hT0[:, :, 64:128], hT[:, :, 0:64]).then_inc(S["h0_ready"], 1)
        pool.wait_ge(S["rpad_out"], 16)
        rp = t["rpad"].rearrange("(h a) w -> h a w", h=H)
        for qr in range(ROWS):
            pool.dma_start(t["rwin"][qr], rp[:, 7 - qr:15 - qr, :]).then_inc(S["rwin_out"], 16)
        pool.wait_ge(S["rwin_out"], 16 * ROWS)
        for gq in range(2):
            for qc in range(GC):
                a = 15 - 8 * gq - qc
                pool.dma_start(cuts[8][64 * gq + qc:64 * gq + 64:8, :].rearrange("p (n w) -> p n w", w=32),
                               t["rwin"].rearrange("q h a w -> q (h a) w")[:, :, a:a + 32]).then_inc(S["raw_in"], 16)
        emptied(pool, "pac")
        seg = ((PADP, 0, NLAT), (CTXP + PADP, NLAT, NCTX))

        def mean(src, m, half):
            p = slice(64 * half, 64 * half + 64)
            for a, b, w in seg:
                link(g.tensor_scalar(df[p, m, b:b + w], src[p, m, a:a + w], K("invw")[p, m:m + 1], None, ALU.mult))

        pool.wait_ge(S["cst_in"], 16)
        link(g.tensor_tensor(s1[:, :, 1:LP], up[:, :, 0:LP - 1], up[:, :, 1:LP], ALU.add))
        mean(s1, 0, 0)
        link(g.tensor_tensor(s2[:, :, 2:LP - 1], s1[:, :, 1:LP - 2], s1[:, :, 3:LP], ALU.add))
        mean(s2, 0, 1)
        link(g.tensor_tensor(s1[:, :, 4:LP - 3], s2[:, :, 2:LP - 5], s2[:, :, 6:LP - 1], ALU.add))
        mean(s1, 1, 0)
        link(g.tensor_tensor(s2[:, :, 8:LP - 7], s1[:, :, 4:LP - 11], s1[:, :, 12:LP - 3], ALU.add))
        mean(s2, 1, 1)
        edge = K("edge").rearrange("p (m s n) -> p m s n", m=2, s=2)
        for a, b, w in seg:
            link(g.tensor_tensor(df[:, :, b:b + 8], df[:, :, b:b + 8], edge[:, :, 0, :], ALU.mult))
            link(g.tensor_tensor(df[:, :, b + w - 8:b + w], df[:, :, b + w - 8:b + w], edge[:, :, 1, :], ALU.mult))
            ins = g.tensor_tensor(df[:, :, b:b + w], df[:, :, b:b + w], up[:, :, a:a + w], ALU.subtract)
        ins.then_inc(S["df_ready"], 1)
        modulation(2)
        modulation(3)
        emptied(pool, "vc")
        pool.dma_start(t["new_v"][0, 0], vp[:, :, 0:DH]).then_inc(S["vcache_out"], 16)
        emptied(pool, "ko")
        pool.dma_start(t["new_k"][0, 0].rearrange("n h e -> n (h e)"), at).then_inc(S["kcache_out"], 16)

        def row(vec, who):
            r = (2 * vec + who) * KD
            return t["modr"][r:r + KD, :].rearrange("a b -> (a b)").unsqueeze(0).to_broadcast([P, D])

        pool.wait_ge(S["raw_in"], 16 * 16)
        for s in range(PAIRS):
            if s >= 4:
                pool.wait_ge(S["smax_done"], s - 3)
            tile, h = s // H, s % H
            var = (0, 1, 1, 2)[tile]
            g.tensor_tensor(bm[:, s % 4, :].rearrange("p (g r c) -> p g r c", g=4, r=8),
                            raw[:, h, :, :].rearrange("p r (g c) -> p g r c", g=4),
                            K("mask")[:, 256 * var:256 * var + 256].rearrange("p (g r c) -> p g r c", g=4, r=8),
                            ALU.add).then_inc(S["bm_ready"], 1)
            if s == 11:
                modulation(4)
            if s == 16:
                modulation(5)
            if s == 22:
                emptied(pool, "modT")
                pool.dma_start(t["modr"], mrow).then_inc(S["mrow_out"], 16)
            if s == 25:
                pool.wait_ge(S["mrow_out"], 16)
                for q, (vec, who) in enumerate(((0, 1), (0, 0), (2, 1), (1, 1))):
                    pool.dma_start(bc[:, q, :], row(vec, who)).then_inc(S["bc_in"], 16)
        emptied(pool, "aT", 4)
        for q, vec in enumerate((2, 1)):
            pool.dma_start(bc2[:, q, :], row(vec, 0)).then_inc(S["bc2_in"], 16)
        for i in range(TT):
            if i < TT - 1:
                pool.wait_ge(S["hn_ready"], i + 1)
                g.tensor_tensor(h2[:, i % 2, :], h2[:, i % 2, :], bc[:, 3, :], ALU.add).then_inc(S["h2_ready"], 1)
                pool.wait_ge(S["h2_ready"], i + 1)
            else:
                pool.wait_ge(S["h2_last"], 1)
            pool.dma_start(t["h2d"][i * P:(i + 1) * P, :], h2[:, i % 2, :]).then_inc(h2_out[i % 2], 16)
        for q, src in enumerate((row(3, 1), row(3, 0), t["final_g"].rearrange("(a n) -> a n", a=1).to_broadcast([P, D]))):
            pool.dma_start(bc[:, q, :], src).then_inc(S["bcend_in"], 16)

        emptied(pool, "rank")
        upto, off, pf = tile_sums()
        rows, nov = (ra[:, o:o + NE] for o in (4736 + 4 * TT * NE, 4736 + 4 * TT * NE + 16))
        link(g.tensor_scalar(nov, rows, float(P), None, ALU.is_gt))
        for q in range(2, TT):
            link(g.tensor_scalar(pf[:, 0, 0:16], rows, float(P * q), None, ALU.is_gt))
            link(g.tensor_tensor(nov, nov, pf[:, 0, 0:16], ALU.add))
        link(g.memset(pf[:, :, :], 0.0))
        link(g.tensor_copy(upto, nov))
        for q, d in enumerate((1, 2, 4, 8)):
            link(g.tensor_tensor(pf[:, 1 - q % 2, 16:32], pf[:, q % 2, 16:32], pf[:, q % 2, 16 - d:32 - d], ALU.add))
        g.tensor_tensor(off, upto, nov, ALU.subtract).then_inc(S["off_ready"], 1)
        pool.wait_ge(h2_out[0], 16 * 3)
        pool.wait_ge(h2_out[1], 16 * 2)
        emptied(pool, "table")

        def gather(b, tile):
            g.tensor_copy(gi[:, b:b + 1], ridx[:, bass.ds(tile, 1)]).then_inc(S["gi_ready"], 1)
            pool.wait_ge(S["gi_ready"], tile + 1)
            pool.sem_inc(S["gi_seen"], 1)
            g.indirect_dma_start(xg[:, b, :], None, t["h2d"],
                                 bass.IndirectOffsetOnAxis(ap=gi[:, b:b + 1], axis=0)).then_inc(xg_in[b], 16)

        gather(0, 0)
        gather(1, 1)

        def tiles(i, b):
            pool.wait_ge(S["xt_full"], i * 4 + (2 * b + 2))
            gather(b, i * 2 + (2 + b))

        def overflow(i, b):
            tiles(i, b)
            pool.wait_ge(xg_in[b], i * 16 + 32)
            pool.sem_inc(S["xg_seen"], 1)

        over_tiles(pool, tiles, overflow)
        for b in range(2):
            pool.wait_ge(xg_in[b], 16 * (NE // 2 + 1))
        pool.wait_ge(S["moe_stored"], 1)
        for c in range(TT):
            for k in range(2):
                g.indirect_dma_start(fy[:, c, k, :], None, t["yd"],
                                     bass.IndirectOffsetOnAxis(ap=slot_u[:, k, c:c + 1], axis=0)).then_inc(fy_in[c], 16)
        pool.wait_ge(S["bcend_in"], 48)
        for c in range(TT - 1):
            pool.wait_ge(S["xn3_ready"], c + 1)
            g.tensor_tensor(fy[:, c, 1, :], fy[:, c, 1, :], bc[:, 2, :], ALU.mult).then_inc(S["out_ready"], 1)
        pool.wait_ge(S["vcache_out"], 16)

    @block.tensor
    def _(pe):
        mm = nc.tensor.matmul

        def take(*key):
            n = NTH[key]
            if key in ASIDE:
                if key[1] == 3:
                    emptied(pe, key[0], 1)
            elif n >= RING:
                emptied(pe, *PLAN[n - RING][0])
            return bank[BANK[key]]

        def give(ins):
            ins.then_inc(S["psum_full"], 1)

        def slot(*key):
            n = LOADNO[key]
            pe.wait_ge(w_slot[SLOT[n]], 16 * SLOT[:n + 1].count(SLOT[n]))
            return slots[:, SLOT[n], :]

        def transposes(key, tiles):
            b = take(*key)
            for q, ap in enumerate(tiles):
                ins = nc.tensor.transpose(b[:, q * P:(q + 1) * P], ap, ident)
            give(ins)

        pe.wait_ge(S["vec_in"], 16 * len(VR))
        pe.wait_ge(S["cst_in"], 16)
        b = take("vec")
        give(nc.tensor.transpose(b[:, 0:NVEC], vrow[0:NVEC, :], ident[0:NVEC, 0:NVEC]))

        def ada(j):
            w = slot("ada", j).rearrange("p (k n) -> p k n", k=KD)
            if j == 0:
                pe.wait_ge(S["cond_ready"], 1)
            b = take("ada", j)
            for k in range(KD):
                for q in range(4):
                    ins = mm(b[32 * q:32 * q + 32, 0:P], cond[:, k, :], w[:, k, q * P:(q + 1) * P],
                             start=k == 0, stop=k == KD - 1)
            give(ins)

        def keep_warm(n):
            for _ in range(n):
                mm(bank[7][:, 0:P], ident, ident, start=True, stop=True)

        def adT(j):
            emptied(pe, "ada", j)
            b = take("adT", j)
            give(nc.tensor.transpose(b[:, 0:P], adr[:, :], ident))

        for i in range(TT):
            pe.wait_ge(S["xn_ready"], i + 1)
            for hf in range(2):
                transposes(("xT", i, hf), [xn[:, i % 2, (4 * hf + q) * P:(4 * hf + q + 1) * P] for q in range(4)])

        for j in (0, 2):
            ada(j)
            adT(j)
        pe.wait_ge(S["cw_in"], 16 * (len(VR2) + 1))
        b = take("cw")
        give(nc.tensor.transpose(b[:, 0:NCW], cwrow[0:NCW, :], ident[0:NCW, 0:NCW]))

        def project(load, latent, prompt, width=512, begun=0):
            w = slot("in", load)[:, 0:KD * width].rearrange("p (k n) -> p k n", k=KD)
            n = width // P
            for m in range(n):
                b = bank[BANK[latent, m]] if begun else take(latent, m)
                for k in range(begun, KD):
                    if begun and m == 0:
                        pe.wait_ge(S["h_ready"], k + 1)
                    ins = mm(b[:, :], w[:, k, m * P:(m + 1) * P], hT[:, k, 0:NLAT], start=k == 0, stop=k == KD - 1)
                give(ins)
            b = take(prompt)
            for m in range(n):
                for k in range(KD):
                    ins = mm(b[:, m * P:(m + 1) * P], w[:, k, m * P:(m + 1) * P], hT[:, k, NLAT:NTOK],
                             start=k == 0, stop=k == KD - 1)
            give(ins)

        w3 = slot("in", 3).rearrange("p (k n) -> p k n", k=KD)
        keep_warm(10)
        emptied(pe, "cw")
        emptied(pe, "adT", 2)

        def begin(k, ms):
            pe.wait_ge(S["h_ready"], k + 1)
            for m in ms:
                mm(bank[BANK["pa", m]][:, :], w3[:, k, m * P:(m + 1) * P], hT[:, k, 0:NLAT], start=k == 0, stop=False)

        begin(0, range(4))
        begin(1, range(4))
        ada(1)
        begin(2, range(4))
        adT(1)
        ada(3)
        begin(3, range(2))
        adT(3)
        begin(3, range(2, 4))
        project(3, "pa", "pac", begun=4)
        ada(4)
        project(4, "g", "gc", 256)
        adT(4)
        ada(5)
        project(0, "q", "qc")
        adT(5)
        ada(6)
        pe.wait_ge(S["cachek_in"], 16)
        for i in range(2):
            transposes(("ck", i), [ckr[:, i, q * P:(q + 1) * P] for q in range(4)])
        project(1, "k", "kc")
        adT(6)
        ada(7)

        def channel_sums(key, pieces):
            b = take(key)
            for m, ap in enumerate(pieces):
                ins = mm(b[:, 0:ap.shape[1]], K("ones"), ap, start=m == 0, stop=m == 1)
            give(ins)

        pe.wait_ge(S["tap_done"], 2 * TAPS)
        channel_sums("mu", [acc[:, m, 0:NLAT] for m in range(2)])
        channel_sums("muc", [acc[:, m, CTXC:CTXC + NCTX] for m in range(2)])
        w = slot("in", 2).rearrange("p (k n) -> p k n", k=KD)
        pe.wait_ge(S["h0_ready"], 1)
        for j in range(5):
            b = take("v", j) if j < 4 else take("vc")
            for k in range(KD):
                lhs = hT0[:, k, :] if j == 0 else hT[:, k, P * j - 64:P * j + 64] if j < 4 else hT[:, k, NLAT:NTOK]
                ins = mm(b[:, :], lhs, w[:, k, :], start=k == 0, stop=k == KD - 1)
            give(ins)
            if j == 1:
                pe.wait_ge(S["sq_ready"], 1)
                channel_sums("var", [sg[:, m, 0:NLAT] for m in range(2)])
                channel_sums("varc", [sg[:, m, NLAT:NTOK] for m in range(2)])
        adT(7)
        ada(8)
        transposes(("ko",), [kpT[:, m, :] for m in range(4)])
        pe.wait_ge(S["df_ready"], 1)
        pe.wait_ge(S["poolw_in"], 16 * 4)
        pe.wait_ge(S["small_in"], 16 * 3)
        for m in range(2):
            b = take("pl", m)
            give(mm(b[:, :], poolw[:, m, :], df[:, m, 0:NLAT], start=True, stop=True))
        b = take("plc")
        for m in range(2):
            ins = mm(b[:, m * P:(m + 1) * P], poolw[:, m, :], df[:, m, NLAT:NTOK], start=True, stop=True)
        give(ins)

        adT(8)

        def pw(m):
            pe.wait_ge(S["act_ready"], 1)
            b = take("pw", m)
            for k in range(2):
                ins = mm(b[:, :], pww[:, k, m * P:(m + 1) * P], sg[:, k, 0:NLAT], start=k == 0, stop=k == 1)
            give(ins)

        def pwc():
            b = take("pwc")
            for m in range(2):
                for k in range(2):
                    ins = mm(b[:, m * P:(m + 1) * P], pww[:, k, m * P:(m + 1) * P], sg[:, k, NLAT:NTOK],
                             start=k == 0, stop=k == 1)
            give(ins)

        def modT():
            pe.wait_ge(S["mod_ready"], 8)
            b = take("modT")
            give(nc.tensor.transpose(b[0:64, 0:P], mod[:, 2:6, :, :].rearrange("p v s k -> p (v s k)"), ident))

        def prompt_scores(j):
            b = take("Sc", j)
            for q in range(4):
                p = slice(64 * j, 64 * j + 64)
                ins = mm(b[:, q * P:(q + 1) * P], qT[p, q, NLAT:NTOK], kpT[p, q, :], start=True, stop=True)
            give(ins)

        wo = []

        def project_out(i, hf):
            if not wo:
                wo.extend(slot("out", j).rearrange("p (k n) -> p k n", k=4) for j in range(2))
            if hf == 0:
                emptied(pe, "aT", i)
            b = take("wo", i, hf)
            for k in range(KD):
                ins = mm(b[:, :], mT[:, k, i * P:(i + 1) * P], wo[k // 4][:, k % 4, 512 * hf:512 * hf + 512],
                         start=k == 0, stop=k == KD - 1)
            give(ins)

        beside = {"pw": pw, "pwc": pwc, "ada": ada, "adT": adT, "modT": modT, "Sc": prompt_scores, "wo": project_out}

        def aT(i):
            pe.wait_ge(S["o_free"], 2 * i + 2)
            transposes(("aT", i), [at[:, m * P:(m + 1) * P] for m in range(4)])

        def o_bank(u):
            if u >= 2:
                pe.wait_ge(S["o_free"], u - 1)
            return bank[6 + u % 2]

        emptied(pe, "k", 3)
        pe.wait_ge(S["cachev_in"], 32)
        for i in range(STEPS):
            if i < PAIRS and i % 2 == 0:
                tile, h = i // H, i % H
                rows = [slice(64 * u, 64 * u + 64) for u in range(2)]
                b = [take("S", i + u) for u in range(2)]
                for u, p in enumerate(rows):
                    mm(b[u][:, 0:256], qT[p, h // 2, tile * P:(tile + 1) * P], kT[p, h // 2, tile * P:tile * P + 256],
                       start=True, stop=True)
                for u, p in enumerate(rows):
                    give(mm(b[u][:, 256:512], qT[p, h // 2, tile * P:(tile + 1) * P], kcT[p, h // 2, :],
                            start=True, stop=True))
            if i in BESIDE:
                beside[BESIDE[i][0]](*BESIDE[i][1:])
            if 2 <= i < PAIRS + 2:
                emptied(pe, "S", i - 2)
                transposes(("PT", i - 2), [pr[:, (i - 2) % 4, q * P:(q + 1) * P] for q in range(4)])
            if 4 <= i < PAIRS + 4:
                s = i - 4
                tile, h = s // H, s % H
                ob = o_bank(s // 4) if s % 4 == 0 else bank[6 + (s // 4) % 2]
                emptied(pe, "PT", s)
                vals = [vl[:, tile, h, :], vl[:, (tile + 1) % 4, h, :], vc[:, 0, h, :], vc[:, 1, h, :]]
                for q in range(4):
                    ins = mm(ob[:, 65 * (h % 4):65 * (h % 4) + 65], pts[:, s % 2, q * P:(q + 1) * P], vals[q],
                             start=q == 0, stop=q == 3)
                ins.then_inc(S["pv_done"], 1)
            if i >= 5 and (i - 5) % 8 == 7:
                aT((i - 5) // 8)
        for j in range(2):
            pe.wait_ge(S["expc_done"], j + 1)
            transposes(("PTc", j), [pr[:, j, q * P:(q + 1) * P] for q in range(4)])
        project_out(0, 1)
        for j in range(2):
            emptied(pe, "PTc", j)
            ob = o_bank(8 + j)
            for q in range(4):
                mm(ob[:, 65 * q:65 * q + 65], pts[:, j, q * P:(q + 1) * P], vp[:, 2 * q + j, :],
                   start=True, stop=True).then_inc(S["pv_done"], 1)
        project_out(1, 0)
        aT(4)

        for i in range(1, TT + LAG):
            c = i - LAG
            if 1 < i < TT:
                project_out(i, 0)
            if c >= 0:
                if c < TT - 1:
                    pe.wait_ge(S["h2_ready"], c + 1)
                else:
                    pe.wait_ge(S["h2_last"], 1)
                for hf in range(2):
                    transposes(("hT", c, hf), [h2[:, c % 2, (4 * hf + q) * P:(4 * hf + q + 1) * P] for q in range(4)])
            if i < TT:
                project_out(i, 1)
            if c >= 0:
                if i >= TT:
                    keep_warm(6)
                emptied(pe, "hT", c, 1)
                b = take("lg", c)
                for k in range(KD):
                    ins = mm(b[:, 0:NE], h2T[:, k, c * P:(c + 1) * P], wr[:, k, :], start=k == 0, stop=k == KD - 1)
                give(ins)
        n = TT * NE
        sel2 = ra[:, 4736 + 2 * n:4736 + 3 * n]
        keep_warm(21)
        pe.wait_ge(S["route_ready"], 1)
        b = take("rank")
        mm(b[:, 0:n], K("tri"), sel2, start=True, stop=True)
        give(mm(b[:, n:2 * n + NE], K("ones"), before, start=True, stop=True))
        keep_warm(34)
        pe.wait_ge(S["tiles_hot"], 1)
        b = take("table")
        for q in range(10):
            if q % TT == 0:
                pe.wait_ge(S["rows_hot"], q // TT + 1)
            ins = mm(b[:, 0:NT], rowhot[:, q, :], tilehot[:, q, :], start=q == 0, stop=q == 9)
        give(ins)
        keep_warm(18)
        emptied(pe, "table")

        def xT(i, b):
            pe.wait_ge(xg_in[b], i * 16 + 16)
            ge(pe, "xt_evac_a", i * 2 + b)
            ge(pe, "xt_evac_d", i * 2 + b)
            for hf in range(2):
                for q in range(4):
                    ins = nc.tensor.transpose(bank[hf][:, q * P:(q + 1) * P], xg[:, b, 4 * hf + q:D:KD], ident)
                ins.then_inc(S["xt_full"], 1)

        def weights(i, b, q):
            if b:
                pe.wait_ge(w_odd[q], i * 16 + 16)
            else:
                pe.wait_ge(w_slot[EVEN[q]], i * 16 + 16 * (EVEN_BASE[q] + 1))
            return wset[b][q].rearrange("p (k n) -> p k n", k=KD if q < 2 else FC)

        def tiles(i, b):
            w = [weights(i, b, 0), weights(i, b, 1)]
            pe.wait_ge(S["xt_evac_a"], i * 2 + (b + 1))
            pe.wait_ge(S["xt_evac_d"], i * 2 + (b + 1))
            for hf in range(2):
                ge(pe, "hid_done", i * 4 + (2 * b + hf - 1))
                for q in range(2):
                    for f in range(2):
                        for k in range(KD):
                            ins = mm(bank[2 + hf][:, (2 * q + f) * P:(2 * q + f + 1) * P],
                                     w[q][:, k, 2 * hf + f:DFF:FC], xt[:, b, k, :], start=k == 0, stop=k == KD - 1)
                ins.then_inc(S["gu_full"], 1)
            xT(i + b, 1 - b)
            wd = weights(i, b, 2)
            pe.wait_ge(S["hid_done"], i * 4 + (2 * b + 2))
            ge(pe, "y_evac_a", i * 2 + (b - 1))
            ge(pe, "y_evac_d", i * 2 + (b - 1))
            for hf in range(2):
                for f in range(FC):
                    ins = mm(bank[4 + 2 * b + hf][:, :], hid[:, b, f, :], wd[:, f, 512 * hf:512 * hf + 512],
                             start=f == 0, stop=f == FC - 1)
                ins.then_inc(S["y_full"], 1)

        xT(0, 0)
        keep_warm(8)
        over_tiles(pe, tiles)

    ctx.close()


_INS = ["x_prompt", "x_sample", "cache_k", "cache_v", "c", "c_ctx", "w_ada", "b_ada", "norm1_g", "norm2_g", "w_in",
        "w_out", "rpb", "pool_w", "pool_scale", "conv_w", "conv_b", "conv_ln_g", "conv_ln_b", "conv_pw_w",
        "conv_pw_b", "w_router", "b_router", "moe_w_gate", "moe_w_up", "moe_w_down", "final_g"]
_OUTS = [("y_prompt", (1, NCTX, D)), ("y_sample", (1, NLAT, D)), ("new_k", (1, 1, NCTX, H, DH)),
         ("new_v", (1, 1, NCTX, H, DH))]
_SCRATCH = [("h2d", (NTOK, D)), ("yd", (BIG * P, D)), ("modr", (64, P)), ("rpad", (120, 48)), ("rwin", (8, H, 8, 48))]


def kernel(**inputs):
    import numpy as _np
    import concourse.bacc as _bacc
    from concourse.bass_utils import run_bass_kernel_spmd as _run

    nc = _bacc.Bacc("TRN2", target_bir_lowering=False, num_devices=1)
    arrays, t = {}, {}
    for name in _INS + ["consts"]:
        a = shape_constants() if name == "consts" else _np.ascontiguousarray(inputs[name])
        arrays[f"in_{name}"] = a
        t[name] = nc.dram_tensor(f"in_{name}", a.shape, F32, kind="ExternalInput").ap()
    for name, shape in _OUTS:
        t[name] = nc.dram_tensor(f"out_{name}", shape, F32, kind="ExternalOutput").ap()
    for name, shape in _SCRATCH:
        t[name] = nc.dram_tensor(f"scratch_{name}", shape, F32, kind="Internal").ap()
    build(nc, t)
    r = _run(nc, [arrays], core_ids=[0])
    return tuple(r.results[0][f"out_{name}"] for name, _ in _OUTS)
```
